# Optimizing a Trainium2 kernel written in Bass

```python
import math
import jax, jax.numpy as jnp
from jax import lax
import numpy as np

D_MODEL = 2048
BATCH = 1
SEQ = 256
DEPTH = 1

PLE_DIM = 256
MIX_WIDTH = D_MODEL
LRU_WIDTH = MIX_WIDTH // 2
LRU_BLOCKS = 16
LRU_BLOCK_DIM = LRU_WIDTH // LRU_BLOCKS
CONV_WIDTH = 4
LRU_C = 8.0
HEAD_DIM = 64
N_HEADS = (MIX_WIDTH - LRU_WIDTH) // HEAD_DIM
N_KV = 4
HEADS_PER_KV = N_HEADS // N_KV
KV_W = N_KV * HEAD_DIM
CMP_LEN = 32
CMP_STRIDE = 16
CMP_HIDDEN = 256
SEL_BLOCK = 64
N_SELECT = 16
N_LOCAL_FORCED = 2
WINDOW = 512
Q_BLOCK = 128
SEL_Q_CHUNK = 32
N_BUCKETS = 32
MAX_DISTANCE = 128
D_FF = 4 * D_MODEL
NORM_EPS = 1e-6
NEG_INF = -1e30
FORCE_SCORE = 1e4

IN_SIZES = (LRU_WIDTH, LRU_WIDTH, N_HEADS * HEAD_DIM, KV_W, KV_W, KV_W, KV_W, KV_W, KV_W, 3 * N_HEADS)
IN_DIM = sum(IN_SIZES)
SPLIT_POINTS = tuple(int(v) for v in np.cumsum(IN_SIZES)[:-1])


def rms_norm(x, g):
    xf = x.astype(jnp.float32)
    y = xf * lax.rsqrt(jnp.mean(xf * xf, axis=-1, keepdims=True) + NORM_EPS)
    return (y * g.astype(jnp.float32)).astype(x.dtype)

def rel_bucket(dist):
    n = jnp.maximum(dist, 0)
    max_exact = N_BUCKETS // 2
    nf = jnp.maximum(n, 1).astype(jnp.float32)
    large = max_exact + (jnp.log(nf / max_exact) / math.log(MAX_DISTANCE / max_exact)
                         * (N_BUCKETS - max_exact)).astype(jnp.int32)
    large = jnp.minimum(large, N_BUCKETS - 1)
    return jnp.where(n < max_exact, n, large)

def rglru_mixer(u, gate_in, conv_w, conv_b, wa, ba, wx, bx, lam):
    B, S = u.shape[0], u.shape[1]
    up = jnp.pad(u, ((0, 0), (CONV_WIDTH - 1, 0), (0, 0)))
    xc = conv_b + sum(up[:, k:k + S] * conv_w[k] for k in range(CONV_WIDTH))
    xb = xc.reshape(B, S, LRU_BLOCKS, LRU_BLOCK_DIM)
    r = jax.nn.sigmoid(jnp.einsum('bsni,nij->bsnj', xb, wa) + ba).reshape(B, S, LRU_WIDTH)
    ig = jax.nn.sigmoid(jnp.einsum('bsni,nij->bsnj', xb, wx) + bx).reshape(B, S, LRU_WIDTH)
    log_a = -LRU_C * r.astype(jnp.float32) * jax.nn.softplus(-lam.astype(jnp.float32))
    a = jnp.exp(log_a)
    b = jnp.sqrt(-jnp.expm1(2.0 * log_a)) * (ig * xc).astype(jnp.float32)

    def combine(left, right):
        a1, b1 = left
        a2, b2 = right
        return a1 * a2, a2 * b1 + b2

    _, h = lax.associative_scan(combine, (a, b), axis=1)
    return h.astype(u.dtype) * jax.nn.gelu(gate_in)

def nsa_mixer(q, k_c, v_c, k_s, v_s, k_w, v_w, gates,
              pe_k, w1_k, w2_k, pe_v, w1_v, w2_v, rel_bias):
    B, S = q.shape[0], q.shape[1]
    G, R, dk = N_KV, HEADS_PER_KV, HEAD_DIM
    q = q.reshape(B, S, G, R, dk)
    k_c, v_c, k_s, v_s, k_w, v_w = [t.reshape(B, S, G, dk) for t in (k_c, v_c, k_s, v_s, k_w, v_w)]
    scale = dk ** -0.5
    pos = jnp.arange(S, dtype=jnp.int32)
    bias_tab = rel_bias.astype(jnp.float32).reshape(N_BUCKETS, G, R)

    n_cmp = (S - CMP_LEN) // CMP_STRIDE + 1
    cmp_idx = np.arange(n_cmp)[:, None] * CMP_STRIDE + np.arange(CMP_LEN)[None, :]

    def compress(t, pe, w1, w2):
        blk = t[:, cmp_idx] + pe[:, None, :]
        blk = blk.transpose(0, 1, 3, 2, 4).reshape(B, n_cmp, G, CMP_LEN * dk)
        return jax.nn.gelu(blk @ w1) @ w2

    kc = compress(k_c, pe_k, w1_k, w2_k)
    vc = compress(v_c, pe_v, w1_v, w2_v)
    cmp_end = jnp.asarray(np.arange(n_cmp) * CMP_STRIDE + CMP_LEN - 1, dtype=jnp.int32)
    dist_c = pos[:, None] - cmp_end[None, :]
    valid_c = dist_c >= 0
    bias_c = bias_tab[rel_bucket(dist_c)].transpose(2, 3, 0, 1)
    s_c = jnp.einsum('bsgrd,bngd->bgrsn', q, kc).astype(jnp.float32) * scale + bias_c
    s_c = jnp.where(valid_c, s_c, NEG_INF)
    any_c = (pos >= CMP_LEN - 1)[:, None]
    p_c = jax.nn.softmax(s_c, axis=-1) * any_c
    o_c = jnp.einsum('bgrsn,bngd->bsgrd', p_c.astype(vc.dtype), vc)

    n_sel = S // SEL_BLOCK
    ratio_sel = SEL_BLOCK // CMP_STRIDE
    ratio_cmp = CMP_LEN // CMP_STRIDE
    jj_np = np.arange(n_sel)[:, None, None]
    ci = ratio_sel * jj_np + np.arange(ratio_sel)[None, :, None] - np.arange(ratio_cmp)[None, None, :]
    jb = np.broadcast_to(jj_np, ci.shape)
    ok = (ci >= 0) & (ci < n_cmp)
    M = np.zeros((n_cmp, n_sel), np.float32)
    np.add.at(M, (ci[ok], jb[ok]), 1.0)
    imp = jnp.einsum('bgrsn,nj->bgsj', p_c, jnp.asarray(M))
    jj = jnp.arange(n_sel, dtype=jnp.int32)
    dblk = (pos // SEL_BLOCK)[:, None] - jj[None, :]
    forced = (jj[None, :] == 0) | ((dblk >= 0) & (dblk < N_LOCAL_FORCED))
    causal_blk = dblk >= 0
    imp = jnp.where(forced, FORCE_SCORE, jnp.where(causal_blk, imp, -FORCE_SCORE))
    n_top = min(N_SELECT, n_sel)
    _, sel_idx = lax.top_k(imp, n_top)

    kb = k_s.reshape(B, n_sel, SEL_BLOCK, G, dk).transpose(0, 3, 1, 2, 4)
    vb = v_s.reshape(B, n_sel, SEL_BLOCK, G, dk).transpose(0, 3, 1, 2, 4)
    n_ch = S // SEL_Q_CHUNK
    q_ch = q.reshape(B, n_ch, SEL_Q_CHUNK, G, R, dk).transpose(1, 0, 2, 3, 4, 5)
    idx_ch = sel_idx.reshape(B, G, n_ch, SEL_Q_CHUNK, n_top).transpose(2, 0, 1, 3, 4)
    pos_ch = pos.reshape(n_ch, SEL_Q_CHUNK)
    b_ar = jnp.arange(B)[:, None, None]
    g_ar = jnp.arange(G)[None, :, None]
    g_ar4 = jnp.arange(G)[None, :, None, None]
    n_keys = n_top * SEL_BLOCK
    in_blk = jnp.arange(SEL_BLOCK, dtype=jnp.int32)

    def sel_chunk(args):
        qc, ic, tc = args
        flat = ic.reshape(B, G, SEL_Q_CHUNK * n_top)
        ks = kb[b_ar, g_ar, flat].reshape(B, G, SEL_Q_CHUNK, n_keys, dk)
        vs = vb[b_ar, g_ar, flat].reshape(B, G, SEL_Q_CHUNK, n_keys, dk)
        kpos = (ic[..., None] * SEL_BLOCK + in_blk).reshape(B, G, SEL_Q_CHUNK, n_keys)
        dist = tc[None, None, :, None] - kpos
        bias = bias_tab[rel_bucket(dist), g_ar4].transpose(0, 1, 4, 2, 3)
        s = jnp.einsum('bqgrd,bgqkd->bgrqk', qc, ks).astype(jnp.float32) * scale + bias
        s = jnp.where((dist >= 0)[:, :, None], s, NEG_INF)
        pr = jax.nn.softmax(s, axis=-1)
        return jnp.einsum('bgrqk,bgqkd->bqgrd', pr.astype(vs.dtype), vs)

    o_s = lax.map(sel_chunk, (q_ch, idx_ch, pos_ch))
    o_s = o_s.transpose(1, 0, 2, 3, 4, 5).reshape(B, S, G, R, dk)

    n_qb = S // Q_BLOCK
    band = Q_BLOCK + WINDOW
    kw_pad = jnp.pad(k_w, ((0, 0), (WINDOW, 0), (0, 0), (0, 0)))
    vw_pad = jnp.pad(v_w, ((0, 0), (WINDOW, 0), (0, 0), (0, 0)))
    kj = jnp.arange(band, dtype=jnp.int32)[None, :]
    dist_w = WINDOW + jnp.arange(Q_BLOCK, dtype=jnp.int32)[:, None] - kj
    band_ok = (dist_w >= 0) & (dist_w < WINDOW)
    bias_w = bias_tab[rel_bucket(dist_w)].transpose(2, 3, 0, 1)
    q_blk = q.reshape(B, n_qb, Q_BLOCK, G, R, dk).transpose(1, 0, 2, 3, 4, 5)
    starts = jnp.arange(n_qb, dtype=jnp.int32) * Q_BLOCK

    def win_block(args):
        qb, st = args
        kw = lax.dynamic_slice_in_dim(kw_pad, st, band, axis=1)
        vw = lax.dynamic_slice_in_dim(vw_pad, st, band, axis=1)
        ok_w = band_ok & (st - WINDOW + kj >= 0)
        s = jnp.einsum('bqgrd,bkgd->bgrqk', qb, kw).astype(jnp.float32) * scale + bias_w
        s = jnp.where(ok_w, s, NEG_INF)
        pr = jax.nn.softmax(s, axis=-1)
        return jnp.einsum('bgrqk,bkgd->bqgrd', pr.astype(vw.dtype), vw)

    o_w = lax.map(win_block, (q_blk, starts))
    o_w = o_w.transpose(1, 0, 2, 3, 4, 5).reshape(B, S, G, R, dk)

    gt = jax.nn.sigmoid(gates).reshape(B, S, G, R, 3)
    o = gt[..., 0:1] * o_c + gt[..., 1:2] * o_s + gt[..., 2:3] * o_w
    return o.reshape(B, S, N_HEADS * dk)

def first_inputs(seed: int = 0) -> dict:
    key = jax.random.key(seed)
    ks = jax.random.split(key, 32)
    f32 = jnp.float32

    def nrm(k, shape, scale):
        return jax.random.normal(k, shape, f32) * scale

    def gain(k, shape):
        return 1.0 + 0.05 * jax.random.normal(k, shape, f32)

    a0 = jax.random.uniform(ks[10], (DEPTH, LRU_WIDTH), f32, 0.9, 0.999)
    return {
        "x": nrm(ks[0], (BATCH, SEQ, D_MODEL), 1.0),
        "p": nrm(ks[1], (DEPTH, BATCH, SEQ, PLE_DIM), 1.0),
        "norm_mix_pre": gain(ks[2], (DEPTH, D_MODEL)),
        "norm_mix_post": gain(ks[3], (DEPTH, D_MODEL)),
        "norm_mlp_pre": gain(ks[4], (DEPTH, D_MODEL)),
        "norm_mlp_post": gain(ks[5], (DEPTH, D_MODEL)),
        "w_in": nrm(ks[6], (DEPTH, D_MODEL, IN_DIM), D_MODEL ** -0.5),
        "conv_w": nrm(ks[7], (DEPTH, CONV_WIDTH, LRU_WIDTH), CONV_WIDTH ** -0.5),
        "conv_b": nrm(ks[8], (DEPTH, LRU_WIDTH), 0.02),
        "lru_wa": nrm(ks[9], (DEPTH, LRU_BLOCKS, LRU_BLOCK_DIM, LRU_BLOCK_DIM), LRU_BLOCK_DIM ** -0.5),
        "lru_ba": nrm(ks[11], (DEPTH, LRU_BLOCKS, LRU_BLOCK_DIM), 0.02),
        "lru_wx": nrm(ks[12], (DEPTH, LRU_BLOCKS, LRU_BLOCK_DIM, LRU_BLOCK_DIM), LRU_BLOCK_DIM ** -0.5),
        "lru_bx": nrm(ks[13], (DEPTH, LRU_BLOCKS, LRU_BLOCK_DIM), 0.02),
        "lru_lambda": jnp.log(a0 / (1.0 - a0)),
        "cmp_pe_k": nrm(ks[14], (DEPTH, CMP_LEN, HEAD_DIM), 0.1),
        "cmp_w1_k": nrm(ks[15], (DEPTH, CMP_LEN * HEAD_DIM, CMP_HIDDEN), (CMP_LEN * HEAD_DIM) ** -0.5),
        "cmp_w2_k": nrm(ks[16], (DEPTH, CMP_HIDDEN, HEAD_DIM), CMP_HIDDEN ** -0.5),
        "cmp_pe_v": nrm(ks[17], (DEPTH, CMP_LEN, HEAD_DIM), 0.1),
        "cmp_w1_v": nrm(ks[18], (DEPTH, CMP_LEN * HEAD_DIM, CMP_HIDDEN), (CMP_LEN * HEAD_DIM) ** -0.5),
        "cmp_w2_v": nrm(ks[19], (DEPTH, CMP_HIDDEN, HEAD_DIM), CMP_HIDDEN ** -0.5),
        "rel_bias": nrm(ks[20], (N_BUCKETS, N_HEADS), 0.1),
        "gnorm_lru": gain(ks[21], (DEPTH, LRU_WIDTH)),
        "gnorm_nsa": gain(ks[22], (DEPTH, N_HEADS * HEAD_DIM)),
        "w_out": nrm(ks[23], (DEPTH, MIX_WIDTH, D_MODEL), MIX_WIDTH ** -0.5),
        "mlp_w1": nrm(ks[24], (DEPTH, D_MODEL, D_FF), D_MODEL ** -0.5),
        "mlp_w2": nrm(ks[25], (DEPTH, D_FF, D_MODEL), D_FF ** -0.5),
        "ple_gate": nrm(ks[26], (DEPTH, D_MODEL, D_MODEL), D_MODEL ** -0.5),
        "ple_proj": nrm(ks[27], (DEPTH, PLE_DIM, D_MODEL), PLE_DIM ** -0.5),
    }

def first_block(x, p, norm_mix_pre, norm_mix_post, norm_mlp_pre, norm_mlp_post, w_in,
              conv_w, conv_b, lru_wa, lru_ba, lru_wx, lru_bx, lru_lambda,
              cmp_pe_k, cmp_w1_k, cmp_w2_k, cmp_pe_v, cmp_w1_v, cmp_w2_v, rel_bias,
              gnorm_lru, gnorm_nsa, w_out, mlp_w1, mlp_w2, ple_gate, ple_proj):
    h = x
    for i in range(DEPTH):
        a = rms_norm(h, norm_mix_pre[i])
        z = a @ w_in[i]
        u, g_lru, q, kc, vc, ksel, vsel, kw, vw, gts = jnp.split(z, SPLIT_POINTS, axis=-1)
        y_lru = rglru_mixer(u, g_lru, conv_w[i], conv_b[i], lru_wa[i], lru_ba[i],
                            lru_wx[i], lru_bx[i], lru_lambda[i])
        y_nsa = nsa_mixer(q, kc, vc, ksel, vsel, kw, vw, gts,
                          cmp_pe_k[i], cmp_w1_k[i], cmp_w2_k[i],
                          cmp_pe_v[i], cmp_w1_v[i], cmp_w2_v[i], rel_bias)
        y = jnp.concatenate([rms_norm(y_lru, gnorm_lru[i]), rms_norm(y_nsa, gnorm_nsa[i])], axis=-1)
        h = h + rms_norm(y @ w_out[i], norm_mix_post[i])
        f = jnp.square(jax.nn.relu(rms_norm(h, norm_mlp_pre[i]) @ mlp_w1[i])) @ mlp_w2[i]
        h = h + rms_norm(f, norm_mlp_post[i])
        h = h + jax.nn.sigmoid(h @ ple_gate[i]) * (p[i] @ ple_proj[i])
    return h


D_MIX = D_MODEL
MLSTM_WIDTH = D_MIX // 2
MLSTM_HEADS = 4
MLSTM_HEAD_DIM = MLSTM_WIDTH // MLSTM_HEADS
MLSTM_CHUNK = 128
S5_WIDTH = D_MIX - MLSTM_WIDTH
S5_GROUP = 16
S5_GROUPS = S5_WIDTH // S5_GROUP
S5_STATE = 64
S5_DT_MIN = 1e-3
S5_DT_MAX = 1e-1
PEER_HEADS = 8
PEER_NKEYS = 128
PEER_EXPERTS = PEER_NKEYS * PEER_NKEYS
PEER_TOPK = 16
PEER_QDIM = 256
PEER_BLOCK = 128
RMS_EPS = 1e-6
N_IN = 4 * MLSTM_WIDTH + 2 * MLSTM_HEADS + S5_WIDTH


def rmsnorm(x, g):
    xf = x.astype(jnp.float32)
    y = xf * lax.rsqrt(jnp.mean(xf * xf, axis=-1, keepdims=True) + RMS_EPS)
    return (y * g.astype(jnp.float32)).astype(x.dtype)

def causal_dwconv(x, w):
    K, C = w.shape
    return lax.conv_general_dilated(
        x, w[:, None, :].astype(x.dtype), window_strides=(1,), padding=((K - 1, 0),),
        dimension_numbers=('NWC', 'WIO', 'NWC'), feature_group_count=C)

def mlstm_chunkwise(q, k, v, li, lf):
    B, H, S, Dh = q.shape
    L = MLSTM_CHUNK
    NC = S // L
    q = q.reshape(B, H, NC, L, Dh) * (Dh ** -0.5)
    k = k.reshape(B, H, NC, L, Dh)
    v = v.reshape(B, H, NC, L, Dh)
    li = li.reshape(B, H, NC, L)
    lf = lf.reshape(B, H, NC, L)
    a = jnp.cumsum(lf, axis=-1)
    A = a[..., -1]
    g = A[..., None] - a + li
    m_loc = jnp.max(g, axis=-1)
    w = jnp.exp(g - m_loc[..., None])
    dC = jnp.einsum('bhcl,bhcld,bhcle->bhcde', w, k, v)
    dn = jnp.einsum('bhcl,bhcld->bhcd', w, k)

    def step(carry, inp):
        C, n, m = carry
        dC_c, dn_c, m_c, A_c = inp
        m_new = jnp.maximum(A_c + m, m_c)
        s_old = jnp.exp(A_c + m - m_new)
        s_new = jnp.exp(m_c - m_new)
        C_new = s_old[..., None, None] * C + s_new[..., None, None] * dC_c
        n_new = s_old[..., None] * n + s_new[..., None] * dn_c
        return (C_new, n_new, m_new), (C, n, m)

    init = (jnp.zeros((B, H, Dh, Dh), jnp.float32), jnp.zeros((B, H, Dh), jnp.float32),
            jnp.zeros((B, H), jnp.float32))
    xs = (jnp.moveaxis(dC, 2, 0), jnp.moveaxis(dn, 2, 0), jnp.moveaxis(m_loc, 2, 0), jnp.moveaxis(A, 2, 0))
    _, (C0, n0, m0) = lax.scan(step, init, xs)
    C0 = jnp.moveaxis(C0, 0, 2)
    n0 = jnp.moveaxis(n0, 0, 2)
    m0 = jnp.moveaxis(m0, 0, 2)

    Dmat = a[..., :, None] - a[..., None, :] + li[..., None, :]
    causal = jnp.tril(jnp.ones((L, L), dtype=bool))
    Dmat = jnp.where(causal, Dmat, -jnp.inf)
    m_inter = a + m0[..., None]
    m_t = jnp.maximum(m_inter, jnp.max(Dmat, axis=-1))
    Wm = jnp.exp(Dmat - m_t[..., None])
    s_inter = jnp.exp(m_inter - m_t)
    qk = jnp.einsum('bhcjd,bhcsd->bhcjs', q, k) * Wm
    num = jnp.einsum('bhcjs,bhcse->bhcje', qk, v) + s_inter[..., None] * jnp.einsum('bhcjd,bhcde->bhcje', q, C0)
    den = jnp.sum(qk, axis=-1) + s_inter * jnp.einsum('bhcjd,bhcd->bhcj', q, n0)
    h = num / jnp.maximum(jnp.abs(den), jnp.exp(-m_t))[..., None]
    return h.reshape(B, H, S, Dh)

def s5_groups(u, lam_re, lam_im, log_dt, b_re, b_im, c_re, c_im, d, glu_w):
    S = u.shape[1]
    f32 = jnp.float32
    lam_re = lam_re.astype(f32); lam_im = lam_im.astype(f32)
    dt = jnp.exp(log_dt.astype(f32))[:, None]
    mag = jnp.exp(lam_re * dt)
    ar = mag * jnp.cos(lam_im * dt)
    ai = mag * jnp.sin(lam_im * dt)
    den = lam_re * lam_re + lam_im * lam_im
    fr = ((ar - 1.0) * lam_re + ai * lam_im) / den
    fi = (ai * lam_re - (ar - 1.0) * lam_im) / den
    b_re = b_re.astype(f32); b_im = b_im.astype(f32)
    bbr = fr[..., None] * b_re - fi[..., None] * b_im
    bbi = fr[..., None] * b_im + fi[..., None] * b_re
    xr = jnp.einsum('bsgh,gph->bsgp', u, bbr)
    xi = jnp.einsum('bsgh,gph->bsgp', u, bbi)
    G, P = ar.shape
    a_r = jnp.broadcast_to(ar[None, None], (1, S, G, P))
    a_i = jnp.broadcast_to(ai[None, None], (1, S, G, P))

    def combine(e1, e2):
        a1r, a1i, b1r, b1i = e1
        a2r, a2i, b2r, b2i = e2
        return (a1r * a2r - a1i * a2i, a1r * a2i + a1i * a2r,
                a2r * b1r - a2i * b1i + b2r, a2r * b1i + a2i * b1r + b2i)

    _, _, sr, si = lax.associative_scan(combine, (a_r, a_i, xr, xi), axis=1)
    y = (jnp.einsum('bsgp,ghp->bsgh', sr, c_re.astype(f32))
         - jnp.einsum('bsgp,ghp->bsgh', si, c_im.astype(f32))
         + d.astype(f32) * u)
    ab = jnp.einsum('bsgh,ghk->bsgk', jax.nn.gelu(y, approximate=False), glu_w.astype(f32))
    return ab[..., :S5_GROUP] * jax.nn.sigmoid(ab[..., S5_GROUP:])

def peer(x, wq, subkeys, u_tab, v_tab):
    B, S, D = x.shape
    f32 = jnp.float32
    half = PEER_QDIM // 2
    q = (x @ wq).astype(f32).reshape(B, S, PEER_HEADS, 2, half)
    s = jnp.einsum('bshpd,pkd->bshpk', q, subkeys.astype(f32))
    s1, i1 = lax.top_k(s[..., 0, :], PEER_TOPK)
    s2, i2 = lax.top_k(s[..., 1, :], PEER_TOPK)
    cand_s = (s1[..., :, None] + s2[..., None, :]).reshape(B, S, PEER_HEADS, PEER_TOPK * PEER_TOPK)
    cand_i = (i1[..., :, None] * PEER_NKEYS + i2[..., None, :]).reshape(B, S, PEER_HEADS, PEER_TOPK * PEER_TOPK)
    top_s, pos = lax.top_k(cand_s, PEER_TOPK)
    idx = jnp.take_along_axis(cand_i, pos, axis=-1)
    gate = jax.nn.softmax(top_s, axis=-1)
    T = B * S
    HK = PEER_HEADS * PEER_TOPK
    xb = x.reshape(T // PEER_BLOCK, PEER_BLOCK, D)
    ib = idx.reshape(T // PEER_BLOCK, PEER_BLOCK, HK)
    gb = gate.reshape(T // PEER_BLOCK, PEER_BLOCK, HK)

    def block(args):
        xt, it, gt = args
        ue = jnp.take(u_tab, it, axis=0)
        ve = jnp.take(v_tab, it, axis=0)
        act = jax.nn.gelu(jnp.einsum('td,ted->te', xt, ue).astype(f32), approximate=False)
        return jnp.einsum('te,ted->td', (gt * act).astype(ve.dtype), ve)

    out = lax.map(block, (xb, ib, gb))
    return out.reshape(B, S, D)

def second_inputs(seed: int = 0) -> dict:
    key = jax.random.key(seed)
    ks = jax.random.split(key, 24)
    f32 = jnp.float32
    nrm = lambda k, shape, s: jax.random.normal(k, shape, f32) * s
    L = DEPTH
    G, P, Hg = S5_GROUPS, S5_STATE, S5_GROUP
    f_bias = jnp.broadcast_to(jnp.linspace(3.0, 6.0, MLSTM_HEADS, dtype=f32), (L, MLSTM_HEADS))
    b_gates = jnp.concatenate([nrm(ks[3], (L, MLSTM_HEADS), 0.1),
                               f_bias + nrm(ks[4], (L, MLSTM_HEADS), 0.1)], axis=-1)
    lam_im0 = jnp.pi * jnp.arange(P, dtype=f32)
    log_dt = jax.random.uniform(ks[8], (L, G), f32, math.log(S5_DT_MIN), math.log(S5_DT_MAX))
    return dict(
        x=nrm(ks[0], (BATCH, SEQ, D_MODEL), 1.0),
        norm1_g=1.0 + nrm(ks[1], (L, D_MODEL), 0.1),
        w_in=nrm(ks[2], (L, D_MODEL, N_IN), D_MODEL ** -0.5),
        b_gates=b_gates,
        conv_qk_w=nrm(ks[5], (L, CONV_WIDTH, 2 * MLSTM_WIDTH), CONV_WIDTH ** -0.5),
        mlstm_norm_g=1.0 + nrm(ks[6], (L, MLSTM_WIDTH), 0.1),
        s5_lambda_re=-0.5 + nrm(ks[7], (L, G, P), 0.01),
        s5_lambda_im=lam_im0 + nrm(ks[9], (L, G, P), 0.01),
        s5_log_dt=log_dt,
        s5_b_re=nrm(ks[10], (L, G, P, Hg), (2 * Hg) ** -0.5),
        s5_b_im=nrm(ks[11], (L, G, P, Hg), (2 * Hg) ** -0.5),
        s5_c_re=nrm(ks[12], (L, G, Hg, P), P ** -0.5),
        s5_c_im=nrm(ks[13], (L, G, Hg, P), P ** -0.5),
        s5_d=nrm(ks[14], (L, G, Hg), 0.5),
        s5_glu_w=nrm(ks[15], (L, G, Hg, 2 * Hg), Hg ** -0.5),
        w_out=nrm(ks[16], (L, D_MIX, D_MODEL), D_MIX ** -0.5),
        norm2_g=1.0 + nrm(ks[17], (L, D_MODEL), 0.1),
        peer_wq=nrm(ks[18], (L, D_MODEL, PEER_HEADS * PEER_QDIM), D_MODEL ** -0.5),
        peer_subkeys=nrm(ks[19], (L, 2, PEER_NKEYS, PEER_QDIM // 2), (PEER_QDIM // 2) ** -0.5),
        peer_u=nrm(ks[20], (L, PEER_EXPERTS, D_MODEL), D_MODEL ** -0.5),
        peer_v=nrm(ks[21], (L, PEER_EXPERTS, D_MODEL), PEER_HEADS ** -0.5),
        final_g=1.0 + nrm(ks[22], (D_MODEL,), 0.1),
    )

def second_block(x, norm1_g, w_in, b_gates, conv_qk_w, mlstm_norm_g, s5_lambda_re, s5_lambda_im,
              s5_log_dt, s5_b_re, s5_b_im, s5_c_re, s5_c_im, s5_d, s5_glu_w, w_out, norm2_g,
              peer_wq, peer_subkeys, peer_u, peer_v, final_g):
    B, S, _ = x.shape
    f32 = jnp.float32
    W, H, Dh = MLSTM_WIDTH, MLSTM_HEADS, MLSTM_HEAD_DIM
    h = x
    for l in range(DEPTH):
        xn = rmsnorm(h, norm1_g[l])
        z = xn @ w_in[l]
        q, k, v, o, gates, u = jnp.split(z, [W, 2 * W, 3 * W, 4 * W, 4 * W + 2 * H], axis=-1)
        qk = jax.nn.silu(causal_dwconv(jnp.concatenate([q, k], axis=-1), conv_qk_w[l]))
        q, k = qk[..., :W], qk[..., W:]
        to_heads = lambda t: t.astype(f32).reshape(B, S, H, Dh).transpose(0, 2, 1, 3)
        gates = gates.astype(f32) + b_gates[l].astype(f32)
        li = gates[..., :H].transpose(0, 2, 1)
        lf = jax.nn.log_sigmoid(gates[..., H:]).transpose(0, 2, 1)
        hm = mlstm_chunkwise(to_heads(q), to_heads(k), to_heads(v), li, lf)
        hm = hm.transpose(0, 2, 1, 3)
        hm = hm * lax.rsqrt(jnp.mean(hm * hm, axis=-1, keepdims=True) + RMS_EPS)
        hm = hm.reshape(B, S, W) * mlstm_norm_g[l].astype(f32) * jax.nn.sigmoid(o.astype(f32))
        ys = s5_groups(u.astype(f32).reshape(B, S, S5_GROUPS, S5_GROUP),
                       s5_lambda_re[l], s5_lambda_im[l], s5_log_dt[l], s5_b_re[l], s5_b_im[l],
                       s5_c_re[l], s5_c_im[l], s5_d[l], s5_glu_w[l]).reshape(B, S, S5_WIDTH)
        mix = jnp.concatenate([hm, ys], axis=-1).astype(h.dtype) @ w_out[l]
        h = h + mix.astype(h.dtype)
        h = h + peer(rmsnorm(h, norm2_g[l]), peer_wq[l], peer_subkeys[l], peer_u[l], peer_v[l]).astype(h.dtype)
    return rmsnorm(h, final_g)


def setup_inputs(seed=0):
    out = dict(first_inputs(seed))
    for name, value in second_inputs(seed + 1).items():
        if name != "x":
            out[name + "_2"] = value
    return out


def reference(
    x, p, norm_mix_pre, norm_mix_post, norm_mlp_pre, norm_mlp_post, w_in, conv_w, conv_b,
    lru_wa, lru_ba, lru_wx, lru_bx, lru_lambda, cmp_pe_k, cmp_w1_k, cmp_w2_k, cmp_pe_v,
    cmp_w1_v, cmp_w2_v, rel_bias, gnorm_lru, gnorm_nsa, w_out, mlp_w1, mlp_w2, ple_gate,
    ple_proj, norm1_g_2, w_in_2, b_gates_2, conv_qk_w_2, mlstm_norm_g_2, s5_lambda_re_2,
    s5_lambda_im_2, s5_log_dt_2, s5_b_re_2, s5_b_im_2, s5_c_re_2, s5_c_im_2, s5_d_2, s5_glu_w_2,
    w_out_2, norm2_g_2, peer_wq_2, peer_subkeys_2, peer_u_2, peer_v_2, final_g_2,
):
    x = first_block(
        x, p, norm_mix_pre, norm_mix_post, norm_mlp_pre, norm_mlp_post, w_in, conv_w, conv_b,
        lru_wa, lru_ba, lru_wx, lru_bx, lru_lambda, cmp_pe_k, cmp_w1_k, cmp_w2_k, cmp_pe_v,
        cmp_w1_v, cmp_w2_v, rel_bias, gnorm_lru, gnorm_nsa, w_out, mlp_w1, mlp_w2, ple_gate,
        ple_proj,
    )
    return second_block(
        x, norm1_g_2, w_in_2, b_gates_2, conv_qk_w_2, mlstm_norm_g_2, s5_lambda_re_2,
        s5_lambda_im_2, s5_log_dt_2, s5_b_re_2, s5_b_im_2, s5_c_re_2, s5_c_im_2, s5_d_2,
        s5_glu_w_2, w_out_2, norm2_g_2, peer_wq_2, peer_subkeys_2, peer_u_2, peer_v_2,
        final_g_2,
    )


_drawn_inputs = setup_inputs


def setup_inputs(seed=0):
    import zlib

    import numpy as np

    out = dict(_drawn_inputs(seed))
    spreads = {}
    factors = {'lru_ba': 8.0,
     'lru_bx': 7.535,
     'cmp_pe_k': 4.124,
     's5_lambda_re_2': 64.0,
     's5_lambda_im_2': 29.616,
     's5_log_dt_2': 35.8,
     's5_b_re_2': 39.456,
     's5_b_im_2': 40.736,
     's5_c_re_2': 39.72,
     's5_c_im_2': 37.76}
    for name, (base, spread) in spreads.items():
        noise = np.random.default_rng([zlib.crc32(name.encode()), seed]).standard_normal(out[name].shape)
        drawn = base * np.exp(spread * noise) if base else spread * noise
        out[name] = __import__('jax').numpy.asarray(drawn.astype(out[name].dtype))
    for name, factor in factors.items():
        out[name] = (out[name] * factor).astype(out[name].dtype)
    return out
```

```python
from contextlib import ExitStack
import math

import numpy as np

import concourse.bass as bass
from concourse import mybir

F32 = mybir.dt.float32
U32 = mybir.dt.uint32
ALU = mybir.AluOpType
ACT = mybir.ActivationFunctionType
AX = mybir.AxisListType

P = 128
SEQ = 256
TT = SEQ // P
D = 2048
KT = D // P
EPS = 1e-6
NEG = -1e30

LRU_W = 1024
HEAD = 64
NH = 16
NKV = 4
REP = NH // NKV
CMP_LEN, CMP_STRIDE = 32, 16
NCMP = (SEQ - CMP_LEN) // CMP_STRIDE + 1
NBUCKET = 32
D_FF = 4 * D
PLE = 256

MW = 1024
MH = 4
MD = MW // MH
GROUPS, GSZ, NSTATE = 64, 16, 64
ST = GROUPS * NSTATE // P
PH = 8
NKEY = 128
TOPK = 16
PAIRS = PH * TOPK

UNIT = KT * P
SLOTS = 5
TWO_PI = 2.0 * math.pi

COLS = {}
for _name, _n in (("norm_mix_pre", 16), ("norm_mix_post", 16), ("norm_mlp_pre", 16), ("norm_mlp_post", 16),
                  ("conv_w", 32), ("conv_b", 8), ("lru_ba", 8), ("lru_bx", 8), ("lru_lambda", 8),
                  ("gnorm_lru", 8), ("gnorm_nsa", 8), ("norm1", 16), ("conv_qk", 64), ("mlstm_norm", 8),
                  ("s5_re", 32), ("s5_im", 32), ("s5_dt", 32), ("s5_d", 8), ("norm2", 16), ("final", 16)):
    COLS[_name] = (sum(n for _, n in COLS.values()), _n)
NCOLS = sum(n for _, n in COLS.values())

CONST = {}
for _name, _n in (("ident", P), ("ones", P), ("tri", P), ("causal", P), ("iota", P), ("time", SEQ), ("any", TT)):
    CONST[_name] = (sum(n for _, n in CONST.values()), _n)
NCONST = sum(n for _, n in CONST.values())


class Queue:

    def __init__(self, sem):
        self.sem, self.count, self.steps, self.seen = sem, 0, [], {}

    @property
    def now(self):
        return (self.sem, self.count)

    def wait(self, *after):
        for sem, value in after:
            if value > self.seen.get(sem.name, 0):
                self.seen[sem.name] = value
                self.steps.append(lambda e, s=sem, v=value: e.wait_ge(s, v))

    def run(self, emit, *after, count=True):
        self.wait(*after)
        if count:
            self.count += 1
            self.steps.append(lambda e: emit(e).then_inc(self.sem, 1))
        else:
            self.steps.append(emit)
        return self.now

    def play(self, engine):
        for step in self.steps:
            step(engine)


def build(nc, A, out):
    with ExitStack() as ctx:
        def sb(name, *shape):
            return ctx.enter_context(nc.sbuf_tensor(name, list(shape), F32))

        def sem(name):
            return ctx.enter_context(nc.semaphore(name))

        arena = sb("arena", P, 32768)
        xn = sb("xn", P, KT, SEQ)
        ring = sb("ring", P, SLOTS, UNIT)
        cols = sb("cols", P, NCOLS)
        const = sb("const", P, NCONST)
        sq = sb("sq", P, 2, 512)
        rstd = sb("rstd", P, SEQ)
        work = sb("work", P, 1536)
        psum = ctx.enter_context(nc.psum_tensor("psum", [P, 8, 512], F32))
        scratch = nc.dram_tensor("scratch_bias", [NH, P, 384], F32, kind="Internal").ap()
        h_save = nc.dram_tensor("scratch_h", [P, KT * SEQ], F32, kind="Internal").ap()

        T, V, A_, G = (Queue(sem(n)) for n in ("pe_done", "dve_done", "act_done", "pool_done"))
        S = Queue(sem("sp_done"))
        slot_sem = [sem(f"slot{i}") for i in range(SLOTS)]
        load_sems = []

        def col(name, i=0, n=1):
            at = COLS[name][0] + i
            return cols[:, at:at + n]

        def con(name):
            at, n = CONST[name]
            return const[:, at:at + n]

        ident, ones = con("ident"), con("ones")

        def area(at, *shape):
            n = int(np.prod(shape))
            v = arena[:, at:at + n]
            if len(shape) == 2:
                v = v.rearrange("p (a b) -> p a b", a=shape[0])
            if len(shape) == 3:
                v = v.rearrange("p (a b c) -> p a b c", a=shape[0], b=shape[1])
            return v

        h = area(0, KT, SEQ)
        y = area(4096, KT, SEQ)

        def tt(q, o, a, b, op, *after):
            return q.run(lambda e: e.tensor_tensor(o, a, b, op), *after)

        def ts(q, o, a, s1, op0, s2, op1, *after):
            if op1 is None:
                return q.run(lambda e: e.tensor_scalar(o, a, s1, None, op0), *after)
            return q.run(lambda e: e.tensor_scalar(o, a, s1, s2, op0, op1), *after)

        def stt(q, o, a, s, b, op0, op1, *after):
            return q.run(lambda e: e.scalar_tensor_tensor(out=o, in0=a, scalar=s, in1=b, op0=op0, op1=op1), *after)

        def act(o, i, func, *after, bias=0.0, scale=1.0, accum=None):
            if accum is None:
                return A_.run(lambda e: e.activation(o, i, func, bias=bias, scale=scale), *after)
            return A_.run(lambda e: e.activation(o, i, func, bias=bias, scale=scale, accum_out=accum), *after)

        def copy(q, o, i, *after):
            if q is A_:
                return act(o, i, ACT.Copy, *after)
            return q.run(lambda e: e.tensor_copy(o, i), *after)

        def fill(q, o, value, *after):
            return q.run(lambda e: e.memset(o, value), *after)

        def mm(o, l, r, start, stop, *after, count=False):
            return T.run(lambda e: e.matmul(o, l, r, start=start, stop=stop), *after, count=count)

        def tr(o, i, *after, count=False):
            n = i.shape[0]
            return T.run(lambda e: e.transpose(o, i, ident[0:n, 0:n]), *after, count=count)

        def load(pairs, *after, queue=None):
            s = sem(f"load{len(load_sems)}")
            load_sems.append(s)
            q = queue or A_
            q.wait(*after)
            for o, i in pairs:
                q.steps.append(lambda e, o=o, i=i: e.dma_start(o, i).then_inc(s, 16))
            return (s, 16 * len(pairs))

        ring_use = [0]
        slot_free = [None] * SLOTS

        def unit(src, n=UNIT):
            k = ring_use[0] % SLOTS
            ring_use[0] += 1
            if slot_free[k]:
                S.wait(slot_free[k])
            dst = ring[:, k, 0:n]
            s, v = slot_sem[k], 16 * ((ring_use[0] - 1) // SLOTS + 1)
            S.steps.append(lambda e: e.dma_start(dst, src).then_inc(s, 16))
            return k, (s, v)

        bank_free = [[] for _ in range(8)]

        def bank(b):
            return bank_free[b]

        gemm_turn = [0]

        def gemm_pair(units, x, *ready):
            b = gemm_turn[0] % 3
            gemm_turn[0] += 1
            for j, srcs in enumerate(units):
                o = psum[:, b, j * SEQ:(j + 1) * SEQ]
                for c, src in enumerate(srcs):
                    k, landed = unit(src)
                    w = ring[:, k, :].rearrange("p (k f) -> p k f", k=KT)
                    waits = [landed, *bank(b), *ready]
                    for i in range(KT):
                        last = i == KT - 1
                        r = mm(o, w[:, i, :], x[:, c * KT + i, :], c == 0 and i == 0, c == len(srcs) - 1 and last,
                               *(waits if i == 0 else ()), count=last)
                    slot_free[k] = r
            return b, r

        def gemm_tokens(srcs, x, *ready):
            b = gemm_turn[0] % 3
            gemm_turn[0] += 1
            for j, src in enumerate(srcs):
                k, landed = unit(src)
                w = ring[:, k, :].rearrange("p (k f) -> p k f", k=KT)
                waits = [landed, *bank(b), *ready]
                for t in range(TT):
                    o = psum[:, b, t * SEQ + j * P:t * SEQ + (j + 1) * P]
                    for i in range(KT):
                        last = i == KT - 1
                        r = mm(o, x[:, i, t * P:(t + 1) * P], w[:, i, :], i == 0, last,
                               *(waits if i == 0 else ()), count=last and t == TT - 1)
                slot_free[k] = r
            return b, r

        sq_free = [None, None]
        sq_turn = [0]

        def sum_squares(src, first, last, *ready, b=7):
            k = sq_turn[0] % 2
            sq_turn[0] += 1
            waits = list(ready) + ([sq_free[k]] if sq_free[k] else [])
            s = act(sq[:, k, :], src, ACT.Square, *waits)
            for j in range(2):
                r = mm(psum[:, b, 0:SEQ], ones, sq[:, k, j * SEQ:(j + 1) * SEQ], first and j == 0, last and j == 1,
                       s, *bank(b), count=j == 1)
            sq_free[k] = r
            return r

        def root(total, width, dst=None, b=7):
            dst = rstd[:, :] if dst is None else dst
            r = ts(V, dst, psum[:, b, 0:SEQ], 1.0 / width, ALU.mult, EPS, ALU.add, total, V.now, A_.now)
            bank_free[b] = [r]
            r = act(dst, dst, ACT.Sqrt, r)
            return V.run(lambda e: e.reciprocal(dst, dst), r)

        def flat(v):
            return v.rearrange("p a b -> p (a b)")

        def norm(src, dst, gain, n, *ready):
            for i in range(0, n, 2):
                r = sum_squares(flat(src[:, i:i + 2, :]), i == 0, i == n - 2, *ready)
            r = root(r, n * P)
            for i in range(n):
                r = stt(V, dst[:, i, :], src[:, i, :], col(gain, i), rstd[:, :], ALU.mult, ALU.mult, V.now, *ready)
            return r

        def project(name, x, dst, ready, per=1):
            for i in range(0, KT, 2):
                b, r = gemm_pair([[A[name][(i + j) * per + c] for c in range(per)] for j in range(2)], x, ready)
                r = copy(V, flat(dst[:, i:i + 2, :]), psum[:, b, :], r)
                bank_free[b] = [r]
                total = sum_squares(flat(dst[:, i:i + 2, :]), i == 0, i == KT - 2, r)
            return root(total, D)

        def add_normed(delta, gain, ready):
            for i in range(KT):
                r = stt(V, delta[:, i, :], delta[:, i, :], col(gain, i), rstd[:, :], ALU.mult, ALU.mult, ready)
            for i in range(0, KT, 4):
                r = tt(V, flat(h[:, i:i + 4, :]), flat(h[:, i:i + 4, :]), flat(delta[:, i:i + 4, :]), ALU.add, V.now)
            return r

        def log1p(dst, e, z, z2, *ready):
            ts(V, z, e, 2.0, ALU.add, None, None, *ready)
            V.run(lambda q: q.reciprocal(z, z), V.now)
            tt(V, z, z, e, ALU.mult, V.now)
            tt(V, z2, z, z, ALU.mult, V.now)
            ts(V, dst, z2, 1.0 / 17, ALU.mult, None, None, V.now)
            for k in range(7, 0, -1):
                stt(V, dst, dst, 1.0 / (2 * k + 1), z2, ALU.add, ALU.mult, V.now)
            stt(V, dst, dst, 1.0, z, ALU.add, ALU.mult, V.now)
            return ts(V, dst, dst, 2.0, ALU.mult, None, None, V.now)

        def softplus_neg(dst, x, neg, e, z, z2, *ready):
            ts(V, neg, x, -1.0, ALU.mult, None, None, *ready)
            r = tt(V, e, neg, x, ALU.min, V.now)
            r = act(e, e, ACT.Exp, r)
            log1p(dst, e, z, z2, r)
            return stt(V, dst, neg, 0.0, dst, ALU.max, ALU.add, V.now)

        def first_block():
            u_pad = area(8192, 8, SEQ + 3)
            gate_in = area(10272, 8, SEQ)
            q = area(12320, NH, SEQ)[0:HEAD]
            k_cmp, v_cmp, k_sel, k_win = (area(16416 + 1024 * i, NKV, SEQ)[0:HEAD] for i in range(4))
            bias = area(20512, NH, SEQ)
            bias_cmp = area(24608, TT, NCMP, NH)
            v_sel, v_win = area(25088, TT, NKV * HEAD), area(25600, TT, NKV * HEAD)
            gates = area(26112, TT, 3 * NH)
            temp = 26208
            lru_w = area(12320, 2, 8, P)
            hot_cmp = area(temp, TT * NCMP, P)[0:NBUCKET + 1]
            hot_rel = area(temp + 3840, 384)[0:NBUCKET + 1]
            tab = work[0:NBUCKET + 1, 0:NH]
            rel = arena[0:NH, temp + 4224:temp + 4608]
            spl = work[:, 16:24], work[:, 24:32], work[:, 32:40], work[:, 40:48], work[:, 48:56]
            pe = work[0:HEAD, 64:128].rearrange("p (w l) -> p w l", w=2)
            w2 = work[:, 128:384].rearrange("p (w f d) -> p w f d", w=2, f=2)

            small = load([(tab[0:NBUCKET], A["rel_bias"]), (hot_cmp, A["hot_cmp"]), (hot_rel, A["hot_rel"]),
                          (pe, A["cmp_pe"]), (w2, A["cmp_w2"])])
            r = fill(V, tab[NBUCKET:NBUCKET + 1], NEG)
            cleared = fill(G, lru_w, 0.0)
            fill(G, u_pad[:, :, 0:3], 0.0)
            lru_loaded = load([(lru_w[g * 64:g * 64 + 64, :, :, g * 64:g * 64 + 64], A["lru_w"][g]) for g in range(2)],
                              cleared)

            r = mm(psum[0:NH, 3, 0:384], tab, hot_rel, True, True, small, r, count=True)
            r = copy(V, rel, psum[0:NH, 3, 0:384], r)
            bank_free[3] = [r]
            stored = load([(scratch, rel.unsqueeze(1).broadcast_to([NH, P, 384]))], r)
            toeplitz = bass.AP(tensor=scratch.tensor, offset=P - 1, ap=[[383, P], [P * 384, NH], [1, SEQ]])
            bias_ready = load([(bias, toeplitz)], stored)
            for i in range(TT * NCMP):
                r = mm(psum[:, 4, i * NH:(i + 1) * NH], hot_cmp[:, i, :], tab, True, True,
                       count=i == TT * NCMP - 1)
            r = copy(V, bias_cmp.rearrange("p a b c -> p (a b c)"), psum[:, 4, 0:TT * NCMP * NH], r)
            bank_free[4] = [r]

            softplus_neg(spl[0], col("lru_lambda", 0, 8), *spl[1:])
            ts(V, spl[0], spl[0], 8.0, ALU.mult, None, None, V.now)
            decay_ready = ts(V, spl[1], spl[0], -1.0, ALU.mult, None, None, V.now)

            normed = norm(h, xn, "norm_mix_pre", KT)

            def features(first):
                return gemm_pair([[A["w_in"][first + j]] for j in range(2)], xn, normed)

            for i in range(0, 8, 2):
                b, r = features(i)
                bank_free[b] = [copy(V, u_pad[:, i:i + 2, 3:], psum[:, b, :].rearrange("p (a t) -> p a t", a=2),
                                     r, G.now)]
            for i in range(0, 8, 2):
                b, r = features(8 + i)
                bank_free[b] = [copy(A_, flat(gate_in[:, i:i + 2, :]), psum[:, b, :], r)]

            def lru_half(first):
                xc, rg, ig, th, dec = (area(temp + 1024 * i, 4, SEQ) for i in range(5))
                for i in range(4):
                    f = first + i
                    ts(V, xc[:, i, :], u_pad[:, f, 0:SEQ], col("conv_w", f), ALU.mult, col("conv_b", f), ALU.add,
                       V.now, bias_ready)
                    for k in range(1, 4):
                        conv = stt(V, xc[:, i, :], u_pad[:, f, k:k + SEQ], col("conv_w", 8 * k + f), xc[:, i, :],
                                   ALU.mult, ALU.add, V.now)
                    b = 3 + i % 2
                    mm(psum[:, b, 0:SEQ], lru_w[:, 0, f, :], xc[:, i, :], True, True, conv, lru_loaded, *bank(b))
                    r = mm(psum[:, b, SEQ:], lru_w[:, 1, f, :], xc[:, i, :], True, True, count=True)
                    act(rg[:, i, :], psum[:, b, 0:SEQ], ACT.Sigmoid, r, V.now, bias=col("lru_ba", f))
                    bank_free[b] = [act(ig[:, i, :], psum[:, b, SEQ:], ACT.Sigmoid, bias=col("lru_bx", f))]
                for i in range(4):
                    act(th[:, i, :], rg[:, i, :], ACT.Tanh, A_.now, decay_ready,
                        scale=spl[0][:, first + i:first + i + 1])
                tanhs = A_.now
                for i in range(4):
                    act(dec[:, i, :], rg[:, i, :], ACT.Exp, scale=spl[1][:, first + i:first + i + 1])
                decays = A_.now
                th, rg, ig, xc = flat(th), flat(rg), flat(ig), flat(xc)
                ts(V, rg, th, 1.0, ALU.add, None, None, decays, tanhs)
                V.run(lambda e: e.reciprocal(rg, rg), V.now)
                r = tt(V, th, th, rg, ALU.mult, V.now)
                root_b = act(th, th, ACT.Sqrt, r, scale=2.0)
                tt(G, ig, ig, xc, ALU.mult, A_.now)
                r = tt(G, ig, ig, th, ALU.mult, root_b, G.now)
                gt = flat(gate_in[:, first:first + 4, :])
                gelu = act(gt, gt, ACT.Gelu_apprx_tanh)
                for i in range(4):
                    s = slice(i * SEQ, (i + 1) * SEQ)
                    o, a, bb = rg[:, s], flat(dec)[:, s], ig[:, s]
                    V.run(lambda e, o=o, a=a, bb=bb: e.tensor_tensor_scan(o, a, bb, 0.0, ALU.mult, ALU.add),
                          r, V.now, decays)
                return tt(V, flat(y[:, first:first + 4, :]), rg, gt, ALU.mult, V.now, gelu)

            def to_heads(dst, first, b, r, scale):
                src = psum[:, b, :].rearrange("p (a t) -> p a t", a=2)
                d = dst[:, first:first + 4, :].rearrange("p (a two) t -> p a two t", two=2)
                act(d[:, :, 0, :], src[0:HEAD], ACT.Copy, r, scale=scale)
                bank_free[b] = [act(d[:, :, 1, :], src[HEAD:P], ACT.Copy, scale=scale)]

            def to_tokens(dst, first):
                b, r = gemm_tokens([A["w_in"][first], A["w_in"][first + 1]], xn, normed)
                bank_free[b] = [copy(A_, flat(dst), psum[:, b, :], r)]

            b, r = features(24)
            to_heads(k_cmp, 0, b, r, 1.0)
            lru_half(0)
            b, r = features(26)
            to_heads(v_cmp, 0, b, r, 1.0)
            b, r = features(28)
            to_heads(k_sel, 0, b, r, 1.0)
            b, r = features(32)
            to_heads(k_win, 0, b, r, 1.0)
            lru_half(4)
            lru_done = T.now
            for i in range(0, 8, 2):
                b, r = features(16 + i)
                to_heads(q, 2 * i, b, r, HEAD ** -0.5)
            to_tokens(v_sel, 30)
            to_tokens(v_win, 34)
            k, landed = unit(A["w_gates"], KT * 3 * NH)
            wg = ring[:, k, 0:KT * 3 * NH].rearrange("p (k f) -> p k f", k=KT)
            for t in range(TT):
                for i in range(KT):
                    r = mm(psum[:, 5, t * 48:(t + 1) * 48], xn[:, i, t * P:(t + 1) * P], wg[:, i, :], i == 0,
                           i == KT - 1, landed, *bank(5), count=t == TT - 1 and i == KT - 1)
            slot_free[k] = r
            bank_free[5] = [act(flat(gates), psum[:, 5, 0:96], ACT.Sigmoid, r)]
            projected = T.now

            lru_all = V.now
            kc = work[0:HEAD, 384:444]
            vc = work[0:NCMP, 448:704].rearrange("p (g d) -> p g d", g=NKV)
            for w, src in enumerate((k_cmp, v_cmp)):
                blk = area(temp + 1024 * w, KT, NKV * NCMP)
                hid = area(temp + 2048 + 128 * w, 2, NKV * NCMP)
                for m in range(2):
                    for par in range(2):
                        for g in range(NKV):
                            v = src[:, g, :].rearrange("p (a kk two) -> p kk two a", kk=8, two=2)[:, :, par, m:m + NCMP]
                            o = blk[64 * par:64 * par + 64, 8 * m:8 * m + 8, g * NCMP:(g + 1) * NCMP]
                            e = pe[:, w, :].rearrange("p (m kk two) -> p m kk two", m=2, two=2)[:, m, :, par]
                            tt(V, o, v, e.unsqueeze(2).broadcast_to([HEAD, 8, NCMP]), ALU.add,
                               A_.now, lru_all, lru_done, small)
                blk_ready = V.now
                for f in range(2):
                    k, landed = unit(A["cmp_w1"][w, f])
                    wk = ring[:, k, :].rearrange("p (k f) -> p k f", k=KT)
                    for i in range(KT):
                        r = mm(psum[:, 6, f * 60:(f + 1) * 60], wk[:, i, :], blk[:, i, :], i == 0, i == KT - 1,
                               landed, blk_ready, *bank(6), count=i == KT - 1)
                    slot_free[k] = r
                r = act(flat(hid), psum[:, 6, 0:120], ACT.Gelu_apprx_tanh, r)
                bank_free[6] = [r]
                if w == 0:
                    for f in range(2):
                        r = mm(psum[0:HEAD, 6, 128:188], w2[:, 0, f, :], hid[:, f, :], f == 0, f == 1, r, small,
                               count=f == 1)
                    r = copy(V, kc, psum[0:HEAD, 6, 128:188], r)
                else:
                    for g in range(NKV):
                        for f in range(2):
                            r2 = mm(psum[0:NCMP, 6, 128 + 64 * g:192 + 64 * g], hid[:, f, g * NCMP:(g + 1) * NCMP],
                                    w2[:, 1, f, :], f == 0, f == 1, r, count=g == NKV - 1 and f == 1)
                    r = copy(V, vc.rearrange("p g d -> p (g d)"), psum[0:NCMP, 6, 128:384], r2)
                bank_free[6] = [r]
            compressed = V.now

            norm(y[:, 0:8, :], y[:, 0:8, :], "gnorm_lru", 8, compressed)

            pv_done = [None, None]

            def buffers(g):
                base = (lambda a, n: flat(xn[:, :, :])[:, a:a + n]) if g % 2 == 0 else \
                    (lambda a, n: arena[:, temp + a:temp + a + n])
                p0 = [base(1536 * w, 512).rearrange("p (h s) -> p h s", h=REP) for w in range(2)]
                p1 = [base(1536 * w + 512, 1024).rearrange("p (h s) -> p h s", h=REP) for w in range(2)]
                pc = work[:, 704 + 120 * (g % 2):824 + 120 * (g % 2)].rearrange("p (t h n) -> p t h n", t=TT, h=REP)
                st = work[:, 944 + 64 * (g % 2):1008 + 64 * (g % 2)]
                return p0, p1, pc, st

            def softmaxes(g):
                p0, p1, pc, st = buffers(g)
                before = [pv_done[g % 2]] if pv_done[g % 2] else [compressed, projected]
                hs = slice(REP * g, REP * g + REP)
                gate = gates.rearrange("p t (h b) -> p t h b", b=3)
                ps = psum[:, 2, 0:120].rearrange("p (t h n) -> p t h n", t=TT, h=REP)
                for t in range(TT):
                    for i in range(REP):
                        r = mm(ps[:, t, i, :], q[:, REP * g + i, t * P:(t + 1) * P], kc[:, g * NCMP:(g + 1) * NCMP],
                               True, True, A_.now, compressed, *bank(2), count=t == TT - 1 and i == REP - 1)
                for t in range(TT):
                    r = tt(V, pc[:, t], ps[:, t], bias_cmp[:, t, :, hs].rearrange("p n h -> p h n"), ALU.add,
                           r, *before)
                bank_free[2] = [r]
                top = st[:, 0:8].rearrange("p (t h) -> p t h", t=TT)
                tot = st[:, 8:16].rearrange("p (t h) -> p t h", t=TT)
                wide = [P, REP, NCMP]
                V.run(lambda e: e.tensor_reduce(top, pc, AX.X, ALU.max), V.now)
                for t in range(TT):
                    tt(V, pc[:, t], pc[:, t], top[:, t].unsqueeze(2).broadcast_to(wide), ALU.subtract, V.now)
                pcf = pc.rearrange("p t h n -> p (t h n)")
                r = act(pcf, pcf, ACT.Exp, V.now)
                V.run(lambda e: e.tensor_reduce(tot, pc, AX.X, ALU.add), r)
                V.run(lambda e: e.reciprocal(tot, tot), V.now)
                for t in range(TT):
                    ts(V, tot[:, t], tot[:, t], con("any")[:, t:t + 1], ALU.mult, None, None, V.now)
                tt(V, tot, tot, gate[:, :, hs, 0], ALU.mult, V.now)
                for t in range(TT):
                    tt(V, pc[:, t], pc[:, t], tot[:, t].unsqueeze(2).broadcast_to(wide), ALU.mult, V.now)
                for w, keys in enumerate((k_sel, k_win)):
                    mx = st[:, 16 + 16 * w:24 + 16 * w]
                    sm = st[:, 24 + 16 * w:32 + 16 * w]
                    s0 = psum[:, 3, :].rearrange("p (h s) -> p h s", h=REP)
                    s1 = psum[:, 4:6, :].rearrange("p b (h s) -> p (b h) s", h=2)
                    for i in range(REP):
                        r0 = mm(s0[:, i, :], q[:, REP * g + i, 0:P], keys[:, g, 0:P], True, True, *bank(3),
                                count=i == REP - 1)
                    for i in range(REP):
                        r1 = mm(s1[:, i, :], q[:, REP * g + i, P:SEQ], keys[:, g, :], True, True, *bank(4),
                                *bank(5), count=i == REP - 1)
                    bank_free[3] = [tt(V, p0[w], s0, bias[:, hs, P:SEQ], ALU.add, r0, bias_ready, *before)]
                    bank_free[4] = bank_free[5] = [tt(V, p1[w], s1, bias[:, hs, :], ALU.add, r1)]
                    V.run(lambda e, m=mx, p=p0[w]: e.tensor_reduce(m[:, 0:4], p, AX.X, ALU.max), V.now)
                    V.run(lambda e, m=mx, p=p1[w]: e.tensor_reduce(m[:, 4:8], p, AX.X, ALU.max), V.now)
                    r = ts(V, mx, mx, -1.0, ALU.mult, None, None, V.now)
                    for t, p in enumerate((p0[w], p1[w])):
                        for i in range(REP):
                            j = REP * t + i
                            act(p[:, i, :], p[:, i, :], ACT.Exp, r, bias=mx[:, j:j + 1], accum=sm[:, j:j + 1])
                    r = V.run(lambda e, m=sm: e.reciprocal(m, m), A_.now)
                    r = tt(V, sm.rearrange("p (t h) -> p t h", t=TT), sm.rearrange("p (t h) -> p t h", t=TT),
                           gate[:, :, hs, 1 + w], ALU.mult, V.now)
                    tt(V, p0[w], p0[w], sm[:, 0:4].unsqueeze(2).broadcast_to([P, REP, P]), ALU.mult, V.now)
                    tt(G, p1[w], p1[w], sm[:, 4:8].unsqueeze(2).broadcast_to([P, REP, SEQ]), ALU.mult, r)
                return [V.now, G.now]

            turned_free = [[], []]
            turn = [0]

            def outputs(g, ready):
                p0, p1, pc, st = buffers(g)
                for i in range(REP):
                    k = turn[0] % 2
                    turn[0] += 1
                    hd = REP * g + i
                    turned = area(temp + 3072 + 1024 * k, 1024)
                    for w in range(2):
                        b = 6 if w == 0 else 1
                        tr(psum[:, b, 0:P], p0[w][:, i, :], *ready, *bank(b))
                        tr(psum[:, b, P:2 * P], p1[w][:, i, 0:P])
                        tr(psum[:, b, 2 * P:3 * P], p1[w][:, i, P:SEQ])
                        r = tr(psum[0:NCMP, b, 3 * P:4 * P], pc[:, w, i, :], count=True)
                        q_ = A_ if w == 0 else V
                        copy(q_, turned[:, 384 * w:384 * w + 384], psum[:, b, 0:384], r, *turned_free[k])
                        c = copy(q_, turned[0:NCMP, 768 + P * w:768 + P * w + P], psum[0:NCMP, b, 384:512])
                        bank_free[b] = [c]
                    o = psum[0:HEAD, 7, 0:SEQ]
                    late = psum[0:HEAD, 7, P:SEQ]
                    for w, v in enumerate((v_sel, v_win)):
                        d = slice(g * HEAD, (g + 1) * HEAD)
                        mm(o, v[:, 0, d], turned[:, 384 * w:384 * w + 256], w == 0, False, V.now, A_.now, *bank(7))
                        mm(late, v[:, 1, d], turned[:, 384 * w + 256:384 * w + 384], False, False)
                    r = mm(o, vc[:, g, :], turned[0:NCMP, 768:1024], False, True, count=True)
                    turned_free[k] = [r]
                    at = HEAD * (hd % 2)
                    bank_free[7] = [copy(A_, y[at:at + HEAD, 8 + hd // 2, :], o, r)]
                pv_done[g % 2] = T.now

            ready = softmaxes(0)
            for g in range(NKV):
                following = softmaxes(g + 1) if g + 1 < NKV else None
                outputs(g, ready)
                ready = following
            r = norm(y[:, 8:16, :], y[:, 8:16, :], "gnorm_nsa", 8, A_.now)

            o = area(24576, KT, SEQ)
            r = project("w_out", y, o, V.now)
            r = add_normed(o, "norm_mix_post", r)

            hidden = area(8192, D_FF // P, SEQ)
            r = norm(h, xn, "norm_mlp_pre", KT, r)
            for i in range(0, D_FF // P, 2):
                b, g_ = gemm_pair([[A["mlp_w1"][i + j]] for j in range(2)], xn, r)
                hd = flat(hidden[:, i:i + 2, :])
                s = act(hd, psum[:, b, :], ACT.Relu, g_)
                bank_free[b] = [s]
                tt(V, hd, hd, hd, ALU.mult, s)
            o = area(24576, KT, SEQ)
            r = project("mlp_w2", hidden, o, V.now, per=4)
            r = add_normed(o, "norm_mlp_post", r)

            emb = area(8192, KT, SEQ)
            pt = work[:, 0:512].rearrange("p (k t) -> p k t", k=2)
            p_in = load([(pt, A["p"])], T.now, V.now)
            for c in range(2):
                k, landed = unit(A["ple_proj"][c])
                w = ring[:, k, :].rearrange("p (f k j) -> p f k j", f=8, k=2)
                for f in range(0, 8, 2):
                    b = gemm_turn[0] % 3
                    gemm_turn[0] += 1
                    for j in range(2):
                        for i in range(2):
                            g_ = mm(psum[:, b, j * SEQ:(j + 1) * SEQ], w[:, f + j, i, :], pt[:, i, :], i == 0, i == 1,
                                    landed, p_in, *bank(b), count=i == 1 and j == 1)
                    bank_free[b] = [copy(A_, flat(emb[:, 8 * c + f:8 * c + f + 2, :]), psum[:, b, :], g_)]
                slot_free[k] = g_
            sig = area(12288, KT, SEQ)
            for i in range(0, KT, 2):
                b, g_ = gemm_pair([[A["ple_gate"][i + j]] for j in range(2)], h, r)
                s = act(flat(sig[:, i:i + 2, :]), psum[:, b, :], ACT.Sigmoid, g_)
                bank_free[b] = [s]
                e2 = flat(emb[:, i:i + 2, :])
                tt(V, e2, e2, flat(sig[:, i:i + 2, :]), ALU.mult, s)
            for i in range(0, KT, 4):
                tt(V, flat(h[:, i:i + 4, :]), flat(h[:, i:i + 4, :]), flat(emb[:, i:i + 4, :]), ALU.add, V.now, T.now)

        def second_block():
            u = area(8192, 8, SEQ)
            qk_pad = area(10240, KT, SEQ + 3)
            qk = area(14400, KT, SEQ)
            v = area(18496, TT, MW)
            sig_o = area(20544, 8, SEQ)
            b_w = area(22592, 8, 2, P)
            c_w = area(24640, 2, ST, 32)
            glu_w = area(26688, 8, 2, P)
            temp = 28736

            small = [work[:, 32 * i:32 * i + 32] for i in range(30)]
            gl = work[:, 960:976].rearrange("p (t g) -> p t g", t=TT)
            bg = work[:, 976:992]
            in_before = [V.now, A_.now, G.now, T.now]
            fill(G, b_w.rearrange("p a b c -> p (a b c)"), 0.0, *in_before)
            fill(G, c_w.rearrange("p a b c -> p (a b c)"), 0.0)
            fill(G, glu_w.rearrange("p a b c -> p (a b c)"), 0.0)
            cleared = fill(G, qk_pad[:, :, 0:3], 0.0)
            pieces = [(bg, A["b_gates2"])]
            for r in range(4):
                for g in range(2):
                    a = 32 * r + 16 * g
                    pieces += [(b_w[a:a + 16, :, c, 64 * g:64 * g + 64], A["s5_b"][r, g, :, :, c, :]) for c in range(2)]
            for g in range(2):
                pieces += [(c_w[64 * g:64 * g + 64, c, :, 16 * g:16 * g + 16], A["s5_c"][g, :, c]) for c in range(2)]
            for g in range(8):
                a = 16 * g
                pieces += [(glu_w[a:a + 16, :, c, a:a + 16], A["s5_glu"][g, :, :, c, :]) for c in range(2)]
            params = load(pieces, cleared)

            normed = norm(h, xn, "norm1", KT, *in_before)

            (dt, x, th, n, ang, tn, em1, mag, hs, sn1, cm1, cs1, arm1, ai, den, fr, fi, phi, t0) = small[:19]
            lre, lim = col("s5_re", 0, ST), col("s5_im", 0, ST)
            magic = 1.5 * 2.0 ** 23
            r = act(dt, col("s5_dt", 0, ST), ACT.Exp, *in_before)
            tt(V, x, lre, dt, ALU.mult, r)
            tt(V, th, lim, dt, ALU.mult)
            ts(V, n, th, 1.0 / TWO_PI, ALU.mult, None, None, V.now)
            ts(V, n, n, magic, ALU.add, magic, ALU.subtract, V.now)
            p1 = 6.28125
            p2 = float(np.float32(np.round((TWO_PI - p1) * 2 ** 24) / 2 ** 24))
            p3 = TWO_PI - p1 - p2
            stt(V, ang, n, -p1, th, ALU.mult, ALU.add, V.now)
            stt(V, ang, n, -p2, ang, ALU.mult, ALU.add, V.now)
            stt(V, ang, n, -p3, ang, ALU.mult, ALU.add, V.now)
            ts(V, ang, ang, 3.1415925, ALU.min, -3.1415925, ALU.max, V.now)
            r = ts(V, phi, ang, 1.0 / TWO_PI, ALU.mult, None, None, V.now)
            act(tn, x, ACT.Tanh, r, scale=0.5)
            act(hs, ang, ACT.Sin, scale=0.5)
            r = act(sn1, ang, ACT.Sin)
            ts(V, t0, tn, -1.0, ALU.mult, 1.0, ALU.add, r)
            V.run(lambda e: e.reciprocal(t0, t0), V.now)
            stt(V, em1, tn, 2.0, t0, ALU.mult, ALU.mult, V.now)
            ts(V, mag, em1, 1.0, ALU.add, None, None, V.now)
            stt(V, cm1, hs, -2.0, hs, ALU.mult, ALU.mult, V.now)
            ts(V, cs1, cm1, 1.0, ALU.add, None, None, V.now)
            tt(V, ai, mag, sn1, ALU.mult, V.now)
            tt(V, arm1, em1, cs1, ALU.mult, V.now)
            tt(V, arm1, arm1, cm1, ALU.add, V.now)
            tt(V, den, lre, lre, ALU.mult)
            tt(V, t0, lim, lim, ALU.mult, V.now)
            tt(V, den, den, t0, ALU.add, V.now)
            V.run(lambda e: e.reciprocal(den, den), V.now)
            tt(V, fr, arm1, lre, ALU.mult, V.now)
            tt(V, t0, ai, lim, ALU.mult, V.now)
            tt(V, fr, fr, t0, ALU.add, V.now)
            tt(V, fr, fr, den, ALU.mult, V.now)
            tt(V, fi, ai, lre, ALU.mult, V.now)
            tt(V, t0, arm1, lim, ALU.mult, V.now)
            tt(V, fi, fi, t0, ALU.subtract, V.now)
            tt(V, fi, fi, den, ALU.mult, V.now)
            c_re, c_im = c_w[:, 0], c_w[:, 1]
            wide = [P, ST, 32]
            frb, fib = fr.unsqueeze(2).broadcast_to(wide), fi.unsqueeze(2).broadcast_to(wide)
            tmp = [area(temp + 1024 * i, ST, 32) for i in range(3)]
            tt(G, tmp[0], c_re, frb, ALU.mult, params, V.now)
            tt(G, tmp[1], c_im, fib, ALU.mult)
            tt(G, tmp[2], c_re, fib, ALU.mult)
            tt(G, c_im, c_im, frb, ALU.mult, G.now)
            tt(G, c_re, tmp[0], tmp[1], ALU.subtract, G.now)
            tt(G, c_im, tmp[2], c_im, ALU.add, G.now)
            c_ready = G.run(lambda e: e.tensor_scalar(c_im, c_im, -1.0, None, ALU.mult), G.now)

            for i in range(0, 8, 2):
                b, r = gemm_pair([[A["w_in2"][32 + i + j]] for j in range(2)], xn, normed)
                bank_free[b] = [copy(A_, flat(u[:, i:i + 2, :]), psum[:, b, :], r)]
            u_ready = A_.now

            def wide2(v):
                return v.rearrange("p (a t) -> p a t", a=2)

            hold = [arena[:, temp + 512 * i:temp + 512 * i + 512] for i in range(7)]
            spare = [arena[:, 4096 + 512 * i:4608 + 512 * i] for i in range(4)]
            t1, t2, w1, w2 = hold[0], hold[1], hold[2], hold[3]
            trig = [(hold[4], hold[5]), (spare[0], spare[1])]
            state = [(hold[6], spare[2]), (spare[3], work[:, 1024:1536])]
            step_reads = [[], []]

            def s5_in(p):
                sn, cs = trig[p % 2]
                zr, zi = state[p % 2]
                free = step_reads[p % 2] + [c_ready]
                for j in range(2):
                    act(zr[:, j * SEQ:(j + 1) * SEQ], con("time"), ACT.Copy, *free,
                        scale=phi[:, 2 * p + j:2 * p + j + 1])
                ts(V, zi, zr, magic, ALU.add, magic, ALU.subtract, A_.now, *free)
                r = tt(V, zr, zr, zi, ALU.subtract, V.now)
                below = float(np.nextafter(np.float32(TWO_PI), np.float32(0)))
                act(sn, zr, ACT.Sin, r, scale=below)
                act(cs, zr, ACT.Sin, scale=below / 2)
                r = act(cs, cs, ACT.Square, A_.now)
                trig_ready = ts(V, cs, cs, -2.0, ALU.mult, 1.0, ALU.add, r)
                for j in range(2):
                    i = 2 * p + j
                    a, f = 32 * (i % 4), i // 4
                    for c in range(2):
                        r = mm(psum[:, 3 + j, c * SEQ:(c + 1) * SEQ], b_w[a:a + 32, f, c, :], u[a:a + 32, f, :],
                               True, True, params, u_ready, *bank(3 + j), count=c == 1)
                ps = psum[:, 3:5, :].rearrange("p a (c t) -> p a c t", c=2)
                br, bi = ps[:, :, 0, :], ps[:, :, 1, :]
                tt(V, wide2(t1), wide2(cs), br, ALU.mult, r, trig_ready, G.now, A_.now)
                tt(V, wide2(t2), wide2(sn), bi, ALU.mult)
                tt(V, zr, t1, t2, ALU.add, V.now)
                tt(V, wide2(t1), wide2(cs), bi, ALU.mult, V.now)
                tt(V, wide2(t2), wide2(sn), br, ALU.mult)
                bank_free[3] = bank_free[4] = [V.now]
                tt(V, zi, t1, t2, ALU.subtract, V.now)
                for j in range(2):
                    s = slice(j * SEQ, (j + 1) * SEQ)
                    m = mag[:, 2 * p + j:2 * p + j + 1].broadcast_to([P, SEQ])
                    for o, z in ((w1, zr), (w2, zi)):
                        r = V.run(lambda e, o=o[:, s], z=z[:, s], m=m: e.tensor_tensor_scan(
                            o, m, z, 0.0, ALU.mult, ALU.add), V.now)
                tt(G, zr, cs, w1, ALU.mult, r)
                tt(G, t1, sn, w2, ALU.mult)
                tt(G, zi, sn, w1, ALU.mult)
                tt(G, t2, cs, w2, ALU.mult)
                tt(G, zr, zr, t1, ALU.subtract, G.now)
                return tt(G, zi, zi, t2, ALU.add, G.now)

            def s5_out(p, ready):
                zr, zi = state[p % 2]
                for j in range(2):
                    i = 2 * p + j
                    a = 32 * (i % 4)
                    o = psum[a:a + 32, 5, 0:SEQ]
                    s = slice(j * SEQ, (j + 1) * SEQ)
                    mm(o, c_w[:, 0, i, :], zr[:, s], True, False, ready, *bank(5))
                    r = mm(o, c_w[:, 1, i, :], zi[:, s], False, True, count=j == 1)
                step_reads[p % 2] = [r, G.now, V.now]
                if p % 2:
                    f = p // 2
                    bank_free[5] = [stt(V, u[:, f, :], u[:, f, :], col("s5_d", f), psum[:, 5, 0:SEQ], ALU.mult,
                                        ALU.add, r)]

            def conv(i):
                o = qk[:, i, :]
                ts(V, o, qk_pad[:, i, 0:SEQ], col("conv_qk", i), ALU.mult, None, None, V.now)
                for k in range(1, 4):
                    stt(V, o, qk_pad[:, i, k:k + SEQ], col("conv_qk", KT * k + i), o, ALU.mult, ALU.add, V.now)

            pending = []
            for p in range(16):
                if p < 8:
                    b, r = gemm_pair([[A["w_in2"][2 * p + j]] for j in range(2)], xn, normed)
                    bank_free[b] = [copy(V, qk_pad[:, 2 * p:2 * p + 2, 3:], wide2(psum[:, b, :]), r, cleared)]
                elif p < 12:
                    f = 2 * (p - 8)
                    b, r = gemm_tokens([A["w_in2"][16 + f + j] for j in range(2)], xn, normed)
                    bank_free[b] = [copy(A_, v[:, :, f * P:(f + 2) * P], wide2(psum[:, b, :]), r)]
                else:
                    f = 2 * (p - 12)
                    b, r = gemm_pair([[A["w_in2"][24 + f + j]] for j in range(2)], xn, normed)
                    bank_free[b] = [copy(A_, flat(sig_o[:, f:f + 2, :]), psum[:, b, :], r)]
                if len(pending) == 2:
                    s5_out(*pending.pop(0))
                pending.append((p, s5_in(p)))
                if p < 8:
                    conv(2 * p)
                    conv(2 * p + 1)
            k, landed = unit(A["w_gates2"], KT * 8)
            wg = ring[:, k, 0:KT * 8].rearrange("p (k f) -> p k f", k=KT)
            for t in range(TT):
                for i in range(KT):
                    r = mm(psum[:, 7, t * 8:(t + 1) * 8], xn[:, i, t * P:(t + 1) * P], wg[:, i, :], i == 0,
                           i == KT - 1, landed, *bank(7), count=t == TT - 1 and i == KT - 1)
            slot_free[k] = r
            glf = work[:, 960:976]
            tt(V, glf, psum[:, 7, 0:16], bg, ALU.add, r, params)
            bank_free[7] = [V.now]
            for item in pending:
                s5_out(*item)

            uf = flat(u)
            r = act(uf, uf, ACT.Gelu, V.now)
            for f in range(8):
                b = 3 + f % 2
                mm(psum[:, b, 0:SEQ], glu_w[:, f, 0, :], u[:, f, :], True, True, r, params, *bank(b))
                g_ = mm(psum[:, b, SEQ:], glu_w[:, f, 1, :], u[:, f, :], True, True, count=True)
                s = act(t1[:, SEQ * (f % 2):SEQ * (f % 2) + SEQ], psum[:, b, SEQ:], ACT.Sigmoid, g_, V.now, G.now)
                bank_free[b] = [tt(V, y[:, 8 + f, :], psum[:, b, 0:SEQ], t1[:, SEQ * (f % 2):SEQ * (f % 2) + SEQ],
                                   ALU.mult, s)]

            sof = flat(sig_o)
            act(sof, sof, ACT.Sigmoid)
            s5_done = [V.now, G.now, T.now]
            sm = work[:, 0:960].rearrange("p (i t h) -> p i t h", t=TT, h=MH)[:, 0:40]
            lf, e_, z_, z2_, ng, a_, tot, c_, mx, mt, nmt, si, em, w_ = (sm[:, i] for i in range(14))
            fl = [(sm[:, i].rearrange("p t h -> p (t h)")) for i in range(40)]
            xg = gl[:, :, MH:2 * MH]
            li = gl[:, :, 0:MH]
            copy(V, sm[:, 14], xg, *s5_done)
            softplus_neg(fl[0], fl[14], fl[4], fl[1], fl[2], fl[3], V.now)
            r = ts(V, fl[0], fl[0], -1.0, ALU.mult, None, None, V.now)
            r2 = act(flat(qk), flat(qk), ACT.Silu, r)
            mm(psum[:, 7, 0:8], con("tri"), fl[0], True, True, r, *bank(7))
            r = mm(psum[:, 7, 8:16], ones, fl[0], True, True, count=True)
            bank_free[7] = [V.run(lambda e: e.tensor_copy(work[:, 40:56], psum[:, 7, 0:16]), r)]
            tt(V, c_, li, a_, ALU.subtract, V.now)
            diag = area(10240, 8, P)
            for i in range(8):
                r = ts(V, diag[:, i, :], ident, fl[7][:, i:i + 1], ALU.mult, None, None, V.now, A_.now, T.now)
            for t in range(TT):
                r2 = mm(psum[:, 3 + t, :], ones, diag[:, MH * t:MH * t + MH, :].rearrange("p a b -> p (a b)"),
                        True, True, r, *bank(3 + t), count=True)
                ps = psum[:, 3 + t, :].rearrange("p (h s) -> p h s", h=MH)
                if t == 0:
                    V.run(lambda e, ps=ps: e.tensor_reduce(fl[15][:, 0:4], ps, AX.X, ALU.max), r2)
                for hd in range(MH):
                    stt(V, diag[:, MH * t + hd, :], ps[:, hd, :], a_[:, t, hd:hd + 1], con("causal"), ALU.add,
                        ALU.add, r2)
                bank_free[3 + t] = [V.now]
            V.run(lambda e: e.tensor_reduce(fl[8], diag, AX.X, ALU.max), V.now)
            m1, wl = fl[16][:, 0:4], fl[17][:, 0:4]
            tt(V, m1, fl[15][:, 0:4], tot[:, 0], ALU.add, V.now)
            tt(V, m1, m1, tot[:, 0], ALU.max, V.now)
            tt(V, wl, c_[:, 0], tot[:, 0], ALU.add, V.now)
            tt(V, wl, wl, m1, ALU.subtract, V.now)
            mi = sm[:, 18]
            copy(V, mi[:, 0], a_[:, 0], V.now)
            tt(V, mi[:, 1], a_[:, 1], m1, ALU.add, V.now)
            tt(V, fl[9], fl[8], fl[18], ALU.max, V.now)
            ts(V, fl[10], fl[9], -1.0, ALU.mult, None, None, V.now)
            r = tt(V, fl[11], fl[18], fl[9], ALU.subtract, V.now)
            act(wl, wl, ACT.Exp, r)
            act(fl[11], fl[11], ACT.Exp)
            act(fl[12], fl[10], ACT.Exp)
            for i in range(8):
                act(diag[:, i, :], diag[:, i, :], ACT.Exp, bias=fl[10][:, i:i + 1])
            ts(V, fl[11], fl[11], MD ** -0.5, ALU.mult, None, None, A_.now)
            weights_ready = V.now

            k_tok = area(11264, MH, MD)
            for hd in range(MH):
                b = 5 + hd % 2
                for j in range(2):
                    r = tr(psum[:, b, j * P:(j + 1) * P], qk[:, 8 + 2 * hd + j, 0:P], A_.now, *bank(b), count=j == 1)
                bank_free[b] = [ts(V, k_tok[:, hd, :], psum[:, b, 0:MD], wl[:, hd:hd + 1], ALU.mult, None, None,
                                   r, weights_ready)]
            probs = area(12288, 8, P)
            turned = area(13312, 8, P)
            for t in range(TT):
                tok = slice(t * P, (t + 1) * P)
                for hd in range(MH):
                    for j in range(2):
                        r = mm(psum[:, 3, hd * P:(hd + 1) * P], qk[:, 2 * hd + j, tok], qk[:, 8 + 2 * hd + j, tok],
                               j == 0, j == 1, *bank(3), count=j == 1)
                cols4 = slice(MH * t, MH * t + MH)
                ps = psum[:, 3, :].rearrange("p (h s) -> p h s", h=MH)
                r = stt(V, probs[:, cols4, :], ps, MD ** -0.5, diag[:, cols4, :], ALU.mult, ALU.mult, r, A_.now)
                bank_free[3] = [r]
                for hd in range(MH):
                    r2 = tr(psum[:, 4, hd * P:(hd + 1) * P], probs[:, MH * t + hd, :], r, *bank(4), count=hd == 3)
                bank_free[4] = [copy(A_, turned[:, cols4, :].rearrange("p a b -> p (a b)"), psum[:, 4, :], r2)]
            hm = area(temp, 8, MD + 1)
            c0 = [area(temp + 2060 + 514 * i, 2, MD + 1) for i in range(2)]
            c0_read = [[], []]
            for hd in range(MH):
                vs = slice(hd * MD, (hd + 1) * MD)
                for j in range(2):
                    b = 5 + j
                    kd = k_tok[:, hd, j * P:(j + 1) * P]
                    mm(psum[:, b, 0:MD], kd, v[:, 0, vs], True, True, V.now, A_.now, *bank(b))
                    r = mm(psum[:, b, MD:MD + 1], kd, ones[:, 0:1], True, True, count=True)
                    bank_free[b] = [copy(A_, c0[hd % 2][:, j, :], psum[:, b, 0:MD + 1], r, *c0_read[hd % 2])]
                c0_ready = A_.now
                for t in range(TT):
                    i = MH * t + hd
                    mm(psum[:, t, 0:MD], turned[:, i, :], v[:, t, vs], True, True, *bank(t))
                    r = mm(psum[:, t, MD:MD + 1], turned[:, i, :], ones[:, 0:1], True, True, count=True)
                    bank_free[t] = [copy(A_, hm[:, i, :], psum[:, t, 0:MD + 1], r, *s5_done)]
                for j in range(2):
                    r = mm(psum[:, 2, 0:MD + 1], qk[:, 2 * hd + j, P:SEQ], c0[hd % 2][:, j, :], j == 0, j == 1,
                           c0_ready, *bank(2), count=j == 1)
                c0_read[hd % 2] = [r]
                i = MH + hd
                bank_free[2] = [stt(V, hm[:, i, :], psum[:, 2, 0:MD + 1], fl[11][:, i:i + 1], hm[:, i, :], ALU.mult,
                                    ALU.add, r, A_.now)]
            dn, ms = fl[20], fl[21]
            d_ = hm[:, :, MD]
            ts(V, fl[22], d_, -1.0, ALU.mult, None, None, V.now, A_.now)
            tt(V, dn, d_, fl[22], ALU.max, V.now)
            tt(V, dn, dn, fl[12], ALU.max, V.now)
            V.run(lambda e: e.reciprocal(dn, dn), V.now)
            for i in range(8):
                r = ts(V, hm[:, i, 0:MD], hm[:, i, 0:MD], dn[:, i:i + 1], ALU.mult, None, None, V.now)
                act(sq[:, i % 2, 0:MD], hm[:, i, 0:MD], ACT.Square, r, A_.now, accum=ms[:, i:i + 1])
            ts(V, ms, ms, 1.0 / MD, ALU.mult, EPS, ALU.add, A_.now)
            r = act(ms, ms, ACT.Sqrt, V.now)
            V.run(lambda e: e.reciprocal(ms, ms), r)
            for i in range(8):
                t, hd = i // MH, i % MH
                r = ts(V, hm[:, i, 0:MD], hm[:, i, 0:MD], ms[:, i:i + 1], ALU.mult, None, None, V.now)
                b = 3 + i % 2
                for j in range(2):
                    r2 = tr(psum[:, b, j * P:(j + 1) * P], hm[:, i, j * P:(j + 1) * P], r, *bank(b), count=j == 1)
                for j in range(2):
                    f = 2 * hd + j
                    tok = slice(t * P, (t + 1) * P)
                    stt(V, y[:, f, tok], psum[:, b, j * P:(j + 1) * P], col("mlstm_norm", f), sig_o[:, f, tok],
                        ALU.mult, ALU.mult, r2)
                bank_free[b] = [V.now]
            mixed = V.now

            for i in range(0, KT, 2):
                b, r = gemm_pair([[A["w_out2"][i + j]] for j in range(2)], y, mixed)
                hh = flat(h[:, i:i + 2, :])
                r = tt(V, hh, hh, psum[:, b, :], ALU.add, r)
                bank_free[b] = [r]
                total = sum_squares(hh, i == 0, i == KT - 2, r)
            saved = load([(h_save, flat(h))], V.now)
            root(total, D)
            for i in range(KT):
                normed2 = stt(V, xn[:, i, :], h[:, i, :], col("norm2", i), rstd[:, :], ALU.mult, ALU.mult, V.now,
                              T.now)

            q2 = area(28672, KT, SEQ)
            sc = area(24576, PH, 4 * P)
            keys = sq.rearrange("p a b -> p (a b)")[:, 0:2 * P].rearrange("p (s k) -> p s k", s=2)
            keys_in = load([(keys, A["subkeys"])], normed2, T.now, A_.now)
            for i in range(0, KT, 2):
                b, r = gemm_pair([[A["wq2"][i + j]] for j in range(2)], xn, normed2)
                r = copy(V, flat(q2[:, i:i + 2, :]), psum[:, b, :], r)
                bank_free[b] = [r]
                b = 3 + (i // 2) % 2
                for t in range(TT):
                    for j in range(2):
                        s = (2 * t + j) * P
                        g_ = mm(psum[:, b, s:s + P], q2[:, i + j, t * P:(t + 1) * P], keys[:, j, :], True, True,
                                r, keys_in, *bank(b), count=t == 1 and j == 1)
                bank_free[b] = [copy(A_, sc[:, i // 2, :], psum[:, b, :], g_)]
            scored = A_.now
            queries_read = T.now
            top_v = work[:, 0:512].rearrange("p (h t s k) -> p h t s k", h=PH, t=TT, s=2)
            top_i = work[:, 512:1024].bitcast(U32).rearrange("p (h t s k) -> p h t s k", h=PH, t=TT, s=2)
            top_f = work[:, 1024:1536].rearrange("p (h t s k) -> p h t s k", h=PH, t=TT, s=2)

            def top16(vals, idx, src):
                a, b = slice(0, 8), slice(8, 16)
                V.run(lambda e: e.max(vals[:, a], src), V.now, scored, queries_read)
                V.run(lambda e: e.max_index(idx[:, a], vals[:, a], src), V.now)
                V.run(lambda e: e.match_replace(src, vals[:, a], src, -3.0e38), V.now)
                V.run(lambda e: e.max(vals[:, b], src), V.now)
                return V.run(lambda e: e.max_index(idx[:, b], vals[:, b], src), V.now)

            for hd in range(PH):
                for t in range(TT):
                    for s in range(2):
                        top16(top_v[:, hd, t, s], top_i[:, hd, t, s], sc[:, hd, (2 * t + s) * P:(2 * t + s + 1) * P])
            copy(V, work[:, 1024:1536], work[:, 512:1024].bitcast(U32), V.now)
            def tail(at, n):
                return arena[:, 28672 + at:28672 + at + n]
            cand = tail(0, 256).rearrange("p (a b) -> p a b", a=TOPK)
            best = tail(256, 256).rearrange("p (t h k) -> p t h k", t=TT, h=PH)
            place = tail(512, 256).bitcast(U32)
            place4 = place.rearrange("p (t h k) -> p t h k", t=TT, h=PH)
            part_u = tail(768, 256).bitcast(U32)
            part = [tail(1024 + 256 * s, 256).rearrange("p (t n) -> p t n", t=TT) for s in range(2)]
            peak = tail(1536, 16)
            lists = tail(1600, 768).rearrange("p (w t n) -> p w t n", w=3, t=TT)
            hot = tail(2400, 1024)
            for t in range(TT):
                for hd in range(PH):
                    a_s = top_v[:, hd, t, 0].unsqueeze(2).broadcast_to([P, TOPK, TOPK])
                    b_s = top_v[:, hd, t, 1].unsqueeze(1).broadcast_to([P, TOPK, TOPK])
                    tt(V, cand, a_s, b_s, ALU.add, V.now)
                    top16(best[:, t, hd], place4[:, t, hd], cand.rearrange("p a b -> p (a b)"))
            for s, op, k in ((0, ALU.logical_shift_right, 4), (1, ALU.bitwise_and, 15)):
                V.run(lambda e, op=op, k=k: e.tensor_scalar(part_u, place, k, None, op), V.now)
                copy(V, part[s].rearrange("p t n -> p (t n)"), part_u, V.now)
            iota16 = con("iota")[:, 0:TOPK]
            for s in range(2):
                for t in range(TT):
                    for hh in range(2):
                        n = 4 * TOPK
                        o = hot.rearrange("p (n k) -> p n k", n=n)
                        tt(V, o, part[s][:, t, hh * n:(hh + 1) * n].unsqueeze(2).broadcast_to([P, n, TOPK]),
                           iota16.unsqueeze(1).broadcast_to([P, n, TOPK]), ALU.is_equal, V.now)
                        for q4 in range(4):
                            o4 = o[:, q4 * TOPK:(q4 + 1) * TOPK, :]
                            tt(V, o4, o4, top_f[:, 4 * hh + q4, t, s].unsqueeze(1).broadcast_to([P, TOPK, TOPK]),
                               ALU.mult, V.now)
                        V.run(lambda e, o=o, d=lists[:, s, t, hh * n:(hh + 1) * n]: e.tensor_reduce(
                            d, o, AX.X, ALU.add), V.now)
            bf = tail(256, 256).rearrange("p (a k) -> p a k", k=TOPK)
            tot16 = peak
            copy(V, peak, bf[:, :, 0], V.now)
            tt(V, bf, bf, peak.unsqueeze(2).broadcast_to([P, 16, TOPK]), ALU.subtract, V.now)
            r = act(tail(256, 256), tail(256, 256), ACT.Exp, V.now)
            V.run(lambda e: e.tensor_reduce(tot16, bf, AX.X, ALU.add), r)
            V.run(lambda e: e.reciprocal(tot16, tot16), V.now)
            routed = tt(V, lists[:, 2].rearrange("p t (h k) -> p (t h) k", h=PH), bf,
                        tot16.unsqueeze(2).broadcast_to([P, 16, TOPK]), ALU.mult, V.now)

            hidden = area(0, NKEY, SEQ)
            pairs = sq.rearrange("p a b -> p (a b)")[:, 0:3 * SEQ].rearrange("p (w t) -> p w t", w=3)
            for k2 in range(0, NKEY, 2):
                b, r = gemm_pair([[A["peer_u"][k2 + j]] for j in range(2)], xn, normed2)
                if k2 == 40:
                    for w in range(3):
                        for t in range(TT):
                            s = (2 * w + t) * P
                            g_ = tr(psum[:, 5 + s // 512, s % 512:s % 512 + P], lists[:, w, t, :], routed,
                                    *bank(5), *bank(6), count=w == 2 and t == 1)
                    copy(V, pairs[:, 0:2, :].rearrange("p w t -> p (w t)"), psum[:, 5, :], g_)
                    listed = copy(V, pairs[:, 2, :], psum[:, 6, 0:SEQ])
                    bank_free[5] = bank_free[6] = [listed]
                waits = [saved] + ([listed, T.now] if k2 >= 96 else [normed2])
                bank_free[b] = [act(flat(hidden[:, k2:k2 + 2, :]), psum[:, b, :], ACT.Gelu, r, *waits)]
            experts_done = T.now

            hots = xn.rearrange("p a b -> p (a b)")
            hot_read = [[experts_done]] * 4
            iota = con("iota")
            def multiply(g, b, r):
                hv = hidden[:, :, 4 * g:4 * g + 4]
                bank_free[b] = [tt(V, hv, hv, psum[:, b, :].rearrange("p (t n) -> p n t", t=4), ALU.mult, r,
                                   A_.now)]

            for g in range(SEQ // 4):
                k = g % 4
                one = hots[:, 1024 * k:1024 * k + 512].rearrange("p (t n) -> p t n", t=4)
                two = hots[:, 1024 * k + 512:1024 * k + 1024].rearrange("p (t n) -> p t n", t=4)
                for j in range(4):
                    t = 4 * g + j
                    ts(G, one[:, j, :], iota, pairs[:, 0, t:t + 1], ALU.is_equal, None, None, listed, *hot_read[k])
                for j in range(4):
                    t = 4 * g + j
                    ts(V, two[:, j, :], iota, pairs[:, 1, t:t + 1], ALU.is_equal, pairs[:, 2, t:t + 1], ALU.mult,
                       listed, *hot_read[k])
                ready = [G.now, V.now]
                b = 3 + g % 4
                for j in range(4):
                    r = mm(psum[:, b, j * P:(j + 1) * P], one[:, j, :], two[:, j, :], True, True, *ready, *bank(b),
                           count=j == 3)
                hot_read[k] = [r]
                if g >= 1:
                    multiply(*last)
                last = (g, b, r)
            multiply(*last)
            gated = V.now

            back = load([(flat(xn[:, :, :]), h_save)], T.now, V.now, G.now)
            for i in range(0, KT, 2):
                b, r = gemm_pair([[A["peer_v"][i + j, c] for c in range(8)] for j in range(2)], hidden, gated)
                hh = flat(xn[:, i:i + 2, :])
                r = tt(V, hh, hh, psum[:, b, :], ALU.add, r, back)
                bank_free[b] = [r]
                total = sum_squares(hh, i == 0, i == KT - 2, r, G.now)
            root(total, D)
            for i in range(KT):
                stt(V, xn[:, i, :], xn[:, i, :], col("final", i), rstd[:, :], ALU.mult, ALU.mult, V.now)


        loaded = load([(cols[:, :], A["cols"]), (const[:, :], A["consts"])])
        x_in = load([(flat(h), A["x"])])
        for q in (T, V, A_, G):
            q.wait(loaded, x_in)

        first_block()
        second_block()

        store = load([(out, flat(xn[:, :, :]))],
                     V.now, A_.now, G.now, T.now, queue=S)
        S.wait(store)

        block = ctx.enter_context(nc.Block())
        block.sync(lambda e: S.play(e))
        block.scalar(lambda e: A_.play(e))
        block.vector(lambda e: V.play(e))
        block.gpsimd(lambda e: G.play(e))
        block.tensor(lambda e: T.play(e))


def _units(w):
    k, f = w.shape
    w = w.reshape(k // UNIT * 1, KT, P, f // P, P) if k >= UNIT else w.reshape(1, k // P, P, f // P, P)
    return w.transpose(3, 0, 2, 1, 4).reshape(-1, P, w.shape[1] * P)


def _columns(v):
    v = v.reshape(-1, v.shape[-1] // P, P)
    return v.transpose(2, 0, 1).reshape(P, -1)


def _features(x):
    t, f = x.shape
    return x.reshape(t, f // P, P).transpose(2, 1, 0).reshape(P, -1)


def _bucket(dist):
    n = np.maximum(dist, 1).astype(np.float32)
    large = 16 + (np.log(n / 16) / math.log(8) * 16).astype(np.int32)
    return np.where(dist < 16, dist, np.minimum(large, NBUCKET - 1))


def _one_hot(dist):
    b = np.where(dist < 0, NBUCKET, _bucket(np.maximum(dist, 0)))
    return (b[None] == np.arange(NBUCKET + 1).reshape(-1, *[1] * dist.ndim)).astype(np.float32)


def _constants():
    i = np.arange(P)
    parts = {
        "ident": np.eye(P), "ones": np.ones((P, P)), "tri": i[:, None] <= i[None, :],
        "causal": np.where(i[None, :] <= i[:, None], 0.0, NEG), "iota": np.tile(i, (P, 1)),
        "time": np.tile(np.arange(1, SEQ + 1), (P, 1)),
        "any": np.arange(SEQ).reshape(TT, P).T >= CMP_LEN - 1,
    }
    return np.concatenate([parts[n].astype(np.float32) for n in CONST], axis=1)


def kernel(**inputs):
    import concourse.bacc as bacc
    from concourse.bass_utils import run_bass_kernel_spmd

    x = {k: np.asarray(v) for k, v in inputs.items()}
    x = {k: v[0] if v.shape[0] == 1 and k != "x" else v for k, v in x.items()}
    arrays = {"consts": _constants(), "x": _features(x["x"][0])}

    def per_state(v):
        return v.reshape(ST, P).T

    col_parts = {
        "norm_mix_pre": x["norm_mix_pre"], "norm_mix_post": x["norm_mix_post"], "norm_mlp_pre": x["norm_mlp_pre"],
        "norm_mlp_post": x["norm_mlp_post"], "conv_w": x["conv_w"], "conv_b": x["conv_b"],
        "lru_ba": x["lru_ba"].reshape(-1), "lru_bx": x["lru_bx"].reshape(-1), "lru_lambda": x["lru_lambda"],
        "gnorm_lru": x["gnorm_lru"], "gnorm_nsa": x["gnorm_nsa"], "norm1": x["norm1_g_2"],
        "conv_qk": x["conv_qk_w_2"], "mlstm_norm": x["mlstm_norm_g_2"],
        "s5_re": x["s5_lambda_re_2"].reshape(-1), "s5_im": x["s5_lambda_im_2"].reshape(-1),
        "s5_dt": np.repeat(x["s5_log_dt_2"], NSTATE), "s5_d": x["s5_d_2"].reshape(-1),
        "norm2": x["norm2_g_2"], "final": x["final_g_2"],
    }
    arrays["cols"] = np.concatenate([_columns(col_parts[n]) for n in COLS], axis=1)

    i = np.arange(384)
    t, n = np.arange(P), np.arange(NCMP)
    dist = (np.arange(TT)[:, None, None] * P + t[None, None, :]) - (n[None, :, None] * CMP_STRIDE + CMP_LEN - 1)
    arrays["hot_rel"] = _one_hot(SEQ - 1 - i)
    arrays["hot_cmp"] = _one_hot(dist).reshape(NBUCKET + 1, TT * NCMP, P)
    arrays["rel_bias"] = x["rel_bias"]
    arrays["cmp_pe"] = np.stack([x["cmp_pe_k"], x["cmp_pe_v"]]).transpose(2, 0, 1)
    arrays["cmp_w1"] = np.stack([_units(x["cmp_w1_k"]), _units(x["cmp_w1_v"])])
    arrays["cmp_w2"] = np.stack([x["cmp_w2_k"], x["cmp_w2_v"]]).reshape(2, 2, P, HEAD).transpose(2, 0, 1, 3)
    arrays["lru_w"] = np.stack([x["lru_wa"], x["lru_wx"]]).reshape(2, 8, 2, 64, 64).transpose(2, 3, 0, 1, 4)
    arrays["w_in"] = _units(x["w_in"][:, :4608])
    arrays["w_gates"] = x["w_in"][:, 4608:].reshape(KT, P, 48).transpose(1, 0, 2).reshape(P, -1)
    for name in ("w_out", "mlp_w1", "mlp_w2", "ple_gate"):
        arrays[name] = _units(x[name])
    arrays["ple_proj"] = x["ple_proj"].reshape(2, P, 2, 8, P).transpose(2, 1, 3, 0, 4).reshape(2, P, UNIT)
    arrays["p"] = _features(x["p"][0]).reshape(P, 2, SEQ)

    w = x["w_in_2"]
    arrays["w_in2"] = np.concatenate([_units(w[:, :4096]), _units(w[:, 4104:])])
    arrays["w_gates2"] = w[:, 4096:4104].reshape(KT, P, 8).transpose(1, 0, 2).reshape(P, -1)
    arrays["b_gates2"] = np.broadcast_to(np.tile(x["b_gates_2"], TT), (P, TT * 8))
    arrays["w_out2"] = _units(x["w_out_2"])
    b = np.stack([x["s5_b_re_2"], x["s5_b_im_2"]])
    arrays["s5_b"] = b.reshape(2, 8, 4, 2, NSTATE, GSZ).transpose(2, 3, 5, 1, 0, 4)
    c = np.stack([x["s5_c_re_2"], x["s5_c_im_2"]])
    arrays["s5_c"] = c.reshape(2, ST, 2, GSZ, NSTATE).transpose(2, 4, 0, 1, 3)
    arrays["s5_glu"] = x["s5_glu_w_2"].reshape(8, 8, GSZ, 2, GSZ).transpose(1, 2, 0, 3, 4)
    arrays["wq2"] = _units(x["peer_wq_2"])
    arrays["subkeys"] = x["peer_subkeys_2"].transpose(2, 0, 1)
    arrays["peer_u"] = x["peer_u_2"].reshape(NKEY, NKEY, KT, P).transpose(1, 3, 2, 0).reshape(NKEY, P, UNIT)
    arrays["peer_v"] = x["peer_v_2"].reshape(NKEY, 8, 16, KT, P).transpose(3, 1, 0, 2, 4).reshape(KT, 8, P, UNIT)

    nc = bacc.Bacc("TRN2", target_bir_lowering=False, num_devices=1)
    arrays = {f"in_{k}": np.ascontiguousarray(v) for k, v in arrays.items()}
    aps = {k[3:]: nc.dram_tensor(k, v.shape, mybir.dt.from_np(v.dtype), kind="ExternalInput").ap()
           for k, v in arrays.items()}
    out = nc.dram_tensor("out", (P, KT * SEQ), F32, kind="ExternalOutput").ap()
    build(nc, aps, out)
    r = run_bass_kernel_spmd(nc, [arrays], core_ids=[0])
    got = np.asarray(r.results[0]["out"])
    return np.ascontiguousarray(got.reshape(P, KT, SEQ).transpose(2, 1, 0)).reshape(1, SEQ, D)
```

```python
from contextlib import ExitStack
import math

import numpy as np

import concourse.bass as bass
from concourse import mybir

F32 = mybir.dt.float32
F32R = mybir.dt.float32r
U32 = mybir.dt.uint32
ALU = mybir.AluOpType
ACT = mybir.ActivationFunctionType
AX = mybir.AxisListType

P = 128
SEQ = 256
TT = SEQ // P
D = 2048
KT = D // P
EPS = 1e-6
NEG = -1e30

LRU_W = 1024
HEAD = 64
NH = 16
NKV = 4
REP = NH // NKV
CMP_LEN, CMP_STRIDE = 32, 16
NCMP = (SEQ - CMP_LEN) // CMP_STRIDE + 1
NBUCKET = 32
D_FF = 4 * D
PLE = 256

MW = 1024
MH = 4
MD = MW // MH
GROUPS, GSZ, NSTATE = 64, 16, 64
ST = GROUPS * NSTATE // P
PH = 8
NKEY = 128
TOPK = 16
PAIRS = PH * TOPK

UNIT = KT * P
HALF = UNIT // 2
SLOTS = 4
SPLITS = 3
CHUNK = 32
HOTS = 4
BUDGET = 26605
TWO_PI = 2.0 * math.pi

COLS = {}
for _name, _n in (("norm_mix_pre", 16), ("norm_mix_post", 16), ("norm_mlp_pre", 16), ("norm_mlp_post", 16),
                  ("conv_w", 32), ("conv_b", 8), ("lru_ba", 8), ("lru_bx", 8), ("lru_lambda", 8),
                  ("gnorm_lru", 8), ("gnorm_nsa", 8), ("norm1", 16), ("conv_qk", 64), ("mlstm_norm", 8),
                  ("s5_re", 32), ("s5_im", 32), ("s5_dt", 32), ("s5_d", 8), ("norm2", 16), ("final", 16)):
    COLS[_name] = (sum(n for _, n in COLS.values()), _n)
NCOLS = sum(n for _, n in COLS.values())

CONST = {}
for _name, _n in (("ident", P), ("ones", P), ("tri", P), ("causal", P), ("iota", P), ("time", SEQ), ("any", TT)):
    CONST[_name] = (sum(n for _, n in CONST.values()), _n)
NCONST = sum(n for _, n in CONST.values())


class Queue:

    def __init__(self, sem):
        self.sem, self.count, self.steps, self.seen = sem, 0, [], {}

    @property
    def now(self):
        return (self.sem, self.count)

    def wait(self, *after):
        for sem, value in after:
            if value > self.seen.get(sem.name, 0):
                self.seen[sem.name] = value
                self.steps.append(lambda e, s=sem, v=value: e.wait_ge(s, v))

    def run(self, emit, *after, count=True):
        self.wait(*after)
        if count:
            self.count += 1
            self.steps.append(lambda e: emit(e).then_inc(self.sem, 1))
        else:
            self.steps.append(emit)
        return self.now

    def play(self, engine):
        for step in self.steps:
            step(engine)


def build(nc, A, out):
    with ExitStack() as ctx:
        def sb(name, *shape):
            return ctx.enter_context(nc.sbuf_tensor(name, list(shape), F32))

        def sem(name):
            return ctx.enter_context(nc.semaphore(name))

        h = sb("h", P, KT, SEQ)
        x2 = ctx.enter_context(nc.sbuf_tensor("x2", [P, KT, 2, SEQ], F32R))
        raw = sb("raw", P, SLOTS, HALF)
        w_hi = ctx.enter_context(nc.sbuf_tensor("w_hi", [P, SPLITS, HALF], F32R))
        w_lo = ctx.enter_context(nc.sbuf_tensor("w_lo", [P, SPLITS, HALF], F32R))
        cols = sb("cols", P, NCOLS)
        const = sb("const", P, NCONST)
        sq = sb("sq", P, 2, 512)
        rstd = sb("rstd", P, SEQ)
        work = sb("work", P, 1536)
        psum = ctx.enter_context(nc.psum_tensor("psum", [P, 8, 512], F32))
        scratch = nc.dram_tensor("scratch_bias", [NH, P, 384], F32, kind="Internal").ap()

        def phase(*tensors):
            total = sum(n for _, n, _ in tensors)
            assert total <= BUDGET, total
            with ExitStack() as held:
                return [held.enter_context(nc.sbuf_tensor(name, [P, n], dt)) for name, n, dt in tensors]

        T, V, A_, G = (Queue(sem(n)) for n in ("pe_done", "dve_done", "act_done", "pool_done"))
        S = Queue(sem("sp_done"))
        slot_sem = [sem(f"slot{i}") for i in range(SLOTS)]
        load_sems = []

        def col(name, i=0, n=1):
            at = COLS[name][0] + i
            return cols[:, at:at + n]

        def con(name):
            at, n = CONST[name]
            return const[:, at:at + n]

        ident, ones = con("ident"), con("ones")

        def cut(buf, at, *shape):
            n = int(np.prod(shape))
            v = buf[:, at:at + n]
            if len(shape) == 2:
                v = v.rearrange("p (a b) -> p a b", a=shape[0])
            if len(shape) == 3:
                v = v.rearrange("p (a b c) -> p a b c", a=shape[0], b=shape[1])
            return v

        def tt(q, o, a, b, op, *after):
            return q.run(lambda e: e.tensor_tensor(o, a, b, op), *after)

        def ts(q, o, a, s1, op0, s2, op1, *after):
            if op1 is None:
                return q.run(lambda e: e.tensor_scalar(o, a, s1, None, op0), *after)
            return q.run(lambda e: e.tensor_scalar(o, a, s1, s2, op0, op1), *after)

        def stt(q, o, a, s, b, op0, op1, *after):
            return q.run(lambda e: e.scalar_tensor_tensor(out=o, in0=a, scalar=s, in1=b, op0=op0, op1=op1), *after)

        def act(o, i, func, *after, bias=0.0, scale=1.0, accum=None):
            if accum is None:
                return A_.run(lambda e: e.activation(o, i, func, bias=bias, scale=scale), *after)
            return A_.run(lambda e: e.activation(o, i, func, bias=bias, scale=scale, accum_out=accum), *after)

        def copy(q, o, i, *after):
            if q is A_:
                return act(o, i, ACT.Copy, *after)
            return q.run(lambda e: e.tensor_copy(o, i), *after)

        def fill(q, o, value, *after):
            return q.run(lambda e: e.memset(o, value), *after)

        def mm(o, l, r, start, stop, *after, count=False):
            return T.run(lambda e: e.matmul(o, l, r, start=start, stop=stop), *after, count=count)

        def tr(o, i, *after, count=False):
            n = i.shape[0]
            return T.run(lambda e: e.transpose(o, i, ident[0:n, 0:n]), *after, count=count)

        def load(pairs, *after, queue=None):
            s = sem(f"load{len(load_sems)}")
            load_sems.append(s)
            q = queue or A_
            q.wait(*after)
            for o, i in pairs:
                q.steps.append(lambda e, o=o, i=i: e.dma_start(o, i).then_inc(s, 16))
            return (s, 16 * len(pairs))

        plan = []
        issued = [0]
        used = [0]
        raw_free = [[] for _ in range(SLOTS)]
        split_free = [[] for _ in range(SPLITS)]
        split_made = [None] * SPLITS
        split_turn = [0]
        arrived = {}

        def plan_units(*srcs):
            for src in srcs:
                plan.extend([(src[:, 0:HALF], HALF, True), (src[:, HALF:UNIT], HALF, True)])

        def issue():
            n = issued[0]
            src, size, split = plan[n]
            k = n % SLOTS
            S.wait(*raw_free[k])
            dst, s, landed = raw[:, k, 0:size], slot_sem[k], (slot_sem[k], 16 * (n // SLOTS + 1))
            S.steps.append(lambda e: e.dma_start(dst, src).then_inc(s, 16))
            issued[0] += 1
            if not split:
                arrived[n] = (dst, None, [landed])
                return
            m = split_turn[0] % SPLITS
            split_turn[0] += 1
            hi, lo = w_hi[:, m, 0:size], w_lo[:, m, 0:size]
            r = act(hi, dst, ACT.Copy, landed, *split_free[m])
            r2 = tt(V, lo, dst, hi.bitcast(F32), ALU.subtract, r, landed, *split_free[m])
            split_made[m] = r2
            raw_free[k] = [r, r2]
            arrived[n] = ((hi, lo), m, [r, r2])

        background = []

        def pump(steps):
            for _ in range(steps):
                if background and next(background[0], self_done) is self_done:
                    background.pop(0)

        self_done = object()
        pace = [0]

        def next_unit(src=None, held=0):
            n = used[0]
            if src is not None:
                assert plan[n][0].offset == src.offset and plan[n][0].tensor.name == src.tensor.name, n
            used[0] += 1
            while issued[0] < min(n + SPLITS - held, len(plan)):
                issue()
            pump(pace[0])
            return n, *arrived.pop(n)

        def leave(n, m, r):
            if m is None:
                raw_free[n % SLOTS] = [r]
            else:
                split_free[m] = [r, split_made[m]]

        bank_free = [[] for _ in range(8)]

        def bank(b):
            return bank_free[b]

        gemm_turn = [0]

        def gemm_bank():
            gemm_turn[0] += 1
            return (gemm_turn[0] - 1) % 3

        def gemm_pair(units, x, *ready):
            b = gemm_bank()
            for j, srcs in enumerate(units):
                o = psum[:, b, j * SEQ:(j + 1) * SEQ]
                for c in range(2 * len(srcs)):
                    n, (hi, lo), m, landed = next_unit(srcs[c // 2][:, (c % 2) * HALF:(c % 2 + 1) * HALF])
                    hi, lo = (w.rearrange("p (k f) -> p k f", k=8) for w in (hi, lo))
                    waits = [*landed, *bank(b), *ready]
                    for i in range(8):
                        k = 8 * c + i
                        first, last = k == 0, k == 16 * len(srcs) - 1
                        mm(o, hi[:, i, :], x[:, k, 0, :], first, False, *(waits if i == 0 else ()))
                        mm(o, hi[:, i, :], x[:, k, 1, :], False, False)
                        r = mm(o, lo[:, i, :], x[:, k, 0, :], False, last, count=i == 7)
                    leave(n, m, r)
            return b, r

        def gemm_tokens(srcs, x, *ready):
            b = gemm_bank()
            for j, src in enumerate(srcs):
                parts = []
                for c in range(2):
                    parts.append(next_unit(src[:, c * HALF:(c + 1) * HALF], held=c))
                waits = [w for p in parts for w in p[3]] + [*bank(b), *ready]
                for t in range(TT):
                    o = psum[:, b, t * SEQ + j * P:t * SEQ + (j + 1) * P]
                    ts_ = slice(t * P, (t + 1) * P)
                    for k in range(KT):
                        hi, lo = (w.rearrange("p (k f) -> p k f", k=8)[:, k % 8, :] for w in parts[k // 8][1])
                        mm(o, x[:, k, 0, ts_], hi, k == 0, False, *(waits if k == 0 else ()))
                        mm(o, x[:, k, 0, ts_], lo, False, False)
                        r = mm(o, x[:, k, 1, ts_], hi, False, k == KT - 1, count=k == KT - 1 and t == TT - 1)
                for p in parts:
                    leave(p[0], p[2], r)
            return b, r

        def gemm_small(width, x, b, *ready):
            n, (hi, lo), m, landed = next_unit()
            hi, lo = (w.rearrange("p (k f) -> p k f", k=KT) for w in (hi, lo))
            for t in range(TT):
                o = psum[:, b, t * width:(t + 1) * width]
                ts_ = slice(t * P, (t + 1) * P)
                for k in range(KT):
                    mm(o, x[:, k, 0, ts_], hi[:, k, :], k == 0, False, *landed, *bank(b), *ready)
                    mm(o, x[:, k, 0, ts_], lo[:, k, :], False, False)
                    r = mm(o, x[:, k, 1, ts_], hi[:, k, :], False, k == KT - 1, count=k == KT - 1 and t == TT - 1)
            leave(n, m, r)
            return r

        def split(src, dst, i, *ready):
            hi, lo = dst[:, i:i + 2, 0, :], dst[:, i:i + 2, 1, :]
            s = src.rearrange("p (a t) -> p a t", a=2)
            r = act(hi, s, ACT.Copy, *ready)
            return tt(V, lo, s, hi.bitcast(F32), ALU.subtract, r, *ready)

        sq_free = [None, None]
        sq_turn = [0]

        def sum_squares(src, first, last, *ready, b=7):
            k = sq_turn[0] % 2
            sq_turn[0] += 1
            waits = list(ready) + ([sq_free[k]] if sq_free[k] else [])
            s = act(sq[:, k, :], src, ACT.Square, *waits)
            for j in range(2):
                r = mm(psum[:, b, 0:SEQ], ones, sq[:, k, j * SEQ:(j + 1) * SEQ], first and j == 0, last and j == 1,
                       s, *bank(b), count=j == 1)
            sq_free[k] = r
            return r

        def root(total, width, dst=None, b=7):
            dst = rstd[:, :] if dst is None else dst
            r = ts(V, dst, psum[:, b, 0:SEQ], 1.0 / width, ALU.mult, EPS, ALU.add, total, V.now, A_.now)
            bank_free[b] = [r]
            r = act(dst, dst, ACT.Sqrt, r)
            return V.run(lambda e: e.reciprocal(dst, dst), r)

        def flat(v):
            return v.rearrange("p a b -> p (a b)")

        def scaled_split(src, dst, gain, n, at=0):
            for i in range(0, n, 2):
                k = sq_turn[0] % 2
                sq_turn[0] += 1
                free = sq_free[k] or V.now
                for j in range(2):
                    r = stt(V, sq[:, k, j * SEQ:(j + 1) * SEQ], src[:, i + j, :], col(gain, i + j), rstd[:, :],
                            ALU.mult, ALU.mult, V.now, free)
                sq_free[k] = r = split(sq[:, k, :], dst, at + i, r, T.now)
            return r

        def norm(src, dst, gain, n, *ready, at=0):
            for i in range(0, n, 2):
                r = sum_squares(flat(src[:, i:i + 2, :]), i == 0, i == n - 2, *ready)
            root(r, n * P)
            return scaled_split(src, dst, gain, n, at)

        def project(name, x, dst, ready, *before, per=1):
            for i in range(0, KT, 2):
                b, r = gemm_pair([[A[name][(i + j) * per + c] for c in range(per)] for j in range(2)], x, ready)
                r = copy(V, flat(dst[:, i:i + 2, :]), psum[:, b, :], r, *before)
                bank_free[b] = [r]
                total = sum_squares(flat(dst[:, i:i + 2, :]), i == 0, i == KT - 2, r)
            return root(total, D)

        def add_normed(delta, gain, ready):
            for i in range(KT):
                r = stt(V, delta[:, i, :], delta[:, i, :], col(gain, i), rstd[:, :], ALU.mult, ALU.mult, ready)
            for i in range(0, KT, 4):
                r = tt(V, flat(h[:, i:i + 4, :]), flat(h[:, i:i + 4, :]), flat(delta[:, i:i + 4, :]), ALU.add, V.now)
            return r

        def log1p(dst, e, z, z2, *ready):
            ts(V, z, e, 2.0, ALU.add, None, None, *ready)
            V.run(lambda q: q.reciprocal(z, z), V.now)
            tt(V, z, z, e, ALU.mult, V.now)
            tt(V, z2, z, z, ALU.mult, V.now)
            ts(V, dst, z2, 1.0 / 17, ALU.mult, None, None, V.now)
            for k in range(7, 0, -1):
                stt(V, dst, dst, 1.0 / (2 * k + 1), z2, ALU.add, ALU.mult, V.now)
            stt(V, dst, dst, 1.0, z, ALU.add, ALU.mult, V.now)
            return ts(V, dst, dst, 2.0, ALU.mult, None, None, V.now)

        def softplus_neg(dst, x, neg, e, z, z2, *ready):
            ts(V, neg, x, -1.0, ALU.mult, None, None, *ready)
            r = tt(V, e, neg, x, ALU.min, V.now)
            r = act(e, e, ACT.Exp, r)
            log1p(dst, e, z, z2, r)
            return stt(V, dst, neg, 0.0, dst, ALU.max, ALU.add, V.now)

        def first_block():
            buf, = phase(("mixers_1", 25512, F32))
            y = cut(buf, 0, KT, SEQ)
            q = cut(buf, 4096, 8, SEQ)
            k_sel, k_win = cut(buf, 6144, NKV, SEQ), cut(buf, 7168, NKV, SEQ)
            k_cmp, v_cmp = (cut(buf, 8192 + 1024 * i, NKV, SEQ)[0:HEAD] for i in range(2))
            bias = cut(buf, 10240, NH, SEQ)
            bias_cmp = cut(buf, 14336, TT, NCMP, NH)
            v_sel, v_win = cut(buf, 14816, TT, NKV * HEAD), cut(buf, 15328, TT, NKV * HEAD)
            gates = cut(buf, 15840, TT, 3 * NH)
            attn = 15936
            u_pad = cut(buf, attn, 8, SEQ + 3)
            gate_in = cut(buf, attn + 2080, 8, SEQ)
            temp = attn + 4128
            lru_w = cut(buf, 4096, 2, 8, P)
            hot_cmp = cut(buf, temp, TT * NCMP, P)[0:NBUCKET + 1]
            hot_rel = cut(buf, temp + 3840, 384)[0:NBUCKET + 1]
            tab = work[0:NBUCKET + 1, 0:NH]
            rel = buf[0:NH, temp + 4224:temp + 4608]
            spl = work[:, 16:24], work[:, 24:32], work[:, 32:40], work[:, 40:48], work[:, 48:56]
            pe = work[0:HEAD, 64:128].rearrange("p (w l) -> p w l", w=2)
            w2 = work[:, 128:384].rearrange("p (w f d) -> p w f d", w=2, f=2)

            plan_units(*[A["w_in"][i] for i in (*range(0, 16), 24, 25, 26, 27, 28, 29, 32, 33, *range(16, 24),
                                                30, 31, 34, 35)])
            plan.append((A["w_gates"], KT * 3 * NH, True))
            for w in range(2):
                for f in range(2):
                    src = A["cmp_w1"][w, f]
                    plan.extend([(src[:, 0:HALF], HALF, False), (src[:, HALF:UNIT], HALF, False)])
            plan_units(*[A["w_out"][i] for i in range(KT)])
            for c in range(D_FF // P // CHUNK):
                plan_units(*[A["mlp_w1"][CHUNK * c + i] for i in range(CHUNK)])
                plan_units(*[A["mlp_w2"][4 * f + 2 * c + k] for f in range(KT) for k in range(2)])
            for c in range(2):
                plan.extend([(A["ple_proj"][c][:, 0:HALF], HALF, False), (A["ple_proj"][c][:, HALF:UNIT], HALF, False)])
            plan_units(*[A["ple_gate"][i] for i in range(KT)])

            small = load([(tab[0:NBUCKET], A["rel_bias"]), (hot_cmp, A["hot_cmp"]), (hot_rel, A["hot_rel"]),
                          (pe, A["cmp_pe"]), (w2, A["cmp_w2"])])
            r = fill(V, tab[NBUCKET:NBUCKET + 1], NEG)
            cleared = fill(G, lru_w, 0.0)
            fill(G, u_pad[:, :, 0:3], 0.0)
            lru_loaded = load([(lru_w[g * 64:g * 64 + 64, :, :, g * 64:g * 64 + 64], A["lru_w"][g]) for g in range(2)],
                              cleared)

            r = mm(psum[0:NH, 3, 0:384], tab, hot_rel, True, True, small, r, count=True)
            r = copy(V, rel, psum[0:NH, 3, 0:384], r)
            bank_free[3] = [r]
            stored = load([(scratch, rel.unsqueeze(1).broadcast_to([NH, P, 384]))], r)
            toeplitz = bass.AP(tensor=scratch.tensor, offset=P - 1, ap=[[383, P], [P * 384, NH], [1, SEQ]])
            bias_ready = load([(bias, toeplitz)], stored)
            for i in range(TT * NCMP):
                r = mm(psum[:, 4, i * NH:(i + 1) * NH], hot_cmp[:, i, :], tab, True, True,
                       count=i == TT * NCMP - 1)
            r = copy(V, bias_cmp.rearrange("p a b c -> p (a b c)"), psum[:, 4, 0:TT * NCMP * NH], r)
            bank_free[4] = [r]

            softplus_neg(spl[0], col("lru_lambda", 0, 8), *spl[1:])
            ts(V, spl[0], spl[0], 8.0, ALU.mult, None, None, V.now)
            decay_ready = ts(V, spl[1], spl[0], -1.0, ALU.mult, None, None, V.now)

            normed = norm(h, x2, "norm_mix_pre", KT)

            def features(first):
                return gemm_pair([[A["w_in"][first + j]] for j in range(2)], x2, normed)

            for i in range(0, 8, 2):
                b, r = features(i)
                bank_free[b] = [copy(V, u_pad[:, i:i + 2, 3:], psum[:, b, :].rearrange("p (a t) -> p a t", a=2),
                                     r, G.now)]
            for i in range(0, 8, 2):
                b, r = features(8 + i)
                bank_free[b] = [copy(A_, flat(gate_in[:, i:i + 2, :]), psum[:, b, :], r)]

            def lru_half(first):
                xc, rg, ig, th, dec = (cut(buf, temp + 1024 * i, 4, SEQ) for i in range(5))
                for i in range(4):
                    f = first + i
                    ts(V, xc[:, i, :], u_pad[:, f, 0:SEQ], col("conv_w", f), ALU.mult, col("conv_b", f), ALU.add,
                       V.now, bias_ready)
                    for k in range(1, 4):
                        conv = stt(V, xc[:, i, :], u_pad[:, f, k:k + SEQ], col("conv_w", 8 * k + f), xc[:, i, :],
                                   ALU.mult, ALU.add, V.now)
                    b = 3 + i % 2
                    mm(psum[:, b, 0:SEQ], lru_w[:, 0, f, :], xc[:, i, :], True, True, conv, lru_loaded, *bank(b))
                    r = mm(psum[:, b, SEQ:], lru_w[:, 1, f, :], xc[:, i, :], True, True, count=True)
                    act(rg[:, i, :], psum[:, b, 0:SEQ], ACT.Sigmoid, r, V.now, bias=col("lru_ba", f))
                    bank_free[b] = [act(ig[:, i, :], psum[:, b, SEQ:], ACT.Sigmoid, bias=col("lru_bx", f))]
                for i in range(4):
                    act(th[:, i, :], rg[:, i, :], ACT.Tanh, A_.now, decay_ready,
                        scale=spl[0][:, first + i:first + i + 1])
                tanhs = A_.now
                for i in range(4):
                    act(dec[:, i, :], rg[:, i, :], ACT.Exp, scale=spl[1][:, first + i:first + i + 1])
                decays = A_.now
                th, rg, ig, xc = flat(th), flat(rg), flat(ig), flat(xc)
                ts(V, rg, th, 1.0, ALU.add, None, None, decays, tanhs)
                V.run(lambda e: e.reciprocal(rg, rg), V.now)
                r = tt(V, th, th, rg, ALU.mult, V.now)
                root_b = act(th, th, ACT.Sqrt, r, scale=2.0)
                tt(G, ig, ig, xc, ALU.mult, A_.now)
                r = tt(G, ig, ig, th, ALU.mult, root_b, G.now)
                gt = flat(gate_in[:, first:first + 4, :])
                gelu = act(gt, gt, ACT.Gelu_apprx_tanh)
                for i in range(4):
                    s = slice(i * SEQ, (i + 1) * SEQ)
                    o, a, bb = rg[:, s], flat(dec)[:, s], ig[:, s]
                    V.run(lambda e, o=o, a=a, bb=bb: e.tensor_tensor_scan(o, a, bb, 0.0, ALU.mult, ALU.add),
                          r, V.now, decays)
                return tt(V, flat(y[:, first:first + 4, :]), rg, gt, ALU.mult, V.now, gelu)

            def to_groups(dst, b, r):
                src = psum[:, b, :].rearrange("p (a t) -> p a t", a=2)
                d = dst.rearrange("p (a two) t -> p a two t", two=2)
                for low in range(2 if dst.shape[0] == P else 1):
                    for g in range(2):
                        r = act(d[HEAD * low:HEAD * low + HEAD, :, g, :], src[HEAD * g:HEAD * g + HEAD], ACT.Copy, r)
                bank_free[b] = [r]

            def to_tokens(dst, first):
                b, r = gemm_tokens([A["w_in"][first], A["w_in"][first + 1]], x2, normed)
                bank_free[b] = [copy(A_, flat(dst), psum[:, b, :], r)]

            b, r = features(24)
            to_groups(k_cmp, b, r)
            lru_half(0)
            b, r = features(26)
            to_groups(v_cmp, b, r)
            b, r = features(28)
            to_groups(k_sel, b, r)
            b, r = features(32)
            to_groups(k_win, b, r)
            lru_half(4)
            lru_done = T.now
            for i in range(0, 8, 2):
                b, r = features(16 + i)
                bank_free[b] = [act(flat(q[:, i:i + 2, :]), psum[:, b, :], ACT.Copy, r, lru_done, scale=HEAD ** -0.5)]
            to_tokens(v_sel, 30)
            to_tokens(v_win, 34)
            r = gemm_small(3 * NH, x2, 5, normed)
            bank_free[5] = [act(flat(gates), psum[:, 5, 0:96], ACT.Sigmoid, r)]
            projected = T.now

            lru_all = V.now
            kc = work[:, 384:444]
            vc = work[0:NCMP, 448:704].rearrange("p (g d) -> p g d", g=NKV)
            for w, src in enumerate((k_cmp, v_cmp)):
                blk = cut(buf, temp + 1024 * w, KT, NKV * NCMP)
                hid = cut(buf, temp + 2048 + 128 * w, 2, NKV * NCMP)
                for m in range(2):
                    for par in range(2):
                        for g in range(NKV):
                            v = src[:, g, :].rearrange("p (a kk two) -> p kk two a", kk=8, two=2)[:, :, par, m:m + NCMP]
                            o = blk[64 * par:64 * par + 64, 8 * m:8 * m + 8, g * NCMP:(g + 1) * NCMP]
                            e = pe[:, w, :].rearrange("p (m kk two) -> p m kk two", m=2, two=2)[:, m, :, par]
                            tt(V, o, v, e.unsqueeze(2).broadcast_to([HEAD, 8, NCMP]), ALU.add,
                               A_.now, lru_all, lru_done, small)
                blk_ready = V.now
                for f in range(2):
                    for c in range(2):
                        n, part, m, landed = next_unit()
                        wk = part.rearrange("p (k f) -> p k f", k=8)
                        for i in range(8):
                            k = 8 * c + i
                            r = mm(psum[:, 6, f * 60:(f + 1) * 60], wk[:, i, :], blk[:, k, :], k == 0, k == KT - 1,
                                   *landed, blk_ready, *bank(6), count=i == 7)
                        leave(n, m, r)
                r = act(flat(hid), psum[:, 6, 0:120], ACT.Gelu_apprx_tanh, r)
                bank_free[6] = [r]
                if w == 0:
                    for f in range(2):
                        r = mm(psum[0:HEAD, 6, 128:188], w2[:, 0, f, :], hid[:, f, :], f == 0, f == 1, r, small,
                               count=f == 1)
                    for low in range(2):
                        r = copy(V, kc[HEAD * low:HEAD * low + HEAD], psum[0:HEAD, 6, 128:188], r)
                else:
                    for g in range(NKV):
                        for f in range(2):
                            r2 = mm(psum[0:NCMP, 6, 128 + 64 * g:192 + 64 * g], hid[:, f, g * NCMP:(g + 1) * NCMP],
                                    w2[:, 1, f, :], f == 0, f == 1, r, count=g == NKV - 1 and f == 1)
                    r = copy(V, vc.rearrange("p g d -> p (g d)"), psum[0:NCMP, 6, 128:384], r2)
                bank_free[6] = [r]
            compressed = V.now

            norm(y[:, 0:8, :], x2, "gnorm_lru", 8, compressed, projected)

            pv_done = [None, None]

            def buffers(g):
                def base(a, n):
                    return buf[:, attn + 3072 * (g % 2) + a:attn + 3072 * (g % 2) + a + n]

                p0 = [base(1536 * w, 512).rearrange("p (h s) -> p h s", h=REP) for w in range(2)]
                p1 = [base(1536 * w + 512, 1024).rearrange("p (h s) -> p h s", h=REP) for w in range(2)]
                pc = work[:, 704 + 120 * (g % 2):824 + 120 * (g % 2)].rearrange("p (t h n) -> p t h n", t=TT, h=REP)
                st = work[:, 944 + 64 * (g % 2):1008 + 64 * (g % 2)]
                return p0, p1, pc, st

            def half_of(v, i):
                return v[HEAD * (i % 2):HEAD * (i % 2) + HEAD]

            def head(v, g, i):
                return half_of(v, i)[:, (REP * g + i) // 2, :]

            def softmaxes(g):
                p0, p1, pc, st = buffers(g)
                before = [pv_done[g % 2]] if pv_done[g % 2] else [compressed, projected]
                hs = slice(REP * g, REP * g + REP)
                gate = gates.rearrange("p t (h b) -> p t h b", b=3)
                ps = psum[:, 0, 0:120].rearrange("p (t h n) -> p t h n", t=TT, h=REP)
                for odd in range(2):
                    turn_waits = [A_.now, compressed, *bank(0)] if odd == 0 else [T.now]
                    for t in range(TT):
                        for i in (odd, odd + 2):
                            r = mm(ps[:, t, i, :], head(q, g, i)[:, t * P:(t + 1) * P],
                                   half_of(kc, i)[:, g * NCMP:(g + 1) * NCMP], True, True, *turn_waits,
                                   count=t == TT - 1 and i == odd + 2)
                for t in range(TT):
                    r = tt(V, pc[:, t], ps[:, t], bias_cmp[:, t, :, hs].rearrange("p n h -> p h n"), ALU.add,
                           r, *before)
                bank_free[0] = [r]
                top = st[:, 0:8].rearrange("p (t h) -> p t h", t=TT)
                tot = st[:, 8:16].rearrange("p (t h) -> p t h", t=TT)
                wide = [P, REP, NCMP]
                V.run(lambda e: e.tensor_reduce(top, pc, AX.X, ALU.max), V.now)
                for t in range(TT):
                    tt(V, pc[:, t], pc[:, t], top[:, t].unsqueeze(2).broadcast_to(wide), ALU.subtract, V.now)
                pcf = pc.rearrange("p t h n -> p (t h n)")
                r = act(pcf, pcf, ACT.Exp, V.now)
                V.run(lambda e: e.tensor_reduce(tot, pc, AX.X, ALU.add), r)
                V.run(lambda e: e.reciprocal(tot, tot), V.now)
                for t in range(TT):
                    ts(V, tot[:, t], tot[:, t], con("any")[:, t:t + 1], ALU.mult, None, None, V.now)
                tt(V, tot, tot, gate[:, :, hs, 0], ALU.mult, V.now)
                for t in range(TT):
                    tt(V, pc[:, t], pc[:, t], tot[:, t].unsqueeze(2).broadcast_to(wide), ALU.mult, V.now)
                for w, keys in enumerate((k_sel, k_win)):
                    mx = st[:, 16 + 16 * w:24 + 16 * w]
                    sm = st[:, 24 + 16 * w:32 + 16 * w]
                    s0 = psum[:, 2:4, 0:SEQ].rearrange("p b (a s) -> p a b s", a=2)
                    s1 = psum[:, 4:6, :].rearrange("p b (a s) -> p a b s", a=2)
                    for i in range(REP):
                        r0 = mm(s0[:, i // 2, i % 2, :], head(q, g, i)[:, 0:P], half_of(keys, i)[:, g, 0:P], True, True,
                                *bank(2), *bank(3), count=i == REP - 1)
                    for i in range(REP):
                        r1 = mm(s1[:, i // 2, i % 2, :], head(q, g, i)[:, P:SEQ], half_of(keys, i)[:, g, :], True, True,
                                *bank(4), *bank(5), count=i == REP - 1)

                    def by_bank(v):
                        return v.rearrange("p (a b) s -> p a b s", b=2)

                    bank_free[2] = bank_free[3] = [tt(V, by_bank(p0[w]), s0, by_bank(bias[:, hs, P:SEQ]), ALU.add, r0,
                                                      bias_ready, *before)]
                    bank_free[4] = bank_free[5] = [tt(V, by_bank(p1[w]), s1, by_bank(bias[:, hs, :]), ALU.add, r1)]
                    V.run(lambda e, m=mx, p=p0[w]: e.tensor_reduce(m[:, 0:4], p, AX.X, ALU.max), V.now)
                    V.run(lambda e, m=mx, p=p1[w]: e.tensor_reduce(m[:, 4:8], p, AX.X, ALU.max), V.now)
                    r = ts(V, mx, mx, -1.0, ALU.mult, None, None, V.now)
                    for t, p in enumerate((p0[w], p1[w])):
                        for i in range(REP):
                            j = REP * t + i
                            act(p[:, i, :], p[:, i, :], ACT.Exp, r, bias=mx[:, j:j + 1], accum=sm[:, j:j + 1])
                    r = V.run(lambda e, m=sm: e.reciprocal(m, m), A_.now)
                    r = tt(V, sm.rearrange("p (t h) -> p t h", t=TT), sm.rearrange("p (t h) -> p t h", t=TT),
                           gate[:, :, hs, 1 + w], ALU.mult, V.now)
                    tt(V, p0[w], p0[w], sm[:, 0:4].unsqueeze(2).broadcast_to([P, REP, P]), ALU.mult, V.now)
                    tt(G, p1[w], p1[w], sm[:, 4:8].unsqueeze(2).broadcast_to([P, REP, SEQ]), ALU.mult, r)
                return [V.now, G.now]

            turned_free = [[], []]
            turn = [0]

            def outputs(g, ready):
                p0, p1, pc, st = buffers(g)
                for i in range(REP):
                    k = turn[0] % 2
                    turn[0] += 1
                    hd = REP * g + i
                    turned = cut(buf, attn + 6144 + 1024 * k, 1024)
                    for w in range(2):
                        b = 6 if w == 0 else 1
                        tr(psum[:, b, 0:P], p0[w][:, i, :], *ready, *bank(b))
                        tr(psum[:, b, P:2 * P], p1[w][:, i, 0:P])
                        tr(psum[:, b, 2 * P:3 * P], p1[w][:, i, P:SEQ])
                        r = tr(psum[0:NCMP, b, 3 * P:4 * P], pc[:, w, i, :], count=True)
                        q_ = A_ if w == 0 else V
                        copy(q_, turned[:, 384 * w:384 * w + 384], psum[:, b, 0:384], r, *turned_free[k])
                        c = copy(q_, turned[0:NCMP, 768 + P * w:768 + P * w + P], psum[0:NCMP, b, 384:512])
                        bank_free[b] = [c]
                    o = psum[0:HEAD, 7, 0:SEQ]
                    late = psum[0:HEAD, 7, P:SEQ]
                    for w, v in enumerate((v_sel, v_win)):
                        d = slice(g * HEAD, (g + 1) * HEAD)
                        mm(o, v[:, 0, d], turned[:, 384 * w:384 * w + 256], w == 0, False, V.now, A_.now, *bank(7))
                        mm(late, v[:, 1, d], turned[:, 384 * w + 256:384 * w + 384], False, False)
                    r = mm(o, vc[:, g, :], turned[0:NCMP, 768:1024], False, True, count=True)
                    turned_free[k] = [r]
                    at = HEAD * (hd % 2)
                    bank_free[7] = [copy(A_, y[at:at + HEAD, 8 + hd // 2, :], o, r)]
                pv_done[g % 2] = T.now

            ready = softmaxes(0)
            for g in range(NKV):
                following = softmaxes(g + 1) if g + 1 < NKV else None
                outputs(g, ready)
                ready = following
            r = norm(y[:, 8:16, :], x2, "gnorm_nsa", 8, A_.now, at=8)

            o = cut(buf, attn, KT, SEQ)
            r = project("w_out", x2, o, r, T.now, V.now, G.now)
            r = add_normed(o, "norm_mix_post", r)

            before = [V.now, A_.now, G.now, T.now]
            o_buf, hid_buf = phase(("mlp_out", KT * SEQ, F32), ("mlp_hidden", CHUNK * 2 * SEQ, F32R))
            o = cut(o_buf, 0, KT, SEQ)
            hidden = cut(hid_buf, 0, CHUNK, 2, SEQ)
            r = norm(h, x2, "norm_mlp_pre", KT, r)
            chunks = D_FF // P // CHUNK
            for c in range(chunks):
                for i in range(0, CHUNK, 2):
                    b, g_ = gemm_pair([[A["mlp_w1"][CHUNK * c + i + j]] for j in range(2)], x2, r)
                    k = sq_turn[0] % 2
                    sq_turn[0] += 1
                    s = act(sq[:, k, :], psum[:, b, :], ACT.Relu, g_, sq_free[k])
                    bank_free[b] = [s]
                    s = tt(V, sq[:, k, :], sq[:, k, :], sq[:, k, :], ALU.mult, s)
                    sq_free[k] = split(sq[:, k, :], hidden, i, s, *before)
                ready = V.now
                for i in range(0, KT, 2):
                    b, g_ = gemm_pair([[A["mlp_w2"][4 * (i + j) + 2 * c + k] for k in range(2)] for j in range(2)],
                                      hidden, ready)
                    oo = flat(o[:, i:i + 2, :])
                    if c == 0:
                        s = copy(V, oo, psum[:, b, :], g_, *before)
                    else:
                        s = tt(V, oo, oo, psum[:, b, :], ALU.add, g_)
                    bank_free[b] = [s]
                    if c == chunks - 1:
                        total = sum_squares(oo, i == 0, i == KT - 2, s)
                before = [T.now]
            r = root(total, D)
            r = add_normed(o, "norm_mlp_post", r)

            before = [V.now, A_.now, G.now, T.now]
            buf, = phase(("embedding", 3 * KT * SEQ, F32))
            emb, sig = cut(buf, 0, KT, SEQ), cut(buf, KT * SEQ, KT, SEQ)
            pt = work[:, 0:512].rearrange("p (k t) -> p k t", k=2)
            p_in = load([(pt, A["p"])], *before)
            for i in range(0, KT, 2):
                r = split(flat(h[:, i:i + 2, :]), x2, i, r, T.now)
            for c in range(4):
                n, part, m, landed = next_unit()
                w = part.rearrange("p (f k j) -> p f k j", f=4, k=2)
                for f in range(0, 4, 2):
                    b = gemm_bank()
                    for j in range(2):
                        for i in range(2):
                            g_ = mm(psum[:, b, j * SEQ:(j + 1) * SEQ], w[:, f + j, i, :], pt[:, i, :], i == 0, i == 1,
                                    *landed, p_in, *bank(b), count=i == 1 and j == 1)
                    bank_free[b] = [copy(A_, flat(emb[:, 4 * c + f:4 * c + f + 2, :]), psum[:, b, :], g_, *before)]
                leave(n, m, g_)
            for i in range(0, KT, 2):
                b, g_ = gemm_pair([[A["ple_gate"][i + j]] for j in range(2)], x2, r)
                s = act(flat(sig[:, i:i + 2, :]), psum[:, b, :], ACT.Sigmoid, g_, *before)
                bank_free[b] = [s]
                e2, hh = flat(emb[:, i:i + 2, :]), flat(h[:, i:i + 2, :])
                s = tt(V, e2, e2, flat(sig[:, i:i + 2, :]), ALU.mult, s)
                tt(V, hh, hh, e2, ALU.add, s)

        def second_block():
            in_before = [V.now, A_.now, G.now, T.now]
            buf, = phase(("mixers_2", 26572, F32))
            y = cut(buf, 0, KT, SEQ)
            u = cut(buf, 4096, 8, SEQ)
            qk_pad = cut(buf, 6144, 4, SEQ + 3)
            qk = cut(buf, 7180, KT, SEQ)
            v = cut(buf, 11276, TT, MW)
            sig_o = cut(buf, 13324, 8, SEQ)
            b_w = cut(buf, 15372, 8, 2, P)
            c_w = cut(buf, 17420, 2, ST, 32)
            glu_w = cut(buf, 19468, 8, 2, P)
            chunk = 15372
            temp = 21516

            plan_units(*[A["w_in2"][32 + i] for i in range(8)],
                       *[A["w_in2"][i + 16 * o + j] for i in range(0, 16, 2) for o in range(2) for j in range(2)])
            plan.append((A["w_gates2"], KT * 8, True))
            plan_units(*[A["w_out2"][i] for i in range(KT)], *[A["wq2"][i] for i in range(KT)])
            for c in range(NKEY // CHUNK):
                plan_units(*[A["peer_u"][CHUNK * c + i] for i in range(CHUNK)])
                plan_units(*[A["peer_v"][f, 2 * c + k] for f in range(KT) for k in range(2)])

            small = [work[:, 32 * i:32 * i + 32] for i in range(30)]
            gl = work[:, 960:976].rearrange("p (t g) -> p t g", t=TT)
            bg = work[:, 976:992]
            fill(G, b_w.rearrange("p a b c -> p (a b c)"), 0.0, *in_before)
            fill(G, c_w.rearrange("p a b c -> p (a b c)"), 0.0)
            fill(G, glu_w.rearrange("p a b c -> p (a b c)"), 0.0)
            cleared = fill(G, qk_pad[:, :, 0:3], 0.0)
            pieces = [(bg, A["b_gates2"])]
            for r in range(4):
                for g in range(2):
                    a = 32 * r + 16 * g
                    pieces += [(b_w[a:a + 16, :, c, 64 * g:64 * g + 64], A["s5_b"][r, g, :, :, c, :]) for c in range(2)]
            for g in range(2):
                pieces += [(c_w[64 * g:64 * g + 64, c, :, 16 * g:16 * g + 16], A["s5_c"][g, :, c]) for c in range(2)]
            for g in range(8):
                a = 16 * g
                pieces += [(glu_w[a:a + 16, :, c, a:a + 16], A["s5_glu"][g, :, :, c, :]) for c in range(2)]
            params = load(pieces, cleared)

            normed = norm(h, x2, "norm1", KT, *in_before)

            (dt, x, th, n, ang, tn, em1, mag, hs, sn1, cm1, cs1, arm1, ai, den, fr, fi, phi, t0) = small[:19]
            lre, lim = col("s5_re", 0, ST), col("s5_im", 0, ST)
            magic = 1.5 * 2.0 ** 23
            r = act(dt, col("s5_dt", 0, ST), ACT.Exp, *in_before)
            tt(V, x, lre, dt, ALU.mult, r)
            tt(V, th, lim, dt, ALU.mult)
            ts(V, n, th, 1.0 / TWO_PI, ALU.mult, None, None, V.now)
            ts(V, n, n, magic, ALU.add, magic, ALU.subtract, V.now)
            p1 = 6.28125
            p2 = float(np.float32(np.round((TWO_PI - p1) * 2 ** 24) / 2 ** 24))
            p3 = TWO_PI - p1 - p2
            stt(V, ang, n, -p1, th, ALU.mult, ALU.add, V.now)
            stt(V, ang, n, -p2, ang, ALU.mult, ALU.add, V.now)
            stt(V, ang, n, -p3, ang, ALU.mult, ALU.add, V.now)
            ts(V, ang, ang, 3.1415925, ALU.min, -3.1415925, ALU.max, V.now)
            r = ts(V, phi, ang, 1.0 / TWO_PI, ALU.mult, None, None, V.now)
            act(tn, x, ACT.Tanh, r, scale=0.5)
            act(hs, ang, ACT.Sin, scale=0.5)
            r = act(sn1, ang, ACT.Sin)
            ts(V, t0, tn, -1.0, ALU.mult, 1.0, ALU.add, r)
            V.run(lambda e: e.reciprocal(t0, t0), V.now)
            stt(V, em1, tn, 2.0, t0, ALU.mult, ALU.mult, V.now)
            ts(V, mag, em1, 1.0, ALU.add, None, None, V.now)
            stt(V, cm1, hs, -2.0, hs, ALU.mult, ALU.mult, V.now)
            ts(V, cs1, cm1, 1.0, ALU.add, None, None, V.now)
            tt(V, ai, mag, sn1, ALU.mult, V.now)
            tt(V, arm1, em1, cs1, ALU.mult, V.now)
            tt(V, arm1, arm1, cm1, ALU.add, V.now)
            tt(V, den, lre, lre, ALU.mult)
            tt(V, t0, lim, lim, ALU.mult, V.now)
            tt(V, den, den, t0, ALU.add, V.now)
            V.run(lambda e: e.reciprocal(den, den), V.now)
            tt(V, fr, arm1, lre, ALU.mult, V.now)
            tt(V, t0, ai, lim, ALU.mult, V.now)
            tt(V, fr, fr, t0, ALU.add, V.now)
            tt(V, fr, fr, den, ALU.mult, V.now)
            tt(V, fi, ai, lre, ALU.mult, V.now)
            tt(V, t0, arm1, lim, ALU.mult, V.now)
            tt(V, fi, fi, t0, ALU.subtract, V.now)
            tt(V, fi, fi, den, ALU.mult, V.now)
            c_re, c_im = c_w[:, 0], c_w[:, 1]
            wide = [P, ST, 32]
            frb, fib = fr.unsqueeze(2).broadcast_to(wide), fi.unsqueeze(2).broadcast_to(wide)
            tmp = [cut(buf, temp + 1024 * i, ST, 32) for i in range(3)]
            tt(G, tmp[0], c_re, frb, ALU.mult, params, V.now)
            tt(G, tmp[1], c_im, fib, ALU.mult)
            tt(G, tmp[2], c_re, fib, ALU.mult)
            tt(G, c_im, c_im, frb, ALU.mult, G.now)
            tt(G, c_re, tmp[0], tmp[1], ALU.subtract, G.now)
            tt(G, c_im, tmp[2], c_im, ALU.add, G.now)
            c_ready = G.run(lambda e: e.tensor_scalar(c_im, c_im, -1.0, None, ALU.mult), G.now)

            for i in range(0, 8, 2):
                b, r = gemm_pair([[A["w_in2"][32 + i + j]] for j in range(2)], x2, normed)
                bank_free[b] = [copy(A_, flat(u[:, i:i + 2, :]), psum[:, b, :], r)]
            u_ready = A_.now

            def wide2(v):
                return v.rearrange("p (a t) -> p a t", a=2)

            hold = [buf[:, temp + 512 * i:temp + 512 * i + 512] for i in range(9)]
            spare = [buf[:, 512 * i:512 * i + 512] for i in range(4)]
            t1, t2, w1, w2, f1, f2 = hold[:6]
            trig = [(hold[6], hold[7]), (spare[0], spare[1])]
            state = [(hold[8], spare[2]), (spare[3], work[:, 1024:1536])]
            below = float(np.nextafter(np.float32(TWO_PI), np.float32(0)))

            def s5_steps():
                turns_free, made, rotated, out_read = [c_ready], [None, None], [None, None], [[], []]
                pairs_n = ST // 2
                for p in range(-1, pairs_n + 1):
                    k, nxt = p % 2, p + 1
                    sn, cs = trig[k]
                    zr, zi = state[k]
                    now, ahead = 0 <= p < pairs_n, nxt < pairs_n
                    if now:
                        bu = made[k][1]
                        ps = psum[:, 3:5, :].rearrange("p a (c t) -> p a c t", c=2)
                        br, bi = ps[:, :, 0, :], ps[:, :, 1, :]
                        tt(V, wide2(t1), wide2(cs), br, ALU.mult, *made[k], *out_read[k], V.now)
                        tt(V, wide2(t2), wide2(sn), bi, ALU.mult)
                        tt(V, zr, t1, t2, ALU.add, V.now)
                        tt(V, wide2(t1), wide2(cs), bi, ALU.mult, V.now)
                        tt(V, wide2(t2), wide2(sn), br, ALU.mult)
                        bank_free[3] = bank_free[4] = [V.now]
                        tt(V, zi, t1, t2, ALU.subtract, V.now)
                    if ahead:
                        for j in range(2):
                            i = 2 * nxt + j
                            turned = act(f1[:, j * SEQ:(j + 1) * SEQ], con("time"), ACT.Copy, *turns_free,
                                         scale=phi[:, i:i + 1])
                    yield
                    if now:
                        for j in range(2):
                            s = slice(j * SEQ, (j + 1) * SEQ)
                            m = mag[:, 2 * p + j:2 * p + j + 1].broadcast_to([P, SEQ])
                            for o, z in ((w1, zr), (w2, zi)):
                                scanned = V.run(lambda e, o=o[:, s], z=z[:, s], m=m: e.tensor_tensor_scan(
                                    o, m, z, 0.0, ALU.mult, ALU.add), V.now, *([rotated[1 - k]] if p else []))
                    if ahead:
                        ts(V, f2, f1, magic, ALU.add, magic, ALU.subtract, turned, V.now)
                    yield
                    if now:
                        tt(G, zr, cs, w1, ALU.mult, scanned)
                        tt(G, zi, sn, w1, ALU.mult)
                        tt(G, sn, sn, w2, ALU.mult, G.now)
                        tt(G, cs, cs, w2, ALU.mult)
                        tt(G, zr, zr, sn, ALU.subtract, G.now)
                        rotated[k] = tt(G, zi, zi, cs, ALU.add, G.now)
                    if ahead:
                        turned = tt(V, f1, f1, f2, ALU.subtract, V.now)
                    yield
                    if p >= 1:
                        out_read[1 - k] = [s5_out(p - 1, rotated[1 - k])]
                    if ahead:
                        sn1_, cs1_ = trig[1 - k]
                        free = [rotated[1 - k]] if p >= 1 else [c_ready]
                        act(sn1_, f1, ACT.Sin, turned, *free, scale=below)
                        r = act(cs1_, f1, ACT.Sin, scale=below / 2)
                        turns_free = [r]
                        r = act(cs1_, cs1_, ACT.Square, r)
                        ready = act(cs1_, cs1_, ACT.Identity, r, scale=-2.0, bias=1.0)
                        for j in range(2):
                            i = 2 * nxt + j
                            a, f = 32 * (i % 4), i // 4
                            for c in range(2):
                                r = mm(psum[:, 3 + j, c * SEQ:(c + 1) * SEQ], b_w[a:a + 32, f, c, :],
                                       u[a:a + 32, f, :], True, True, params, u_ready, *bank(3 + j), count=c == 1)
                        made[1 - k] = [ready, r]
                    yield

            def s5_out(p, ready):
                zr, zi = state[p % 2]
                for j in range(2):
                    i = 2 * p + j
                    a = 32 * (i % 4)
                    o = psum[a:a + 32, 5, 0:SEQ]
                    s = slice(j * SEQ, (j + 1) * SEQ)
                    mm(o, c_w[:, 0, i, :], zr[:, s], True, False, ready, *bank(5))
                    r = mm(o, c_w[:, 1, i, :], zi[:, s], False, True, count=j == 1)
                if p % 2:
                    f = p // 2
                    bank_free[5] = [stt(V, u[:, f, :], u[:, f, :], col("s5_d", f), psum[:, 5, 0:SEQ], ALU.mult,
                                        ALU.add, r)]
                return r

            def conv(i, arrived):
                o, pad = qk[:, i, :], qk_pad[:, i % 4, :]
                r = act(o, pad[:, 0:SEQ], ACT.Copy, arrived, scale=col("conv_qk", i))
                for k in range(1, 4):
                    r = stt(V, o, pad[:, k:k + SEQ], col("conv_qk", KT * k + i), o, ALU.mult, ALU.add, r)
                return r

            background.append(s5_steps())
            pace[0] = 1
            pad_read = [cleared, cleared]
            for p in range(8):
                b, r = gemm_pair([[A["w_in2"][2 * p + j]] for j in range(2)], x2, normed)
                r = copy(A_, qk_pad[:, 2 * p % 4:2 * p % 4 + 2, 3:], wide2(psum[:, b, :]), r, cleared, pad_read[p % 2])
                bank_free[b] = [r]
                conv(2 * p, r)
                pad_read[p % 2] = conv(2 * p + 1, r)
                if p < 4:
                    b, r = gemm_tokens([A["w_in2"][16 + 2 * p + j] for j in range(2)], x2, normed)
                    bank_free[b] = [copy(A_, v[:, :, 2 * p * P:(2 * p + 2) * P], wide2(psum[:, b, :]), r)]
                else:
                    f = 2 * (p - 4)
                    b, r = gemm_pair([[A["w_in2"][24 + f + j]] for j in range(2)], x2, normed)
                    bank_free[b] = [copy(A_, flat(sig_o[:, f:f + 2, :]), psum[:, b, :], r)]
            r = gemm_small(8, x2, 7, normed)
            glf = work[:, 960:976]
            tt(V, glf, psum[:, 7, 0:16], bg, ALU.add, r, params)
            bank_free[7] = [V.now]
            while background:
                pump(1)
            pace[0] = 0

            uf = flat(u)
            r = act(uf, uf, ACT.Gelu, V.now)
            for f in range(8):
                b = 3 + f % 2
                mm(psum[:, b, 0:SEQ], glu_w[:, f, 0, :], u[:, f, :], True, True, r, params, *bank(b))
                g_ = mm(psum[:, b, SEQ:], glu_w[:, f, 1, :], u[:, f, :], True, True, count=True)
                s = act(t1[:, SEQ * (f % 2):SEQ * (f % 2) + SEQ], psum[:, b, SEQ:], ACT.Sigmoid, g_, V.now, G.now)
                bank_free[b] = [tt(V, y[:, 8 + f, :], psum[:, b, 0:SEQ], t1[:, SEQ * (f % 2):SEQ * (f % 2) + SEQ],
                                   ALU.mult, s)]

            sof = flat(sig_o)
            act(sof, sof, ACT.Sigmoid)
            s5_done = [V.now, G.now, T.now]
            sm = work[:, 0:960].rearrange("p (i t h) -> p i t h", t=TT, h=MH)[:, 0:40]
            lf, e_, z_, z2_, ng, a_, tot, c_, mx, mt, nmt, si, em, w_ = (sm[:, i] for i in range(14))
            fl = [(sm[:, i].rearrange("p t h -> p (t h)")) for i in range(40)]
            xg = gl[:, :, MH:2 * MH]
            li = gl[:, :, 0:MH]
            copy(V, sm[:, 14], xg, *s5_done)
            softplus_neg(fl[0], fl[14], fl[4], fl[1], fl[2], fl[3], V.now)
            r = ts(V, fl[0], fl[0], -1.0, ALU.mult, None, None, V.now)
            r2 = act(flat(qk), flat(qk), ACT.Silu, r)
            mm(psum[:, 7, 0:8], con("tri"), fl[0], True, True, r, *bank(7))
            r = mm(psum[:, 7, 8:16], ones, fl[0], True, True, count=True)
            bank_free[7] = [V.run(lambda e: e.tensor_copy(work[:, 40:56], psum[:, 7, 0:16]), r)]
            tt(V, c_, li, a_, ALU.subtract, V.now)
            diag = cut(buf, chunk, 8, P)
            for i in range(8):
                r = ts(V, diag[:, i, :], ident, fl[7][:, i:i + 1], ALU.mult, None, None, V.now, *s5_done)
            for t in range(TT):
                r2 = mm(psum[:, 3 + t, :], ones, diag[:, MH * t:MH * t + MH, :].rearrange("p a b -> p (a b)"),
                        True, True, r, *bank(3 + t), count=True)
                ps = psum[:, 3 + t, :].rearrange("p (h s) -> p h s", h=MH)
                if t == 0:
                    V.run(lambda e, ps=ps: e.tensor_reduce(fl[15][:, 0:4], ps, AX.X, ALU.max), r2)
                for hd in range(MH):
                    stt(V, diag[:, MH * t + hd, :], ps[:, hd, :], a_[:, t, hd:hd + 1], con("causal"), ALU.add,
                        ALU.add, r2)
                bank_free[3 + t] = [V.now]
            V.run(lambda e: e.tensor_reduce(fl[8], diag, AX.X, ALU.max), V.now)
            m1, wl = fl[16][:, 0:4], fl[17][:, 0:4]
            tt(V, m1, fl[15][:, 0:4], tot[:, 0], ALU.add, V.now)
            tt(V, m1, m1, tot[:, 0], ALU.max, V.now)
            tt(V, wl, c_[:, 0], tot[:, 0], ALU.add, V.now)
            tt(V, wl, wl, m1, ALU.subtract, V.now)
            mi = sm[:, 18]
            copy(V, mi[:, 0], a_[:, 0], V.now)
            tt(V, mi[:, 1], a_[:, 1], m1, ALU.add, V.now)
            tt(V, fl[9], fl[8], fl[18], ALU.max, V.now)
            ts(V, fl[10], fl[9], -1.0, ALU.mult, None, None, V.now)
            r = tt(V, fl[11], fl[18], fl[9], ALU.subtract, V.now)
            act(wl, wl, ACT.Exp, r)
            act(fl[11], fl[11], ACT.Exp)
            act(fl[12], fl[10], ACT.Exp)
            for i in range(8):
                act(diag[:, i, :], diag[:, i, :], ACT.Exp, bias=fl[10][:, i:i + 1])
            ts(V, fl[11], fl[11], MD ** -0.5, ALU.mult, None, None, A_.now)
            weights_ready = V.now

            k_tok = cut(buf, chunk + 1024, MH, MD)
            for hd in range(MH):
                b = 5 + hd % 2
                for j in range(2):
                    r = tr(psum[:, b, j * P:(j + 1) * P], qk[:, 8 + 2 * hd + j, 0:P], A_.now, *bank(b), count=j == 1)
                bank_free[b] = [ts(V, k_tok[:, hd, :], psum[:, b, 0:MD], wl[:, hd:hd + 1], ALU.mult, None, None,
                                   r, weights_ready)]
            probs = cut(buf, chunk + 2048, 8, P)
            turned = cut(buf, chunk + 3072, 8, P)
            for t in range(TT):
                tok = slice(t * P, (t + 1) * P)
                for hd in range(MH):
                    for j in range(2):
                        r = mm(psum[:, 3, hd * P:(hd + 1) * P], qk[:, 2 * hd + j, tok], qk[:, 8 + 2 * hd + j, tok],
                               j == 0, j == 1, *bank(3), count=j == 1)
                cols4 = slice(MH * t, MH * t + MH)
                ps = psum[:, 3, :].rearrange("p (h s) -> p h s", h=MH)
                r = stt(V, probs[:, cols4, :], ps, MD ** -0.5, diag[:, cols4, :], ALU.mult, ALU.mult, r, A_.now)
                bank_free[3] = [r]
                for hd in range(MH):
                    r2 = tr(psum[:, 4, hd * P:(hd + 1) * P], probs[:, MH * t + hd, :], r, *bank(4), count=hd == 3)
                bank_free[4] = [copy(A_, turned[:, cols4, :].rearrange("p a b -> p (a b)"), psum[:, 4, :], r2)]
            hm = cut(buf, temp, 8, MD + 1)
            c0 = [cut(buf, temp + 2060 + 514 * i, 2, MD + 1) for i in range(2)]
            c0_read = [[], []]
            for hd in range(MH):
                vs = slice(hd * MD, (hd + 1) * MD)
                for j in range(2):
                    b = 5 + j
                    kd = k_tok[:, hd, j * P:(j + 1) * P]
                    mm(psum[:, b, 0:MD], kd, v[:, 0, vs], True, True, V.now, A_.now, *bank(b))
                    r = mm(psum[:, b, MD:MD + 1], kd, ones[:, 0:1], True, True, count=True)
                    bank_free[b] = [copy(A_, c0[hd % 2][:, j, :], psum[:, b, 0:MD + 1], r, *c0_read[hd % 2])]
                c0_ready = A_.now
                for t in range(TT):
                    i = MH * t + hd
                    mm(psum[:, t, 0:MD], turned[:, i, :], v[:, t, vs], True, True, *bank(t))
                    r = mm(psum[:, t, MD:MD + 1], turned[:, i, :], ones[:, 0:1], True, True, count=True)
                    bank_free[t] = [copy(A_, hm[:, i, :], psum[:, t, 0:MD + 1], r, *s5_done)]
                for j in range(2):
                    r = mm(psum[:, 2, 0:MD + 1], qk[:, 2 * hd + j, P:SEQ], c0[hd % 2][:, j, :], j == 0, j == 1,
                           c0_ready, *bank(2), count=j == 1)
                c0_read[hd % 2] = [r]
                i = MH + hd
                bank_free[2] = [stt(V, hm[:, i, :], psum[:, 2, 0:MD + 1], fl[11][:, i:i + 1], hm[:, i, :], ALU.mult,
                                    ALU.add, r, A_.now)]
            dn, ms = fl[20], fl[21]
            d_ = hm[:, :, MD]
            ts(V, fl[22], d_, -1.0, ALU.mult, None, None, V.now, A_.now)
            tt(V, dn, d_, fl[22], ALU.max, V.now)
            tt(V, dn, dn, fl[12], ALU.max, V.now)
            V.run(lambda e: e.reciprocal(dn, dn), V.now)
            for i in range(8):
                r = ts(V, hm[:, i, 0:MD], hm[:, i, 0:MD], dn[:, i:i + 1], ALU.mult, None, None, V.now)
                act(sq[:, i % 2, 0:MD], hm[:, i, 0:MD], ACT.Square, r, A_.now, accum=ms[:, i:i + 1])
            ts(V, ms, ms, 1.0 / MD, ALU.mult, EPS, ALU.add, A_.now)
            r = act(ms, ms, ACT.Sqrt, V.now)
            V.run(lambda e: e.reciprocal(ms, ms), r)
            for i in range(8):
                t, hd = i // MH, i % MH
                r = ts(V, hm[:, i, 0:MD], hm[:, i, 0:MD], ms[:, i:i + 1], ALU.mult, None, None, V.now)
                b = 3 + i % 2
                for j in range(2):
                    r2 = tr(psum[:, b, j * P:(j + 1) * P], hm[:, i, j * P:(j + 1) * P], r, *bank(b), count=j == 1)
                for j in range(2):
                    f = 2 * hd + j
                    tok = slice(t * P, (t + 1) * P)
                    stt(V, y[:, f, tok], psum[:, b, j * P:(j + 1) * P], col("mlstm_norm", f), sig_o[:, f, tok],
                        ALU.mult, ALU.mult, r2)
                bank_free[b] = [V.now]
            mixed = V.now

            for i in range(0, KT, 2):
                mixed = split(flat(y[:, i:i + 2, :]), x2, i, mixed, T.now)
            for i in range(0, KT, 2):
                b, r = gemm_pair([[A["w_out2"][i + j]] for j in range(2)], x2, mixed)
                hh = flat(h[:, i:i + 2, :])
                r = tt(V, hh, hh, psum[:, b, :], ALU.add, r)
                bank_free[b] = [r]
                total = sum_squares(hh, i == 0, i == KT - 2, r)
            root(total, D)
            normed2 = scaled_split(h, x2, "norm2", KT)

            before = [V.now, A_.now, G.now, T.now]
            gate_buf, route = phase(("peer_gates", CHUNK * SEQ, F32), ("routing", 3 * KT * SEQ, F32))
            _, hid_buf, hot_buf = phase(("peer_gates_", CHUNK * SEQ, F32), ("peer_hidden", CHUNK * 2 * SEQ, F32R),
                                        ("one_hots", 2 * HOTS * (P + 2 * CHUNK), F32R))
            gates = cut(gate_buf, 0, CHUNK, SEQ)
            hidden = cut(hid_buf, 0, CHUNK, 2, SEQ)
            hots1 = cut(hot_buf, 0, 2, HOTS, P)
            hots2 = hot_buf[:, 2 * HOTS * P:].rearrange("p (b t w n) -> p b t w n", b=2, t=HOTS, w=2)

            q2 = cut(route, 0, KT, SEQ)
            sc = cut(route, 4096, PH, 4 * P)
            keys = cut(route, 8192, 2, P)
            keys_in = load([(keys, A["subkeys"])], *before)
            for i in range(0, KT, 2):
                b, r = gemm_pair([[A["wq2"][i + j]] for j in range(2)], x2, normed2)
                r = copy(V, flat(q2[:, i:i + 2, :]), psum[:, b, :], r, *before)
                bank_free[b] = [r]
                b = 3 + (i // 2) % 2
                for t in range(TT):
                    for j in range(2):
                        s = (2 * t + j) * P
                        g_ = mm(psum[:, b, s:s + P], q2[:, i + j, t * P:(t + 1) * P], keys[:, j, :], True, True,
                                r, keys_in, *bank(b), count=t == 1 and j == 1)
                bank_free[b] = [copy(A_, sc[:, i // 2, :], psum[:, b, :], g_, *before)]
            scored = A_.now
            queries_read = T.now
            top_v = work[:, 0:512].rearrange("p (h t s k) -> p h t s k", h=PH, t=TT, s=2)
            top_i = work[:, 512:1024].bitcast(U32).rearrange("p (h t s k) -> p h t s k", h=PH, t=TT, s=2)
            top_f = work[:, 1024:1536].rearrange("p (h t s k) -> p h t s k", h=PH, t=TT, s=2)

            def top16(vals, idx, src):
                a, b = slice(0, 8), slice(8, 16)
                V.run(lambda e: e.max(vals[:, a], src), V.now, scored, queries_read)
                V.run(lambda e: e.max_index(idx[:, a], vals[:, a], src), V.now)
                V.run(lambda e: e.match_replace(src, vals[:, a], src, -3.0e38), V.now)
                V.run(lambda e: e.max(vals[:, b], src), V.now)
                return V.run(lambda e: e.max_index(idx[:, b], vals[:, b], src), V.now)

            def tail(at, n):
                return route[:, 8448 + at:8448 + at + n]

            cand = tail(0, 256).rearrange("p (a b) -> p a b", a=TOPK)
            best = tail(256, 256).rearrange("p (t h k) -> p t h k", t=TT, h=PH)
            place = tail(512, 256).bitcast(U32)
            place4 = place.rearrange("p (t h k) -> p t h k", t=TT, h=PH)
            part_u = tail(768, 256).bitcast(U32)
            part = [tail(1024 + 256 * s, 256).rearrange("p (t n) -> p t n", t=TT) for s in range(2)]
            peak = tail(1536, 16)
            lists = tail(1600, 768).rearrange("p (w t n) -> p w t n", w=3, t=TT)
            hot = tail(2400, 1024)
            def routing():
                for hd in range(PH):
                    for t in range(TT):
                        for s in range(2):
                            top16(top_v[:, hd, t, s], top_i[:, hd, t, s], sc[:, hd, (2 * t + s) * P:(2 * t + s + 1) * P])
                        yield
                yield
                copy(V, work[:, 1024:1536], work[:, 512:1024].bitcast(U32), V.now)
                for t in range(TT):
                    for hd in range(PH):
                        a_s = top_v[:, hd, t, 0].unsqueeze(2).broadcast_to([P, TOPK, TOPK])
                        b_s = top_v[:, hd, t, 1].unsqueeze(1).broadcast_to([P, TOPK, TOPK])
                        tt(V, cand, a_s, b_s, ALU.add, V.now)
                        top16(best[:, t, hd], place4[:, t, hd], cand.rearrange("p a b -> p (a b)"))
                        yield
                for s, op, k in ((0, ALU.logical_shift_right, 4), (1, ALU.bitwise_and, 15)):
                    V.run(lambda e, op=op, k=k: e.tensor_scalar(part_u, place, k, None, op), V.now)
                    copy(V, part[s].rearrange("p t n -> p (t n)"), part_u, V.now)
                iota16 = con("iota")[:, 0:TOPK]
                for s in range(2):
                    for t in range(TT):
                        for hh in range(2):
                            n = 4 * TOPK
                            o = hot.rearrange("p (n k) -> p n k", n=n)
                            tt(V, o, part[s][:, t, hh * n:(hh + 1) * n].unsqueeze(2).broadcast_to([P, n, TOPK]),
                               iota16.unsqueeze(1).broadcast_to([P, n, TOPK]), ALU.is_equal, V.now)
                            for q4 in range(4):
                                o4 = o[:, q4 * TOPK:(q4 + 1) * TOPK, :]
                                tt(V, o4, o4, top_f[:, 4 * hh + q4, t, s].unsqueeze(1).broadcast_to([P, TOPK, TOPK]),
                                   ALU.mult, V.now)
                            V.run(lambda e, o=o, d=lists[:, s, t, hh * n:(hh + 1) * n]: e.tensor_reduce(
                                d, o, AX.X, ALU.add), V.now)
                            yield
                bf = tail(256, 256).rearrange("p (a k) -> p a k", k=TOPK)
                copy(V, peak, bf[:, :, 0], V.now)
                tt(V, bf, bf, peak.unsqueeze(2).broadcast_to([P, 16, TOPK]), ALU.subtract, V.now)
                r = act(tail(256, 256), tail(256, 256), ACT.Exp, V.now)
                V.run(lambda e: e.tensor_reduce(peak, bf, AX.X, ALU.add), r)
                V.run(lambda e: e.reciprocal(peak, peak), V.now)
                yield tt(V, lists[:, 2].rearrange("p t (h k) -> p (t h) k", h=PH), bf,
                            peak.unsqueeze(2).broadcast_to([P, 16, TOPK]), ALU.mult, V.now)

            pairs = work[:, 0:4 * SEQ].rearrange("p (w t) -> p w t", w=4)
            iota = con("iota")
            batches = 2
            hot_read = [[] for _ in range(batches)]
            mask_read = [[] for _ in range(batches)]
            masks = work[:, 1280:1280 + batches * HOTS * CHUNK].rearrange("p (b t n) -> p b t n", b=batches, t=HOTS)

            def turn_lists():
                for w in range(3):
                    for t in range(TT):
                        s = (2 * w + t) * P
                        r = tr(psum[:, 5 + s // 512, s % 512:s % 512 + P], lists[:, w, t, :], V.now,
                               *bank(5), *bank(6), count=w == 2 and t == 1)
                gate = work[:, 1024:1280]
                copy(V, work[:, 0:512], psum[:, 5, :], r)
                r = copy(V, gate, psum[:, 6, 0:SEQ])
                bank_free[5] = bank_free[6] = [r]
                big = ts(V, pairs[:, 2, :], gate, 4097.0, ALU.mult, None, None, r)
                tt(V, pairs[:, 3, :], pairs[:, 2, :], gate, ALU.subtract, big)
                tt(V, pairs[:, 2, :], pairs[:, 2, :], pairs[:, 3, :], ALU.subtract, V.now)
                return tt(V, pairs[:, 3, :], gate, pairs[:, 2, :], ALU.subtract, V.now)

            def make_hots(c, t, listed):
                k = t // HOTS % batches
                toks = slice(t, t + HOTS)
                one, two, mask = hots1[:, k], hots2[:, k], masks[:, k]
                wide, thin = [P, HOTS, P], [P, HOTS, CHUNK]

                def row(w, shape):
                    return pairs[:, w, toks].unsqueeze(2).broadcast_to(shape)

                keys2 = iota[:, CHUNK * c:CHUNK * (c + 1)].unsqueeze(1).broadcast_to(thin)
                m = tt(V, mask, keys2, row(1, thin), ALU.is_equal, listed, *mask_read[k])
                v1 = tt(V, one, iota.unsqueeze(1).broadcast_to(wide), row(0, wide), ALU.is_equal, *hot_read[k])
                tt(V, two[:, :, 0, :], mask, row(2, thin), ALU.mult, m)
                g1 = tt(G, two[:, :, 1, :], mask, row(3, thin), ALU.mult, m, *hot_read[k])
                mask_read[k] = [g1]
                return [g1, V.now]

            def gate_chunk(c, listed, onto, gates_read):
                made = make_hots(c, 0, listed)
                for t in range(0, SEQ, HOTS):
                    following = make_hots(c, t + HOTS, listed) if t + HOTS < SEQ else None
                    yield
                    k, b = t // HOTS % batches, 3 + (t // 16) % 2
                    for i in range(HOTS):
                        at = CHUNK * ((t + i) % 16)
                        o = psum[:, b, at:at + CHUNK]
                        mm(o, hots1[:, k, i, :], hots2[:, k, i, 0, :], True, False, *made, *bank(b))
                        r = mm(o, hots1[:, k, i, :], hots2[:, k, i, 1, :], False, True, count=i == HOTS - 1)
                    hot_read[k] = [r]
                    made = following
                    if (t + HOTS) % 16 == 0:
                        g = gates[:, :, t + HOTS - 16:t + HOTS]
                        p = psum[:, b, :].rearrange("p (t n) -> p n t", n=CHUNK)
                        if onto:
                            bank_free[b] = [tt(V, g, g, p, ALU.mult, r, A_.now)]
                        else:
                            bank_free[b] = [copy(A_, g, p, r, gates_read)]
                    yield

            background.append(routing())
            pace[0] = 1
            for c in range(NKEY // CHUNK):
                if c:
                    while background:
                        pump(1)
                    gates_ready = [A_.now]
                pace[0] = pace[0] if c == 0 else 0
                for i in range(0, CHUNK, 2):
                    b, r = gemm_pair([[A["peer_u"][CHUNK * c + i + j]] for j in range(2)], x2, normed2)
                    if c == 0:
                        bank_free[b] = [act(flat(gates[:, i:i + 2, :]), psum[:, b, :], ACT.Gelu, r, *before)]
                        continue
                    k = sq_turn[0] % 2
                    sq_turn[0] += 1
                    s = act(sq[:, k, :], psum[:, b, :], ACT.Gelu, r, sq_free[k])
                    bank_free[b] = [s]
                    s = tt(V, sq[:, k, :], sq[:, k, :], flat(gates[:, i:i + 2, :]), ALU.mult, s, *gates_ready)
                    sq_free[k] = split(sq[:, k, :], hidden, i, s, hidden_free)
                if c == 0:
                    while background:
                        pump(1)
                    pace[0] = 0
                    listed = turn_lists()
                    for _ in gate_chunk(0, listed, True, None):
                        pass
                    for i in range(0, CHUNK, 2):
                        split(flat(gates[:, i:i + 2, :]), hidden, i, V.now)
                    hidden_ready = V.now
                else:
                    hidden_ready = V.now
                if c + 1 < NKEY // CHUNK:
                    background.append(gate_chunk(c + 1, listed, False, V.now))
                    pace[0] = 2
                for i in range(0, KT, 2):
                    b, r = gemm_pair([[A["peer_v"][i + j, 2 * c + k] for k in range(2)] for j in range(2)], hidden,
                                     hidden_ready)
                    hh = flat(h[:, i:i + 2, :])
                    r = tt(V, hh, hh, psum[:, b, :], ALU.add, r)
                    bank_free[b] = [r]
                    if c == NKEY // CHUNK - 1:
                        total = sum_squares(hh, i == 0, i == KT - 2, r)
                hidden_free = T.now
            root(total, D)
            for i in range(KT):
                stt(V, h[:, i, :], h[:, i, :], col("final", i), rstd[:, :], ALU.mult, ALU.mult, V.now)


        loaded = load([(cols[:, :], A["cols"]), (const[:, :], A["consts"])])
        x_in = load([(flat(h[:, :, :]), A["x"])])
        for q in (T, V, A_, G):
            q.wait(loaded, x_in)

        first_block()
        second_block()

        store = load([(out, flat(h[:, :, :]))],
                     V.now, A_.now, G.now, T.now, queue=S)
        S.wait(store)

        block = ctx.enter_context(nc.Block())
        block.sync(lambda e: S.play(e))
        block.scalar(lambda e: A_.play(e))
        block.vector(lambda e: V.play(e))
        block.gpsimd(lambda e: G.play(e))
        block.tensor(lambda e: T.play(e))


def _units(w):
    k, f = w.shape
    w = w.reshape(k // UNIT * 1, KT, P, f // P, P) if k >= UNIT else w.reshape(1, k // P, P, f // P, P)
    return w.transpose(3, 0, 2, 1, 4).reshape(-1, P, w.shape[1] * P)


def _columns(v):
    v = v.reshape(-1, v.shape[-1] // P, P)
    return v.transpose(2, 0, 1).reshape(P, -1)


def _features(x):
    t, f = x.shape
    return x.reshape(t, f // P, P).transpose(2, 1, 0).reshape(P, -1)


def _bucket(dist):
    n = np.maximum(dist, 1).astype(np.float32)
    large = 16 + (np.log(n / 16) / math.log(8) * 16).astype(np.int32)
    return np.where(dist < 16, dist, np.minimum(large, NBUCKET - 1))


def _one_hot(dist):
    b = np.where(dist < 0, NBUCKET, _bucket(np.maximum(dist, 0)))
    return (b[None] == np.arange(NBUCKET + 1).reshape(-1, *[1] * dist.ndim)).astype(np.float32)


def _constants():
    i = np.arange(P)
    parts = {
        "ident": np.eye(P), "ones": np.ones((P, P)), "tri": i[:, None] <= i[None, :],
        "causal": np.where(i[None, :] <= i[:, None], 0.0, NEG), "iota": np.tile(i, (P, 1)),
        "time": np.tile(np.arange(1, SEQ + 1), (P, 1)),
        "any": np.arange(SEQ).reshape(TT, P).T >= CMP_LEN - 1,
    }
    return np.concatenate([parts[n].astype(np.float32) for n in CONST], axis=1)


def kernel(**inputs):
    import concourse.bacc as bacc
    from concourse.bass_utils import run_bass_kernel_spmd

    x = {k: np.asarray(v) for k, v in inputs.items()}
    x = {k: v[0] if v.shape[0] == 1 and k != "x" else v for k, v in x.items()}
    arrays = {"consts": _constants(), "x": _features(x["x"][0])}

    def per_state(v):
        return v.reshape(ST, P).T

    col_parts = {
        "norm_mix_pre": x["norm_mix_pre"], "norm_mix_post": x["norm_mix_post"], "norm_mlp_pre": x["norm_mlp_pre"],
        "norm_mlp_post": x["norm_mlp_post"], "conv_w": x["conv_w"], "conv_b": x["conv_b"],
        "lru_ba": x["lru_ba"].reshape(-1), "lru_bx": x["lru_bx"].reshape(-1), "lru_lambda": x["lru_lambda"],
        "gnorm_lru": x["gnorm_lru"], "gnorm_nsa": x["gnorm_nsa"], "norm1": x["norm1_g_2"],
        "conv_qk": x["conv_qk_w_2"], "mlstm_norm": x["mlstm_norm_g_2"],
        "s5_re": x["s5_lambda_re_2"].reshape(-1), "s5_im": x["s5_lambda_im_2"].reshape(-1),
        "s5_dt": np.repeat(x["s5_log_dt_2"], NSTATE), "s5_d": x["s5_d_2"].reshape(-1),
        "norm2": x["norm2_g_2"], "final": x["final_g_2"],
    }
    arrays["cols"] = np.concatenate([_columns(col_parts[n]) for n in COLS], axis=1)

    i = np.arange(384)
    t, n = np.arange(P), np.arange(NCMP)
    dist = (np.arange(TT)[:, None, None] * P + t[None, None, :]) - (n[None, :, None] * CMP_STRIDE + CMP_LEN - 1)
    arrays["hot_rel"] = _one_hot(SEQ - 1 - i)
    arrays["hot_cmp"] = _one_hot(dist).reshape(NBUCKET + 1, TT * NCMP, P)
    arrays["rel_bias"] = x["rel_bias"]
    arrays["cmp_pe"] = np.stack([x["cmp_pe_k"], x["cmp_pe_v"]]).transpose(2, 0, 1)
    arrays["cmp_w1"] = np.stack([_units(x["cmp_w1_k"]), _units(x["cmp_w1_v"])])
    arrays["cmp_w2"] = np.stack([x["cmp_w2_k"], x["cmp_w2_v"]]).reshape(2, 2, P, HEAD).transpose(2, 0, 1, 3)
    arrays["lru_w"] = np.stack([x["lru_wa"], x["lru_wx"]]).reshape(2, 8, 2, 64, 64).transpose(2, 3, 0, 1, 4)
    arrays["w_in"] = _units(x["w_in"][:, :4608])
    arrays["w_gates"] = x["w_in"][:, 4608:].reshape(KT, P, 48).transpose(1, 0, 2).reshape(P, -1)
    for name in ("w_out", "mlp_w1", "mlp_w2", "ple_gate"):
        arrays[name] = _units(x[name])
    arrays["ple_proj"] = x["ple_proj"].reshape(2, P, 2, 8, P).transpose(2, 1, 3, 0, 4).reshape(2, P, UNIT)
    arrays["p"] = _features(x["p"][0]).reshape(P, 2, SEQ)

    w = x["w_in_2"]
    arrays["w_in2"] = np.concatenate([_units(w[:, :4096]), _units(w[:, 4104:])])
    arrays["w_gates2"] = w[:, 4096:4104].reshape(KT, P, 8).transpose(1, 0, 2).reshape(P, -1)
    arrays["b_gates2"] = np.broadcast_to(np.tile(x["b_gates_2"], TT), (P, TT * 8))
    arrays["w_out2"] = _units(x["w_out_2"])
    b = np.stack([x["s5_b_re_2"], x["s5_b_im_2"]])
    arrays["s5_b"] = b.reshape(2, 8, 4, 2, NSTATE, GSZ).transpose(2, 3, 5, 1, 0, 4)
    c = np.stack([x["s5_c_re_2"], x["s5_c_im_2"]])
    arrays["s5_c"] = c.reshape(2, ST, 2, GSZ, NSTATE).transpose(2, 4, 0, 1, 3)
    arrays["s5_glu"] = x["s5_glu_w_2"].reshape(8, 8, GSZ, 2, GSZ).transpose(1, 2, 0, 3, 4)
    arrays["wq2"] = _units(x["peer_wq_2"])
    arrays["subkeys"] = x["peer_subkeys_2"].transpose(2, 0, 1)
    arrays["peer_u"] = x["peer_u_2"].reshape(NKEY, NKEY, KT, P).transpose(1, 3, 2, 0).reshape(NKEY, P, UNIT)
    arrays["peer_v"] = x["peer_v_2"].reshape(NKEY, 8, 16, KT, P).transpose(3, 1, 0, 2, 4).reshape(KT, 8, P, UNIT)

    nc = bacc.Bacc("TRN2", target_bir_lowering=False, num_devices=1)
    arrays = {f"in_{k}": np.ascontiguousarray(v) for k, v in arrays.items()}
    aps = {k[3:]: nc.dram_tensor(k, v.shape, mybir.dt.from_np(v.dtype), kind="ExternalInput").ap()
           for k, v in arrays.items()}
    out = nc.dram_tensor("out", (P, KT * SEQ), F32, kind="ExternalOutput").ap()
    build(nc, aps, out)
    r = run_bass_kernel_spmd(nc, [arrays], core_ids=[0])
    got = np.asarray(r.results[0]["out"])
    return np.ascontiguousarray(got.reshape(P, KT, SEQ).transpose(2, 1, 0)).reshape(1, SEQ, D)
```

```python
from contextlib import ExitStack
import math

import numpy as np

import concourse.bass as bass
from concourse import mybir

F32 = mybir.dt.float32
F32R = mybir.dt.float32r
BF16 = mybir.dt.bfloat16
U32 = mybir.dt.uint32
ALU = mybir.AluOpType
ACT = mybir.ActivationFunctionType
AX = mybir.AxisListType

P = 128
SEQ = 256
TT = SEQ // P
D = 2048
KT = D // P
EPS = 1e-6
NEG = -1e30

HEAD = 64
NH = 16
NKV = 4
REP = NH // NKV
CMP_LEN, CMP_STRIDE = 32, 16
NCMP = (SEQ - CMP_LEN) // CMP_STRIDE + 1
NBUCKET = 32
D_FF = 4 * D

MW = 1024
MH = 4
MD = MW // MH
GROUPS, GSZ, NSTATE = 64, 16, 64
ST = GROUPS * NSTATE // P
PH = 8
NKEY = 128
TOPK = 16

UNIT = KT * P
HALF = UNIT // 2
SLOTS = 4
SPLITS = 3
CHUNK = 32
HOTS = 8
BUDGET = 26605
TWO_PI = 2.0 * math.pi

COLS = {}
for _name, _n in (("norm_mix_pre", 16), ("norm_mix_post", 16), ("norm_mlp_pre", 16), ("norm_mlp_post", 16),
                  ("conv_w", 32), ("conv_b", 8), ("lru_ba", 8), ("lru_bx", 8), ("lru_lambda", 8),
                  ("gnorm_lru", 8), ("gnorm_nsa", 8), ("norm1", 16), ("conv_qk", 64), ("mlstm_norm", 8),
                  ("s5_re", 32), ("s5_im", 32), ("s5_dt", 32), ("s5_d", 8), ("norm2", 16), ("final", 16)):
    COLS[_name] = (sum(n for _, n in COLS.values()), _n)
NCOLS = sum(n for _, n in COLS.values())

CONST = {}
for _name, _n in (("ident", P), ("ones", P), ("tri", P), ("causal", P), ("iota", P), ("time", SEQ), ("any", TT)):
    CONST[_name] = (sum(n for _, n in CONST.values()), _n)
NCONST = sum(n for _, n in CONST.values())


class Queue:

    def __init__(self, sem):
        self.sem, self.count, self.steps, self.seen = sem, 0, [], {}

    @property
    def now(self):
        return (self.sem, self.count)

    def wait(self, *after):
        for sem, value in after:
            if value > self.seen.get(sem.name, 0):
                self.seen[sem.name] = value
                self.steps.append(lambda e, s=sem, v=value: e.wait_ge(s, v))

    def run(self, emit, *after, count=True):
        self.wait(*after)
        if count:
            self.count += 1
            self.steps.append(lambda e: emit(e).then_inc(self.sem, 1))
        else:
            self.steps.append(emit)
        return self.now

    def play(self, engine):
        for step in self.steps:
            step(engine)


def build(nc, A, out):
    with ExitStack() as ctx:
        def sb(name, *shape):
            return ctx.enter_context(nc.sbuf_tensor(name, list(shape), F32))

        def sem(name):
            return ctx.enter_context(nc.semaphore(name))

        h = sb("h", P, KT, SEQ)
        x2 = ctx.enter_context(nc.sbuf_tensor("x2", [P, KT, 2, SEQ], F32R))
        raw = sb("raw", P, SLOTS, HALF)
        w_hi = ctx.enter_context(nc.sbuf_tensor("w_hi", [P, SPLITS, HALF], F32R))
        w_lo = ctx.enter_context(nc.sbuf_tensor("w_lo", [P, SPLITS, HALF], F32R))
        cols = sb("cols", P, NCOLS)
        const = sb("const", P, NCONST)
        sq = sb("sq", P, 2, 512)
        rstd = sb("rstd", P, SEQ)
        work = sb("work", P, 1536)
        psum = ctx.enter_context(nc.psum_tensor("psum", [P, 8, 512], F32))
        scratch = nc.dram_tensor("scratch_bias", [NH, P, 384], F32, kind="Internal").ap()

        def phase(*tensors):
            total = sum(n // 2 if dt == BF16 else n for _, n, dt in tensors)
            assert total <= BUDGET, total
            with ExitStack() as held:
                return [held.enter_context(nc.sbuf_tensor(name, [P, n], dt)) for name, n, dt in tensors]

        T, V, A_, G = (Queue(sem(n)) for n in ("pe_done", "dve_done", "act_done", "pool_done"))
        S = Queue(sem("sp_done"))
        slot_sem = [sem(f"slot{i}") for i in range(SLOTS)]
        load_sems = []

        def col(name, i=0, n=1):
            at = COLS[name][0] + i
            return cols[:, at:at + n]

        def con(name):
            at, n = CONST[name]
            return const[:, at:at + n]

        ident, ones = con("ident"), con("ones")

        def cut(buf, at, *shape):
            n = int(np.prod(shape))
            v = buf[:, at:at + n]
            if len(shape) == 2:
                v = v.rearrange("p (a b) -> p a b", a=shape[0])
            if len(shape) == 3:
                v = v.rearrange("p (a b c) -> p a b c", a=shape[0], b=shape[1])
            return v

        def tt(q, o, a, b, op, *after):
            return q.run(lambda e: e.tensor_tensor(o, a, b, op), *after)

        def ts(q, o, a, s1, op0, s2, op1, *after):
            if op1 is None:
                return q.run(lambda e: e.tensor_scalar(o, a, s1, None, op0), *after)
            return q.run(lambda e: e.tensor_scalar(o, a, s1, s2, op0, op1), *after)

        def stt(q, o, a, s, b, op0, op1, *after):
            return q.run(lambda e: e.scalar_tensor_tensor(out=o, in0=a, scalar=s, in1=b, op0=op0, op1=op1), *after)

        def act(o, i, func, *after, bias=0.0, scale=1.0, accum=None):
            if accum is None:
                return A_.run(lambda e: e.activation(o, i, func, bias=bias, scale=scale), *after)
            return A_.run(lambda e: e.activation(o, i, func, bias=bias, scale=scale, accum_out=accum), *after)

        def copy(q, o, i, *after):
            if q is A_:
                return act(o, i, ACT.Copy, *after)
            return q.run(lambda e: e.tensor_copy(o, i), *after)

        def fill(q, o, value, *after):
            return q.run(lambda e: e.memset(o, value), *after)

        def mm(o, l, r, start, stop, *after, count=False):
            return T.run(lambda e: e.matmul(o, l, r, start=start, stop=stop), *after, count=count)

        def tr(o, i, *after, count=False):
            n = i.shape[0]
            return T.run(lambda e: e.transpose(o, i, ident[0:n, 0:n]), *after, count=count)

        def load(pairs, *after, queue=None):
            s = sem(f"load{len(load_sems)}")
            load_sems.append(s)
            q = queue or A_
            q.wait(*after)
            for o, i in pairs:
                q.steps.append(lambda e, o=o, i=i: e.dma_start(o, i).then_inc(s, 16))
            return (s, 16 * len(pairs))

        plan = []
        issued = [0]
        used = [0]
        raw_free = [[] for _ in range(SLOTS)]
        split_free = [[] for _ in range(SPLITS)]
        split_made = [None] * SPLITS
        split_turn = [0]
        arrived = {}

        def plan_tokens(src):
            plan.extend([(src[:, c * HALF:(c + 1) * HALF], HALF, True) for c in range(4)])

        def plan_units(*srcs):
            for src in srcs:
                plan.extend([(src[:, 0:HALF], HALF, True), (src[:, HALF:UNIT], HALF, True)])

        def issue():
            n = issued[0]
            src, size, split = plan[n]
            k = n % SLOTS
            S.wait(*raw_free[k])
            dst, s, landed = raw[:, k, 0:size], slot_sem[k], (slot_sem[k], 16 * (n // SLOTS + 1))
            S.steps.append(lambda e: e.dma_start(dst, src).then_inc(s, 16))
            issued[0] += 1
            if not split:
                arrived[n] = (dst, None, [landed])
                return
            m = split_turn[0] % SPLITS
            split_turn[0] += 1
            hi, lo = w_hi[:, m, 0:size], w_lo[:, m, 0:size]
            r = act(hi, dst, ACT.Copy, landed, *split_free[m])
            q = G if pool_helps[0] and m == 0 else V
            r2 = tt(q, lo, dst, hi.bitcast(F32), ALU.subtract, r, landed, *split_free[m])
            split_made[m] = r2
            raw_free[k] = [r, r2]
            arrived[n] = ((hi, lo), m, [r, r2])

        pool_helps = [False]
        background = []

        def pump(steps):
            for _ in range(steps):
                if background and next(background[0], finished) is finished:
                    background.pop(0)

        finished = object()
        pace = [0]

        def next_unit(src=None, held=0):
            n = used[0]
            if src is not None:
                assert plan[n][0].offset == src.offset and plan[n][0].tensor.name == src.tensor.name, n
            used[0] += 1
            while issued[0] < min(n + SPLITS - held, len(plan)):
                issue()
            pump(pace[0])
            return n, *arrived.pop(n)

        def prefetch():
            while issued[0] < min(used[0] + SPLITS, len(plan)):
                issue()

        def leave(n, m, r):
            if m is None:
                raw_free[n % SLOTS] = [r]
            else:
                split_free[m] = [r, split_made[m]]

        bank_free = [[] for _ in range(8)]

        def bank(b):
            return bank_free[b]

        gemm_turn = [0]

        gemm_banks = [3]

        def gemm_bank():
            gemm_turn[0] += 1
            return (gemm_turn[0] - 1) % gemm_banks[0]

        def tile_ready(ready, k):
            return [r[k // 2] if isinstance(r, list) else r for r in ready]

        def gemm_pair(units, x, *ready, halves=None):
            b = gemm_bank()
            for j, srcs in enumerate(units):
                o = psum[:, b, j * SEQ:(j + 1) * SEQ]
                cs = halves or range(2 * len(srcs))
                for c in cs:
                    n, (hi, lo), m, landed = next_unit(srcs[c // 2][:, (c % 2) * HALF:(c % 2 + 1) * HALF])
                    hi, lo = (w.rearrange("p (k f) -> p k f", k=8) for w in (hi, lo))
                    for i in range(8):
                        k = 8 * c + i
                        first, last = k == 8 * cs[0], k == 8 * cs[-1] + 7
                        mm(o, hi[:, i, :], x[:, k, 0, :], first, False, *landed, *bank(b), *tile_ready(ready, k))
                        mm(o, hi[:, i, :], x[:, k, 1, :], False, False)
                        r = mm(o, lo[:, i, :], x[:, k, 0, :], False, last, count=i == 7)
                    leave(n, m, r)
            return b, r

        def gemm_tokens(src, x, *ready):
            banks = [gemm_bank() for _ in range(TT)]
            for c in range(4):
                n, (hi, lo), m, landed = next_unit(src[:, c * HALF:(c + 1) * HALF])
                hi, lo = (w.rearrange("p (k f) -> p k f", k=4) for w in (hi, lo))
                for t, b in enumerate(banks):
                    o = psum[:, b, 0:SEQ]
                    tok = slice(t * P, (t + 1) * P)
                    for i in range(4):
                        k = 4 * c + i
                        mm(o, x[:, k, 0, tok], hi[:, i, :], k == 0, False, *landed, *bank(b), *tile_ready(ready, k))
                        mm(o, x[:, k, 0, tok], lo[:, i, :], False, False)
                        r = mm(o, x[:, k, 1, tok], hi[:, i, :], False, k == KT - 1, count=i == 3 and t == TT - 1)
                leave(n, m, r)
            return banks, r

        def gemm_small(width, x, b, *ready):
            n, (hi, lo), m, landed = next_unit()
            hi, lo = (w.rearrange("p (k f) -> p k f", k=KT) for w in (hi, lo))
            o = psum[0:width, b, 0:SEQ]
            for k in range(KT):
                mm(o, hi[:, k, :], x[:, k, 0, :], k == 0, False, *landed, *bank(b), *tile_ready(ready, k))
                mm(o, hi[:, k, :], x[:, k, 1, :], False, False)
                r = mm(o, lo[:, k, :], x[:, k, 0, :], False, k == KT - 1, count=k == KT - 1)
            leave(n, m, r)
            i = sq_turn[0] % 2
            sq_turn[0] += 1
            r = copy(V, sq[0:width, i, 0:SEQ], o, r, *([sq_free[i]] if sq_free[i] else []))
            for t in range(TT):
                r = tr(psum[:, b, SEQ + t * width:SEQ + (t + 1) * width], sq[0:width, i, t * P:(t + 1) * P], r,
                       count=t == TT - 1)
            sq_free[i] = r
            return psum[:, b, SEQ:SEQ + TT * width], r

        def split(src, dst, i, *ready):
            hi, lo = dst[:, i:i + 2, 0, :], dst[:, i:i + 2, 1, :]
            s = src.rearrange("p (a t) -> p a t", a=2)
            r = act(hi, s, ACT.Copy, *ready)
            return tt(V, lo, s, hi.bitcast(F32), ALU.subtract, r, *ready)

        sq_free = [None, None]
        sq_turn = [0]

        def sum_squares(src, first, last, *ready, b=7):
            k = sq_turn[0] % 2
            sq_turn[0] += 1
            waits = list(ready) + ([sq_free[k]] if sq_free[k] else [])
            s = act(sq[:, k, :], src, ACT.Square, *waits)
            for j in range(2):
                r = mm(psum[:, b, 0:SEQ], ones, sq[:, k, j * SEQ:(j + 1) * SEQ], first and j == 0, last and j == 1,
                       s, *bank(b), count=j == 1)
            sq_free[k] = r
            return r

        def root(total, width, dst=None, b=7):
            dst = rstd[:, :] if dst is None else dst
            r = ts(V, dst, psum[:, b, 0:SEQ], 1.0 / width, ALU.mult, EPS, ALU.add, total, V.now, A_.now)
            bank_free[b] = [r]
            r = act(dst, dst, ACT.Sqrt, r)
            return V.run(lambda e: e.reciprocal(dst, dst), r)

        def flat(v):
            return v.rearrange("p a b -> p (a b)")

        def scaled_split(src, dst, gain, n, at=0):
            scale_ready, dst_free, made = V.now, T.now, []
            for i in range(0, n, 2):
                k = sq_turn[0] % 2
                sq_turn[0] += 1
                free = sq_free[k] or scale_ready
                for j in range(2):
                    r = stt(V, sq[:, k, j * SEQ:(j + 1) * SEQ], src[:, i + j, :], col(gain, i + j), rstd[:, :],
                            ALU.mult, ALU.mult, scale_ready, free)
                sq_free[k] = r = split(sq[:, k, :], dst, at + i, r, dst_free)
                made.append(r)
            return made

        def norm(src, dst, gain, n, *ready, at=0):
            for i in range(0, n, 2):
                r = sum_squares(flat(src[:, i:i + 2, :]), i == 0, i == n - 2, *tile_ready(ready, i))
            root(r, n * P)
            return scaled_split(src, dst, gain, n, at)

        def add_normed(delta, gain, ready):
            added = []
            for i in range(0, KT, 2):
                d, hh = delta(i), flat(h[:, i:i + 2, :])
                for j in range(2):
                    r = stt(V, d[:, j, :], d[:, j, :], col(gain, i + j), rstd[:, :], ALU.mult, ALU.mult, ready)
                added.append(tt(V, hh, hh, flat(d), ALU.add, r))
            return added

        def log1p(dst, e, z, z2, *ready):
            ts(V, z, e, 2.0, ALU.add, None, None, *ready)
            V.run(lambda q: q.reciprocal(z, z), V.now)
            tt(V, z, z, e, ALU.mult, V.now)
            tt(V, z2, z, z, ALU.mult, V.now)
            ts(V, dst, z2, 1.0 / 17, ALU.mult, None, None, V.now)
            for k in range(7, 0, -1):
                stt(V, dst, dst, 1.0 / (2 * k + 1), z2, ALU.add, ALU.mult, V.now)
            stt(V, dst, dst, 1.0, z, ALU.add, ALU.mult, V.now)
            return ts(V, dst, dst, 2.0, ALU.mult, None, None, V.now)

        def softplus_neg(dst, x, neg, e, z, z2, *ready):
            ts(V, neg, x, -1.0, ALU.mult, None, None, *ready)
            r = tt(V, e, neg, x, ALU.min, V.now)
            r = act(e, e, ACT.Exp, r)
            log1p(dst, e, z, z2, r)
            return stt(V, dst, neg, 0.0, dst, ALU.max, ALU.add, V.now)

        def first_block():
            buf, = phase(("mixers_1", 26176, F32))
            y = cut(buf, 0, KT, SEQ)
            q = cut(buf, 4096, 8, SEQ)
            k_sel, k_win = cut(buf, 6144, NKV, SEQ), cut(buf, 7168, NKV, SEQ)
            k_cmp, v_cmp = (cut(buf, 8192 + 1024 * i, NKV, SEQ)[0:HEAD] for i in range(2))
            bias = cut(buf, 10240, NH, SEQ)
            bias_cmp = cut(buf, 14336, TT, NCMP, NH)
            v_sel, v_win = cut(buf, 14816, TT, NKV * HEAD), cut(buf, 15328, TT, NKV * HEAD)
            gates = cut(buf, 15840, TT, 3 * NH)
            attn = 15936
            u_pad = cut(buf, attn, 8, SEQ + 3)
            gate_in = cut(buf, attn + 2080, 8, SEQ)
            temp = attn + 4128
            lru_w = cut(buf, 4096, 2, 8, P)
            hot_cmp = cut(buf, temp, TT * NCMP, P)[0:NBUCKET + 1]
            hot_rel = cut(buf, temp + 3840, 384)[0:NBUCKET + 1]
            tab = work[0:NBUCKET + 1, 0:NH]
            rel = buf[0:NH, temp + 4224:temp + 4608]
            spl = work[:, 16:24], work[:, 24:32], work[:, 32:40], work[:, 40:48], work[:, 48:56]
            pe = work[0:HEAD, 64:128].rearrange("p (w l) -> p w l", w=2)
            w2 = work[:, 128:384].rearrange("p (w f d) -> p w f d", w=2, f=2)

            plan_units(*[A["w_in"][i] for i in (*range(0, 16), 24, 25, 26, 27, 28, 29, 32, 33)])
            plan_tokens(A["w_v_sel"])
            plan_tokens(A["w_v_win"])
            plan_units(*[A["w_in"][i] for i in range(16, 24)])
            plan.append((A["w_gates"], KT * 3 * NH, True))
            for w in range(2):
                for f in range(2):
                    src = A["cmp_w1"][w, f]
                    plan.extend([(src[:, 0:HALF], HALF, False), (src[:, HALF:UNIT], HALF, False)])
            plan.extend([(A["w_out"][i][:, c * HALF:(c + 1) * HALF], HALF, True) for c in range(2) for i in range(KT)])
            for c in range(D_FF // P // CHUNK):
                plan_units(*[A["mlp_w1"][CHUNK * c + i] for i in range(CHUNK)])
                plan_units(*[A["mlp_w2"][4 * f + 2 * c + k] for f in range(KT) for k in range(2)])
            for c in range(2):
                plan.extend([(A["ple_proj"][c][:, 0:HALF], HALF, False), (A["ple_proj"][c][:, HALF:UNIT], HALF, False)])
            plan_units(*[A["ple_gate"][i] for i in range(KT)])

            prefetch()

            small = load([(tab[0:NBUCKET], A["rel_bias"]), (hot_cmp, A["hot_cmp"]), (hot_rel, A["hot_rel"]),
                          (pe, A["cmp_pe"]), (w2, A["cmp_w2"])])
            table_ready = fill(V, tab[NBUCKET:NBUCKET + 1], NEG)
            cleared = fill(G, lru_w, 0.0)
            fill(G, u_pad[:, :, 0:3], 0.0)
            lru_loaded = load([(lru_w[g * 64:g * 64 + 64, :, :, g * 64:g * 64 + 64], A["lru_w"][g]) for g in range(2)],
                              cleared)

            normed = norm(h, x2, "norm_mix_pre", KT)

            def features(first):
                return gemm_pair([[A["w_in"][first + j]] for j in range(2)], x2, normed)

            for i in range(0, 8, 2):
                b, r = features(i)
                bank_free[b] = [copy(V, u_pad[:, i:i + 2, 3:], psum[:, b, :].rearrange("p (a t) -> p a t", a=2),
                                     r, G.now)]
            r = mm(psum[0:NH, 3, 0:384], tab, hot_rel, True, True, small, table_ready, count=True)
            r = copy(V, rel, psum[0:NH, 3, 0:384], r)
            bank_free[3] = [r]
            stored = load([(scratch, rel.unsqueeze(1).broadcast_to([NH, P, 384]))], r)
            toeplitz = bass.AP(tensor=scratch.tensor, offset=P - 1, ap=[[383, P], [P * 384, NH], [1, SEQ]])
            bias_ready = load([(bias, toeplitz)], stored)
            for i in range(TT * NCMP):
                r = mm(psum[:, 4, i * NH:(i + 1) * NH], hot_cmp[:, i, :], tab, True, True,
                       count=i == TT * NCMP - 1)
            r = copy(V, bias_cmp.rearrange("p a b c -> p (a b c)"), psum[:, 4, 0:TT * NCMP * NH], r)
            bank_free[4] = [r]

            softplus_neg(spl[0], col("lru_lambda", 0, 8), *spl[1:])
            ts(V, spl[0], spl[0], 8.0, ALU.mult, None, None, V.now)
            decay_ready = ts(V, spl[1], spl[0], -1.0, ALU.mult, None, None, V.now)
            for i in range(0, 8, 2):
                b, r = features(8 + i)
                bank_free[b] = [copy(A_, flat(gate_in[:, i:i + 2, :]), psum[:, b, :], r)]

            def lru_half(first):
                xc, rg, ig, th, dec = (cut(buf, temp + 1024 * i, 4, SEQ) for i in range(5))
                def convolve(i):
                    f = first + i
                    ts(V, xc[:, i, :], u_pad[:, f, 0:SEQ], col("conv_w", f), ALU.mult, col("conv_b", f), ALU.add,
                       V.now, bias_ready)
                    for k in range(1, 4):
                        conv = stt(V, xc[:, i, :], u_pad[:, f, k:k + SEQ], col("conv_w", 8 * k + f), xc[:, i, :],
                                   ALU.mult, ALU.add, V.now)
                    return conv

                region_free = V.now
                convs = [convolve(0)]
                yield
                for i in range(4):
                    f = first + i
                    if i < 3:
                        convs.append(convolve(i + 1))
                    conv, b = convs[i], 3 + i % 2
                    mm(psum[:, b, 0:SEQ], lru_w[:, 0, f, :], xc[:, i, :], True, True, conv, lru_loaded, *bank(b))
                    r = mm(psum[:, b, SEQ:], lru_w[:, 1, f, :], xc[:, i, :], True, True, count=True)
                    act(rg[:, i, :], psum[:, b, 0:SEQ], ACT.Sigmoid, r, region_free, bias=col("lru_ba", f))
                    bank_free[b] = [act(ig[:, i, :], psum[:, b, SEQ:], ACT.Sigmoid, bias=col("lru_bx", f))]
                    yield
                for i in range(4):
                    act(th[:, i, :], rg[:, i, :], ACT.Tanh, A_.now, decay_ready,
                        scale=spl[0][:, first + i:first + i + 1])
                tanhs = A_.now
                for i in range(4):
                    act(dec[:, i, :], rg[:, i, :], ACT.Exp, scale=spl[1][:, first + i:first + i + 1])
                decays = A_.now
                th, rg, ig, xc = flat(th), flat(rg), flat(ig), flat(xc)
                ts(V, rg, th, 1.0, ALU.add, None, None, decays, tanhs)
                V.run(lambda e: e.reciprocal(rg, rg), V.now)
                r = tt(V, th, th, rg, ALU.mult, V.now)
                yield
                root_b = act(th, th, ACT.Sqrt, r, scale=2.0)
                tt(G, ig, ig, xc, ALU.mult, A_.now)
                r = tt(G, ig, ig, th, ALU.mult, root_b, G.now)
                gt = flat(gate_in[:, first:first + 4, :])
                gelu = act(gt, gt, ACT.Gelu_apprx_tanh)
                yield
                for i in range(4):
                    s = slice(i * SEQ, (i + 1) * SEQ)
                    o, a, bb = rg[:, s], flat(dec)[:, s], ig[:, s]
                    V.run(lambda e, o=o, a=a, bb=bb: e.tensor_tensor_scan(o, a, bb, 0.0, ALU.mult, ALU.add),
                          r, V.now, decays)
                tt(V, flat(y[:, first:first + 4, :]), rg, gt, ALU.mult, V.now, gelu)
                yield

            def to_groups(dst, b, r):
                src = psum[:, b, :].rearrange("p (a t) -> p a t", a=2)
                d = dst.rearrange("p (a two) t -> p a two t", two=2)
                for low in range(2 if dst.shape[0] == P else 1):
                    for g in range(2):
                        r = act(d[HEAD * low:HEAD * low + HEAD, :, g, :], src[HEAD * g:HEAD * g + HEAD], ACT.Copy, r)
                bank_free[b] = [r]

            def to_tokens(dst, src):
                banks, r = gemm_tokens(src, x2, normed)
                for t, b in enumerate(banks):
                    bank_free[b] = [copy(A_, dst[:, t, :], psum[:, b, 0:SEQ], r)]

            background.extend([lru_half(0), lru_half(4)])
            pace[0] = 1
            for first, dst in ((24, k_cmp), (26, v_cmp), (28, k_sel), (32, k_win)):
                b, r = features(first)
                to_groups(dst, b, r)
            to_tokens(v_sel, A["w_v_sel"])
            to_tokens(v_win, A["w_v_win"])
            while background:
                pump(1)
            lru_done, lru_all = T.now, V.now

            kc = work[:, 384:444]
            vc = work[0:NCMP, 448:704].rearrange("p (g d) -> p g d", g=NKV)
            blocks = [cut(buf, temp + 1024 * w, KT, NKV * NCMP) for w in range(2)]
            hids = [cut(buf, temp + 2048 + 128 * w, 2, NKV * NCMP) for w in range(2)]
            grouped = A_.now

            def windows():
                for w, src in enumerate((k_cmp, v_cmp)):
                    for m in range(2):
                        for par in range(2):
                            for g in range(NKV):
                                v = src[:, g, :].rearrange("p (a kk two) -> p kk two a", kk=8, two=2)
                                v = v[:, :, par, m:m + NCMP]
                                o = blocks[w][64 * par:64 * par + 64, 8 * m:8 * m + 8, g * NCMP:(g + 1) * NCMP]
                                e = pe[:, w, :].rearrange("p (m kk two) -> p m kk two", m=2, two=2)[:, m, :, par]
                                tt(V, o, v, e.unsqueeze(2).broadcast_to([HEAD, 8, NCMP]), ALU.add,
                                   grouped, lru_all, lru_done, small)
                            yield

            background.append(windows())
            for i in range(0, 8, 2):
                b, r = features(16 + i)
                bank_free[b] = [act(flat(q[:, i:i + 2, :]), psum[:, b, :], ACT.Copy, r, lru_done, scale=HEAD ** -0.5)]
            pace[0] = 0
            while background:
                pump(1)
            blocks_ready = V.now
            sums, r = gemm_small(3 * NH, x2, 5, normed)
            bank_free[5] = [act(flat(gates), sums, ACT.Sigmoid, r)]
            projected = T.now

            hid_ready = []
            for w, blk in enumerate(blocks):
                b = 6 - w
                for f in range(2):
                    for c in range(2):
                        n, part, m, landed = next_unit()
                        wk = part.rearrange("p (k f) -> p k f", k=8)
                        for i in range(8):
                            k = 8 * c + i
                            r = mm(psum[:, b, f * 60:(f + 1) * 60], wk[:, i, :], blk[:, k, :], k == 0, k == KT - 1,
                                   *landed, blocks_ready, *bank(b), count=i == 7)
                        leave(n, m, r)
                bank_free[b] = [act(flat(hids[w]), psum[:, b, 0:120], ACT.Gelu_apprx_tanh, r)]
                hid_ready.append(bank_free[b][0])
            lru_normed = norm(y[:, 0:8, :], x2, "gnorm_lru", 8, lru_all)
            for f in range(2):
                r = mm(psum[0:HEAD, 6, 128:188], w2[:, 0, f, :], hids[0][:, f, :], f == 0, f == 1, hid_ready[0], small,
                       count=f == 1)
            for low in range(2):
                r = copy(V, kc[HEAD * low:HEAD * low + HEAD], psum[0:HEAD, 6, 128:188], r)
            bank_free[6] = [r]
            for g in range(NKV):
                for f in range(2):
                    r = mm(psum[0:NCMP, 5, 128 + 64 * g:192 + 64 * g], hids[1][:, f, g * NCMP:(g + 1) * NCMP],
                           w2[:, 1, f, :], f == 0, f == 1, hid_ready[1], count=g == NKV - 1 and f == 1)
            bank_free[5] = [copy(V, vc.rearrange("p g d -> p (g d)"), psum[0:NCMP, 5, 128:384], r)]
            compressed = V.now

            pv_done = [None, None]

            def buffers(g):
                def base(a, n):
                    return buf[:, attn + 3072 * (g % 2) + a:attn + 3072 * (g % 2) + a + n]

                p0 = [base(1536 * w, 512).rearrange("p (h s) -> p h s", h=REP) for w in range(2)]
                p1 = [base(1536 * w + 512, 1024).rearrange("p (h s) -> p h s", h=REP) for w in range(2)]
                pc = work[:, 704 + 120 * (g % 2):824 + 120 * (g % 2)].rearrange("p (t h n) -> p t h n", t=TT, h=REP)
                st = work[:, 944 + 64 * (g % 2):1008 + 64 * (g % 2)]
                return p0, p1, pc, st

            def half_of(v, i):
                return v[HEAD * (i % 2):HEAD * (i % 2) + HEAD]

            def head(v, g, i):
                return half_of(v, i)[:, (REP * g + i) // 2, :]

            def softmaxes(g):
                p0, p1, pc, st = buffers(g)
                before = [pv_done[g % 2]] if pv_done[g % 2] else [compressed, projected]
                hs = slice(REP * g, REP * g + REP)
                gate = gates.rearrange("p t (h b) -> p t h b", b=3)
                ps = psum[:, 7, SEQ:SEQ + 120].rearrange("p (t h n) -> p t h n", t=TT, h=REP)
                for odd in range(2):
                    turn_waits = [A_.now, compressed, *bank(7)] if odd == 0 else [T.now]
                    for t in range(TT):
                        for i in (odd, odd + 2):
                            r = mm(ps[:, t, i, :], head(q, g, i)[:, t * P:(t + 1) * P],
                                   half_of(kc, i)[:, g * NCMP:(g + 1) * NCMP], True, True, *turn_waits,
                                   count=t == TT - 1 and i == odd + 2)
                for t in range(TT):
                    r = tt(V, pc[:, t], ps[:, t], bias_cmp[:, t, :, hs].rearrange("p n h -> p h n"), ALU.add,
                           r, *before)
                bank_free[7] = [r]
                top = st[:, 0:8].rearrange("p (t h) -> p t h", t=TT)
                tot = st[:, 8:16].rearrange("p (t h) -> p t h", t=TT)
                wide = [P, REP, NCMP]
                V.run(lambda e: e.tensor_reduce(top, pc, AX.X, ALU.max), V.now)
                for t in range(TT):
                    tt(V, pc[:, t], pc[:, t], top[:, t].unsqueeze(2).broadcast_to(wide), ALU.subtract, V.now)
                pcf = pc.rearrange("p t h n -> p (t h n)")
                exps = act(pcf, pcf, ACT.Exp, V.now)
                yield
                V.run(lambda e: e.tensor_reduce(tot, pc, AX.X, ALU.add), exps)
                V.run(lambda e: e.reciprocal(tot, tot), V.now)
                for t in range(TT):
                    ts(V, tot[:, t], tot[:, t], con("any")[:, t:t + 1], ALU.mult, None, None, V.now)
                tt(V, tot, tot, gate[:, :, hs, 0], ALU.mult, V.now)
                for t in range(TT):
                    tt(V, pc[:, t], pc[:, t], tot[:, t].unsqueeze(2).broadcast_to(wide), ALU.mult, V.now)
                for w, keys in enumerate((k_sel, k_win)):
                    mx = st[:, 16 + 16 * w:24 + 16 * w]
                    sm = st[:, 24 + 16 * w:32 + 16 * w]
                    s0 = psum[:, 2:4, 0:SEQ].rearrange("p b (a s) -> p a b s", a=2)
                    s1 = psum[:, 4:6, :].rearrange("p b (a s) -> p a b s", a=2)
                    for i in range(REP):
                        r0 = mm(s0[:, i // 2, i % 2, :], head(q, g, i)[:, 0:P], half_of(keys, i)[:, g, 0:P], True, True,
                                *bank(2), *bank(3), count=i == REP - 1)
                    for i in range(REP):
                        r1 = mm(s1[:, i // 2, i % 2, :], head(q, g, i)[:, P:SEQ], half_of(keys, i)[:, g, :], True, True,
                                *bank(4), *bank(5), count=i == REP - 1)

                    def by_bank(v):
                        return v.rearrange("p (a b) s -> p a b s", b=2)

                    bank_free[2] = bank_free[3] = [tt(V, by_bank(p0[w]), s0, by_bank(bias[:, hs, P:SEQ]), ALU.add, r0,
                                                      bias_ready, *before)]
                    bank_free[4] = bank_free[5] = [tt(V, by_bank(p1[w]), s1, by_bank(bias[:, hs, :]), ALU.add, r1)]
                    V.run(lambda e, m=mx, p=p0[w]: e.tensor_reduce(m[:, 0:4], p, AX.X, ALU.max), V.now)
                    V.run(lambda e, m=mx, p=p1[w]: e.tensor_reduce(m[:, 4:8], p, AX.X, ALU.max), V.now)
                    r = ts(V, mx, mx, -1.0, ALU.mult, None, None, V.now)
                    for t, p in enumerate((p0[w], p1[w])):
                        for i in range(REP):
                            j = REP * t + i
                            exps = act(p[:, i, :], p[:, i, :], ACT.Exp, r, bias=mx[:, j:j + 1],
                                       accum=sm[:, j:j + 1])
                    yield
                    r = V.run(lambda e, m=sm: e.reciprocal(m, m), exps)
                    r = tt(V, sm.rearrange("p (t h) -> p t h", t=TT), sm.rearrange("p (t h) -> p t h", t=TT),
                           gate[:, :, hs, 1 + w], ALU.mult, V.now)
                    tt(V, p0[w], p0[w], sm[:, 0:4].unsqueeze(2).broadcast_to([P, REP, P]), ALU.mult, V.now)
                    tt(G, p1[w], p1[w], sm[:, 4:8].unsqueeze(2).broadcast_to([P, REP, SEQ]), ALU.mult, r)
                weighted[g] = [V.now, G.now]
                yield

            turned_free = [[], []]
            turn = [0]

            def turn_head(g, i):
                p0, p1, pc, st = buffers(g)
                ready = weighted[g]
                k = turn[0] % 2
                turn[0] += 1
                turned = cut(buf, attn + 6144 + 1024 * k, 1024)
                for w in range(2):
                    b = 6 if w == 0 else 1
                    tr(psum[:, b, 0:P], p0[w][:, i, :], *ready, *bank(b))
                    tr(psum[:, b, P:2 * P], p1[w][:, i, 0:P])
                    tr(psum[:, b, 2 * P:3 * P], p1[w][:, i, P:SEQ])
                    r = tr(psum[0:NCMP, b, 3 * P:4 * P], pc[:, w, i, :], count=True)
                    q_ = A_ if w == 0 else V
                    copy(q_, turned[:, 384 * w:384 * w + 384], psum[:, b, 0:384], r, *turned_free[k])
                    c = copy(q_, turned[0:NCMP, 768 + P * w:768 + P * w + P], psum[0:NCMP, b, 384:512])
                    bank_free[b] = [c]
                if i == REP - 1:
                    pv_done[g % 2] = T.now
                return k, turned, [A_.now, V.now]

            def weigh_values(g, i, k, turned, ready):
                hd = REP * g + i
                o = psum[0:HEAD, 7, 0:SEQ]
                late = psum[0:HEAD, 7, P:SEQ]
                for w, v in enumerate((v_sel, v_win)):
                    d = slice(g * HEAD, (g + 1) * HEAD)
                    mm(o, v[:, 0, d], turned[:, 384 * w:384 * w + 256], w == 0, False, *ready, *bank(7))
                    mm(late, v[:, 1, d], turned[:, 384 * w + 256:384 * w + 384], False, False)
                r = mm(o, vc[:, g, :], turned[0:NCMP, 768:1024], False, True, count=True)
                turned_free[k] = [r]
                at = HEAD * (hd % 2)
                bank_free[7] = [copy(A_, y[at:at + HEAD, 8 + hd // 2, :], o, r)]

            weighted = {}

            def attention():
                for _ in softmaxes(0):
                    yield
                for g in range(NKV):
                    following = softmaxes(g + 1) if g + 1 < NKV else iter(())
                    turned = turn_head(g, 0)
                    for i in range(REP):
                        next(following, None)
                        after = turn_head(g, i + 1) if i + 1 < REP else None
                        weigh_values(g, i, *turned)
                        turned = after
                        yield

            def projected_pair(i):
                at = 8192 + i * SEQ if i < 8 else attn + 8192 + (i - 8) * SEQ
                return cut(buf, at, 2, SEQ)

            background.append(attention())
            pace[0] = 1
            gemm_banks[0] = 1
            for i in range(0, KT, 2):
                b, r = gemm_pair([[A["w_out"][i + j]] for j in range(2)], x2, lru_normed, halves=[0])
                bank_free[b] = [copy(A_, flat(projected_pair(i)), psum[:, b, :], r, compressed, lru_all)]
            pace[0] = 0
            while background:
                pump(1)
            gemm_banks[0] = 3
            r = norm(y[:, 8:16, :], x2, "gnorm_nsa", 8, A_.now, at=8)
            r = lru_normed + r
            for i in range(0, KT, 2):
                b, g_ = gemm_pair([[A["w_out"][i + j]] for j in range(2)], x2, r, halves=[1])
                o = flat(projected_pair(i))
                bank_free[b] = [tt(V, o, o, psum[:, b, :], ALU.add, g_)]
                total = sum_squares(o, i == 0, i == KT - 2, V.now)
            root(total, D)
            r = add_normed(projected_pair, "norm_mix_post", V.now)

            before = [V.now, A_.now, G.now, T.now]
            o_buf, hid_buf = phase(("mlp_out", KT * SEQ, F32), ("mlp_hidden", CHUNK * 2 * SEQ, F32R))
            o = cut(o_buf, 0, KT, SEQ)
            hidden = cut(hid_buf, 0, CHUNK, 2, SEQ)
            r = norm(h, x2, "norm_mlp_pre", KT, r)
            chunks = D_FF // P // CHUNK
            for c in range(chunks):
                ready = []
                for i in range(0, CHUNK, 2):
                    b, g_ = gemm_pair([[A["mlp_w1"][CHUNK * c + i + j]] for j in range(2)], x2, r)
                    k = sq_turn[0] % 2
                    sq_turn[0] += 1
                    s = act(sq[:, k, :], psum[:, b, :], ACT.Relu, g_, sq_free[k])
                    bank_free[b] = [s]
                    s = tt(V, sq[:, k, :], sq[:, k, :], sq[:, k, :], ALU.mult, s)
                    sq_free[k] = split(sq[:, k, :], hidden, i, s, *before)
                    ready.append(sq_free[k])
                for i in range(0, KT, 2):
                    b, g_ = gemm_pair([[A["mlp_w2"][4 * (i + j) + 2 * c + k] for k in range(2)] for j in range(2)],
                                      hidden, ready)
                    oo = flat(o[:, i:i + 2, :])
                    if c == 0:
                        s = copy(V, oo, psum[:, b, :], g_, *before)
                    else:
                        s = tt(V, oo, oo, psum[:, b, :], ALU.add, g_)
                    bank_free[b] = [s]
                    if c == chunks - 1:
                        total = sum_squares(oo, i == 0, i == KT - 2, s)
                before = [T.now]
            r = root(total, D)
            r = add_normed(lambda i: o[:, i:i + 2, :], "norm_mlp_post", r)

            before = [V.now, A_.now, G.now, T.now]
            buf, = phase(("embedding", 3 * KT * SEQ, F32))
            emb, sig = cut(buf, 0, KT, SEQ), cut(buf, KT * SEQ, KT, SEQ)
            pt = work[:, 0:512].rearrange("p (k t) -> p k t", k=2)
            p_in = load([(pt, A["p"])], *before)
            x2_free = T.now
            for i in range(0, KT, 2):
                r[i // 2] = split(flat(h[:, i:i + 2, :]), x2, i, r[i // 2], x2_free)
            for c in range(4):
                n, part, m, landed = next_unit()
                w = part.rearrange("p (f k j) -> p f k j", f=4, k=2)
                for f in range(0, 4, 2):
                    b = gemm_bank()
                    for j in range(2):
                        for i in range(2):
                            g_ = mm(psum[:, b, j * SEQ:(j + 1) * SEQ], w[:, f + j, i, :], pt[:, i, :], i == 0, i == 1,
                                    *landed, p_in, *bank(b), count=i == 1 and j == 1)
                    bank_free[b] = [copy(A_, flat(emb[:, 4 * c + f:4 * c + f + 2, :]), psum[:, b, :], g_, *before)]
                leave(n, m, g_)
            for i in range(0, KT, 2):
                b, g_ = gemm_pair([[A["ple_gate"][i + j]] for j in range(2)], x2, r)
                s = act(flat(sig[:, i:i + 2, :]), psum[:, b, :], ACT.Sigmoid, g_, *before)
                bank_free[b] = [s]
                e2, hh = flat(emb[:, i:i + 2, :]), flat(h[:, i:i + 2, :])
                s = tt(V, e2, e2, flat(sig[:, i:i + 2, :]), ALU.mult, s)
                tt(V, hh, hh, e2, ALU.add, s)

        def second_block():
            in_before = [V.now, A_.now, G.now, T.now]
            buf, = phase(("mixers_2", 26572, F32))
            y = cut(buf, 0, KT, SEQ)
            u = cut(buf, 4096, 8, SEQ)
            qk_pad = cut(buf, 6144, 4, SEQ + 3)
            qk = cut(buf, 7180, KT, SEQ)
            v = cut(buf, 11276, TT, MW)
            sig_o = cut(buf, 13324, 8, SEQ)
            b_w = cut(buf, 15372, 8, 2, P)
            c_w = cut(buf, 17420, 2, ST, 32)
            glu_w = cut(buf, 19468, 8, 2, P)
            chunk = 15372
            temp = 21516

            plan_units(*[A["w_in2"][32 + i] for i in range(8)])
            for p in range(8):
                plan_units(*[A["w_in2"][2 * p + j] for j in range(2)])
                if p < 4:
                    plan_tokens(A["w_v2"][p])
                else:
                    plan_units(*[A["w_in2"][24 + 2 * (p - 4) + j] for j in range(2)])
            plan.append((A["w_gates2"], KT * 8, True))
            plan.extend([(A["w_out2"][i][:, c * HALF:(c + 1) * HALF], HALF, True) for c in (1, 0) for i in range(KT)])
            plan_units(*[A["wq2"][i] for i in range(KT)])
            for c in range(NKEY // CHUNK):
                plan_units(*[A["peer_u"][CHUNK * c + i] for i in range(CHUNK)])
                plan_units(*[A["peer_v"][f, 2 * c + k] for f in range(KT) for k in range(2)])

            prefetch()
            small = [work[:, 32 * i:32 * i + 32] for i in range(30)]
            gl = work[:, 960:976].rearrange("p (t g) -> p t g", t=TT)
            bg = work[:, 976:992]
            fill(G, b_w.rearrange("p a b c -> p (a b c)"), 0.0, *in_before)
            fill(G, c_w.rearrange("p a b c -> p (a b c)"), 0.0)
            fill(G, glu_w.rearrange("p a b c -> p (a b c)"), 0.0)
            cleared = fill(G, qk_pad[:, :, 0:3], 0.0)
            pieces = [(bg, A["b_gates2"])]
            for r in range(4):
                for g in range(2):
                    a = 32 * r + 16 * g
                    pieces += [(b_w[a:a + 16, :, c, 64 * g:64 * g + 64], A["s5_b"][r, g, :, :, c, :]) for c in range(2)]
            for g in range(2):
                pieces += [(c_w[64 * g:64 * g + 64, c, :, 16 * g:16 * g + 16], A["s5_c"][g, :, c]) for c in range(2)]
            for g in range(8):
                a = 16 * g
                pieces += [(glu_w[a:a + 16, :, c, a:a + 16], A["s5_glu"][g, :, :, c, :]) for c in range(2)]
            params = load(pieces, cleared)

            normed = norm(h, x2, "norm1", KT, *in_before)

            (dt, x, th, n, ang, tn, em1, mag, hs, sn1, cm1, cs1, arm1, ai, den, fr, fi, phi, t0) = small[:19]
            lre, lim = col("s5_re", 0, ST), col("s5_im", 0, ST)
            magic = 1.5 * 2.0 ** 23
            c_ready = []

            def s5_constants():
                r = act(dt, col("s5_dt", 0, ST), ACT.Exp, *in_before)
                tt(V, x, lre, dt, ALU.mult, r)
                tt(V, th, lim, dt, ALU.mult)
                ts(V, n, th, 1.0 / TWO_PI, ALU.mult, None, None, V.now)
                ts(V, n, n, magic, ALU.add, magic, ALU.subtract, V.now)
                p1 = 6.28125
                p2 = float(np.float32(np.round((TWO_PI - p1) * 2 ** 24) / 2 ** 24))
                p3 = TWO_PI - p1 - p2
                stt(V, ang, n, -p1, th, ALU.mult, ALU.add, V.now)
                stt(V, ang, n, -p2, ang, ALU.mult, ALU.add, V.now)
                stt(V, ang, n, -p3, ang, ALU.mult, ALU.add, V.now)
                ts(V, ang, ang, 3.1415925, ALU.min, -3.1415925, ALU.max, V.now)
                r = ts(V, phi, ang, 1.0 / TWO_PI, ALU.mult, None, None, V.now)
                act(tn, x, ACT.Tanh, r, scale=0.5)
                act(hs, ang, ACT.Sin, scale=0.5)
                r = act(sn1, ang, ACT.Sin)
                ts(V, t0, tn, -1.0, ALU.mult, 1.0, ALU.add, r)
                V.run(lambda e: e.reciprocal(t0, t0), V.now)
                stt(V, em1, tn, 2.0, t0, ALU.mult, ALU.mult, V.now)
                ts(V, mag, em1, 1.0, ALU.add, None, None, V.now)
                stt(V, cm1, hs, -2.0, hs, ALU.mult, ALU.mult, V.now)
                ts(V, cs1, cm1, 1.0, ALU.add, None, None, V.now)
                tt(V, ai, mag, sn1, ALU.mult, V.now)
                tt(V, arm1, em1, cs1, ALU.mult, V.now)
                tt(V, arm1, arm1, cm1, ALU.add, V.now)
                tt(V, den, lre, lre, ALU.mult)
                tt(V, t0, lim, lim, ALU.mult, V.now)
                tt(V, den, den, t0, ALU.add, V.now)
                V.run(lambda e: e.reciprocal(den, den), V.now)
                tt(V, fr, arm1, lre, ALU.mult, V.now)
                tt(V, t0, ai, lim, ALU.mult, V.now)
                tt(V, fr, fr, t0, ALU.add, V.now)
                tt(V, fr, fr, den, ALU.mult, V.now)
                tt(V, fi, ai, lre, ALU.mult, V.now)
                tt(V, t0, arm1, lim, ALU.mult, V.now)
                tt(V, fi, fi, t0, ALU.subtract, V.now)
                tt(V, fi, fi, den, ALU.mult, V.now)
                c_re, c_im = c_w[:, 0], c_w[:, 1]
                wide = [P, ST, 32]
                frb, fib = fr.unsqueeze(2).broadcast_to(wide), fi.unsqueeze(2).broadcast_to(wide)
                tmp = [cut(buf, temp + 1024 * i, ST, 32) for i in range(3)]
                tt(G, tmp[0], c_re, frb, ALU.mult, params, V.now)
                tt(G, tmp[1], c_im, fib, ALU.mult)
                tt(G, tmp[2], c_re, fib, ALU.mult)
                tt(G, c_im, c_im, frb, ALU.mult, G.now)
                tt(G, c_re, tmp[0], tmp[1], ALU.subtract, G.now)
                tt(G, c_im, tmp[2], c_im, ALU.add, G.now)
                c_ready.append(G.run(lambda e: e.tensor_scalar(c_im, c_im, -1.0, None, ALU.mult), G.now))
                yield
            background.append(s5_constants())

            for i in range(0, 8, 2):
                b, r = gemm_pair([[A["w_in2"][32 + i + j]] for j in range(2)], x2, normed)
                bank_free[b] = [copy(A_, flat(u[:, i:i + 2, :]), psum[:, b, :], r)]
                if i == 0:
                    pump(1)
            u_ready = A_.now
            while background:
                pump(1)

            def wide2(v):
                return v.rearrange("p (a t) -> p a t", a=2)

            hold = [buf[:, temp + 512 * i:temp + 512 * i + 512] for i in range(9)]
            spare = [buf[:, 512 * i:512 * i + 512] for i in range(4)]
            t1, t2, w1, w2, f1, f2 = hold[:6]
            trig = [(hold[6], hold[7]), (spare[0], spare[1])]
            state = [(hold[8], spare[2]), (spare[3], work[:, 1024:1536])]
            below = float(np.nextafter(np.float32(TWO_PI), np.float32(0)))

            def s5_steps():
                turns_free, made, rotated, out_read = c_ready, [None, None], [None, None], [[], []]
                pairs_n = ST // 2
                for p in range(-1, pairs_n + 1):
                    k, nxt = p % 2, p + 1
                    sn, cs = trig[k]
                    zr, zi = state[k]
                    now, ahead = 0 <= p < pairs_n, nxt < pairs_n
                    if now:
                        ps = psum[:, 3:5, :].rearrange("p a (c t) -> p a c t", c=2)
                        br, bi = ps[:, :, 0, :], ps[:, :, 1, :]
                        tt(V, wide2(t1), wide2(cs), br, ALU.mult, *made[k], *out_read[k], V.now)
                        tt(V, wide2(t2), wide2(sn), bi, ALU.mult)
                        tt(V, zr, t1, t2, ALU.add, V.now)
                        tt(V, wide2(t1), wide2(cs), bi, ALU.mult, V.now)
                        tt(V, wide2(t2), wide2(sn), br, ALU.mult)
                        bank_free[3] = bank_free[4] = [V.now]
                        tt(V, zi, t1, t2, ALU.subtract, V.now)
                    if ahead:
                        for j in range(2):
                            i = 2 * nxt + j
                            turned = act(f1[:, j * SEQ:(j + 1) * SEQ], con("time"), ACT.Copy, *turns_free,
                                         scale=phi[:, i:i + 1])
                    yield
                    if now:
                        for j in range(2):
                            s = slice(j * SEQ, (j + 1) * SEQ)
                            m = mag[:, 2 * p + j:2 * p + j + 1].broadcast_to([P, SEQ])
                            for o, z in ((w1, zr), (w2, zi)):
                                scanned = V.run(lambda e, o=o[:, s], z=z[:, s], m=m: e.tensor_tensor_scan(
                                    o, m, z, 0.0, ALU.mult, ALU.add), V.now, *([rotated[1 - k]] if p else []))
                    if ahead:
                        ts(V, f2, f1, magic, ALU.add, magic, ALU.subtract, turned, V.now)
                    yield
                    if now:
                        tt(G, zr, cs, w1, ALU.mult, scanned)
                        tt(G, zi, sn, w1, ALU.mult)
                        tt(G, sn, sn, w2, ALU.mult, G.now)
                        tt(G, cs, cs, w2, ALU.mult)
                        tt(G, zr, zr, sn, ALU.subtract, G.now)
                        rotated[k] = tt(G, zi, zi, cs, ALU.add, G.now)
                    if ahead:
                        turned = tt(V, f1, f1, f2, ALU.subtract, V.now)
                    yield
                    if p >= 1:
                        out_read[1 - k] = [s5_out(p - 1, rotated[1 - k])]
                    if ahead:
                        sn1_, cs1_ = trig[1 - k]
                        free = [rotated[1 - k]] if p >= 1 else c_ready
                        act(sn1_, f1, ACT.Sin, turned, *free, scale=below)
                        r = act(cs1_, f1, ACT.Sin, scale=below / 2)
                        turns_free = [r]
                        r = act(cs1_, cs1_, ACT.Square, r)
                        ready = act(cs1_, cs1_, ACT.Identity, r, scale=-2.0, bias=1.0)
                        for j in range(2):
                            i = 2 * nxt + j
                            a, f = 32 * (i % 4), i // 4
                            for c in range(2):
                                r = mm(psum[:, 3 + j, c * SEQ:(c + 1) * SEQ], b_w[a:a + 32, f, c, :],
                                       u[a:a + 32, f, :], True, True, params, u_ready, *bank(3 + j), count=c == 1)
                        made[1 - k] = [ready, r]
                    yield

            def s5_out(p, ready):
                zr, zi = state[p % 2]
                for j in range(2):
                    i = 2 * p + j
                    a = 32 * (i % 4)
                    o = psum[a:a + 32, 5, 0:SEQ]
                    s = slice(j * SEQ, (j + 1) * SEQ)
                    mm(o, c_w[:, 0, i, :], zr[:, s], True, False, ready, *bank(5))
                    r = mm(o, c_w[:, 1, i, :], zi[:, s], False, True, count=j == 1)
                if p % 2:
                    f = p // 2
                    bank_free[5] = [stt(V, u[:, f, :], u[:, f, :], col("s5_d", f), psum[:, 5, 0:SEQ], ALU.mult,
                                        ALU.add, r)]
                return r

            def conv(i, arrived):
                o, pad = qk[:, i, :], qk_pad[:, i % 4, :]
                r = act(o, pad[:, 0:SEQ], ACT.Copy, arrived, scale=col("conv_qk", i))
                for k in range(1, 4):
                    r = stt(V, o, pad[:, k:k + SEQ], col("conv_qk", KT * k + i), o, ALU.mult, ALU.add, r)
                return r

            background.append(s5_steps())
            pace[0] = 1
            pad_read = [cleared, cleared]
            for p in range(8):
                pump(1)
                b, r = gemm_pair([[A["w_in2"][2 * p + j]] for j in range(2)], x2, normed)
                r = copy(A_, qk_pad[:, 2 * p % 4:2 * p % 4 + 2, 3:], wide2(psum[:, b, :]), r, cleared, pad_read[p % 2])
                bank_free[b] = [r]
                conv(2 * p, r)
                pad_read[p % 2] = conv(2 * p + 1, r)
                if p < 4:
                    banks, r = gemm_tokens(A["w_v2"][p], x2, normed)
                    for t, b in enumerate(banks):
                        bank_free[b] = [copy(A_, v[:, t, 2 * p * P:(2 * p + 2) * P], psum[:, b, 0:SEQ], r)]
                else:
                    f = 2 * (p - 4)
                    b, r = gemm_pair([[A["w_in2"][24 + f + j]] for j in range(2)], x2, normed)
                    bank_free[b] = [copy(A_, flat(sig_o[:, f:f + 2, :]), psum[:, b, :], r)]
            sums, r = gemm_small(8, x2, 7, normed)
            glf = work[:, 960:976]
            tt(V, glf, sums, bg, ALU.add, r, params)
            bank_free[7] = [V.now]
            while background:
                pump(1)
            pace[0] = 0

            uf = flat(u)
            r = act(uf, uf, ACT.Gelu, V.now)
            for f in range(8):
                b = 3 + f % 2
                mm(psum[:, b, 0:SEQ], glu_w[:, f, 0, :], u[:, f, :], True, True, r, params, *bank(b))
                g_ = mm(psum[:, b, SEQ:], glu_w[:, f, 1, :], u[:, f, :], True, True, count=True)
                s = act(t1[:, SEQ * (f % 2):SEQ * (f % 2) + SEQ], psum[:, b, SEQ:], ACT.Sigmoid, g_, V.now, G.now)
                bank_free[b] = [tt(V, y[:, 8 + f, :], psum[:, b, 0:SEQ], t1[:, SEQ * (f % 2):SEQ * (f % 2) + SEQ],
                                   ALU.mult, s)]

            sof = flat(sig_o)
            act(sof, sof, ACT.Sigmoid)

            def mlstm():
                s5_done = [V.now, G.now, T.now]
                sm = work[:, 0:960].rearrange("p (i t h) -> p i t h", t=TT, h=MH)[:, 0:40]
                a_, tot, c_, m_inter_t = (sm[:, i] for i in (5, 6, 7, 18))
                flats = [sm[:, i].rearrange("p t h -> p (t h)") for i in range(23)]
                (log_f, exp_f, z_f, z2_f, neg_f, _, _, c_flat, within_max, m_tok, neg_m, inter, floor, _, x_f, c_max,
                 m1_flat, wl_flat, m_inter, _, den_abs, mean_sq, neg_den) = flats
                xg = gl[:, :, MH:2 * MH]
                li = gl[:, :, 0:MH]
                copy(V, sm[:, 14], xg, *s5_done)
                softplus_neg(log_f, x_f, neg_f, exp_f, z_f, z2_f, V.now)
                r = ts(V, log_f, log_f, -1.0, ALU.mult, None, None, V.now)
                r2 = act(flat(qk), flat(qk), ACT.Silu, r)
                yield
                mm(psum[:, 7, 0:8], con("tri"), log_f, True, True, r, *bank(7))
                r = mm(psum[:, 7, 8:16], ones, log_f, True, True, count=True)
                bank_free[7] = [V.run(lambda e: e.tensor_copy(work[:, 40:56], psum[:, 7, 0:16]), r)]
                tt(V, c_, li, a_, ALU.subtract, V.now)
                diag = cut(buf, chunk, 8, P)
                for i in range(8):
                    r = ts(V, diag[:, i, :], ident, c_flat[:, i:i + 1], ALU.mult, None, None, V.now, *s5_done)
                yield
                for t in range(TT):
                    r2 = mm(psum[:, 3 + t, :], ones, diag[:, MH * t:MH * t + MH, :].rearrange("p a b -> p (a b)"),
                            True, True, r, *bank(3 + t), count=True)
                    ps = psum[:, 3 + t, :].rearrange("p (h s) -> p h s", h=MH)
                    if t == 0:
                        V.run(lambda e, ps=ps: e.tensor_reduce(c_max[:, 0:4], ps, AX.X, ALU.max), r2)
                    for hd in range(MH):
                        stt(V, diag[:, MH * t + hd, :], ps[:, hd, :], a_[:, t, hd:hd + 1], con("causal"), ALU.add,
                            ALU.add, r2)
                    bank_free[3 + t] = [V.now]
                yield
                V.run(lambda e: e.tensor_reduce(within_max, diag, AX.X, ALU.max), V.now)
                m1, wl = m1_flat[:, 0:4], wl_flat[:, 0:4]
                tt(V, m1, c_max[:, 0:4], tot[:, 0], ALU.add, V.now)
                tt(V, m1, m1, tot[:, 0], ALU.max, V.now)
                tt(V, wl, c_[:, 0], tot[:, 0], ALU.add, V.now)
                tt(V, wl, wl, m1, ALU.subtract, V.now)
                mi = m_inter_t
                copy(V, mi[:, 0], a_[:, 0], V.now)
                tt(V, mi[:, 1], a_[:, 1], m1, ALU.add, V.now)
                tt(V, m_tok, within_max, m_inter, ALU.max, V.now)
                ts(V, neg_m, m_tok, -1.0, ALU.mult, None, None, V.now)
                r = tt(V, inter, m_inter, m_tok, ALU.subtract, V.now)
                act(wl, wl, ACT.Exp, r)
                act(inter, inter, ACT.Exp)
                act(floor, neg_m, ACT.Exp)
                for i in range(8):
                    act(diag[:, i, :], diag[:, i, :], ACT.Exp, bias=neg_m[:, i:i + 1])
                ts(V, inter, inter, MD ** -0.5, ALU.mult, None, None, A_.now)
                weights_ready, scores_weights = V.now, A_.now
                yield

                k_tok = cut(buf, chunk + 1024, MH, MD)
                for hd in range(MH):
                    b = 5 + hd % 2
                    for j in range(2):
                        r = tr(psum[:, b, j * P:(j + 1) * P], qk[:, 8 + 2 * hd + j, 0:P], scores_weights, *bank(b), count=j == 1)
                    bank_free[b] = [ts(V, k_tok[:, hd, :], psum[:, b, 0:MD], wl[:, hd:hd + 1], ALU.mult, None, None,
                                       r, weights_ready)]
                    if hd % 2:
                        yield
                probs = cut(buf, chunk + 2048, 8, P)
                turned = cut(buf, chunk + 3072, 8, P)
                for t in range(TT):
                    tok = slice(t * P, (t + 1) * P)
                    for hd in range(MH):
                        for j in range(2):
                            r = mm(psum[:, 3, hd * P:(hd + 1) * P], qk[:, 2 * hd + j, tok], qk[:, 8 + 2 * hd + j, tok],
                                   j == 0, j == 1, *bank(3), count=j == 1)
                    cols4 = slice(MH * t, MH * t + MH)
                    ps = psum[:, 3, :].rearrange("p (h s) -> p h s", h=MH)
                    r = stt(V, probs[:, cols4, :], ps, MD ** -0.5, diag[:, cols4, :], ALU.mult, ALU.mult, r,
                            scores_weights)
                    bank_free[3] = [r]
                    yield
                    for hd in range(MH):
                        r2 = tr(psum[:, 4, hd * P:(hd + 1) * P], probs[:, MH * t + hd, :], r, *bank(4), count=hd == 3)
                    turned_ready = copy(A_, turned[:, cols4, :].rearrange("p a b -> p (a b)"), psum[:, 4, :], r2)
                    bank_free[4] = [turned_ready]
                hm = cut(buf, temp, 8, MD + 1)
                c0 = [cut(buf, temp + 2060 + 514 * i, 2, MD + 1) for i in range(2)]
                c0_read = [[], []]
                keys_ready = V.now
                for hd in range(MH):
                    vs = slice(hd * MD, (hd + 1) * MD)
                    for j in range(2):
                        b = 5 + j
                        kd = k_tok[:, hd, j * P:(j + 1) * P]
                        mm(psum[:, b, 0:MD], kd, v[:, 0, vs], True, True, keys_ready, turned_ready, *bank(b))
                        r = mm(psum[:, b, MD:MD + 1], kd, ones[:, 0:1], True, True, count=True)
                        bank_free[b] = [copy(A_, c0[hd % 2][:, j, :], psum[:, b, 0:MD + 1], r, *c0_read[hd % 2])]
                    c0_ready = A_.now
                    for t in range(TT):
                        i, b = MH * t + hd, 3 + t
                        mm(psum[:, b, 0:MD], turned[:, i, :], v[:, t, vs], True, True, *bank(b))
                        r = mm(psum[:, b, MD:MD + 1], turned[:, i, :], ones[:, 0:1], True, True, count=True)
                        within = copy(A_, hm[:, i, :], psum[:, b, 0:MD + 1], r, *s5_done)
                        bank_free[b] = [within]
                    yield
                    for j in range(2):
                        r = mm(psum[:, 7, 0:MD + 1], qk[:, 2 * hd + j, P:SEQ], c0[hd % 2][:, j, :], j == 0, j == 1,
                               c0_ready, *bank(7), count=j == 1)
                    c0_read[hd % 2] = [r]
                    i = MH + hd
                    bank_free[7] = [stt(V, hm[:, i, :], psum[:, 7, 0:MD + 1], inter[:, i:i + 1], hm[:, i, :], ALU.mult,
                                        ALU.add, r, within)]
                dn, ms = den_abs, mean_sq
                d_ = hm[:, :, MD]
                ts(V, neg_den, d_, -1.0, ALU.mult, None, None, V.now, A_.now)
                tt(V, dn, d_, neg_den, ALU.max, V.now)
                tt(V, dn, dn, floor, ALU.max, V.now)
                V.run(lambda e: e.reciprocal(dn, dn), V.now)
                for i in range(8):
                    r = ts(V, hm[:, i, 0:MD], hm[:, i, 0:MD], dn[:, i:i + 1], ALU.mult, None, None, V.now)
                    act(sq[:, i % 2, 0:MD], hm[:, i, 0:MD], ACT.Square, r, A_.now, accum=ms[:, i:i + 1])
                ts(V, ms, ms, 1.0 / MD, ALU.mult, EPS, ALU.add, A_.now)
                r = act(ms, ms, ACT.Sqrt, V.now)
                V.run(lambda e: e.reciprocal(ms, ms), r)
                yield
                scaled = V.now
                heads = [ts(V, hm[:, i, 0:MD], hm[:, i, 0:MD], ms[:, i:i + 1], ALU.mult, None, None, scaled)
                         for i in range(8)]
                yield
                for i in range(8):
                    t, hd = i // MH, i % MH
                    r = heads[i]
                    b = 3 + i % 2
                    for j in range(2):
                        r2 = tr(psum[:, b, j * P:(j + 1) * P], hm[:, i, j * P:(j + 1) * P], r, *bank(b), count=j == 1)
                    for j in range(2):
                        f = 2 * hd + j
                        tok = slice(t * P, (t + 1) * P)
                        stt(V, y[:, f, tok], psum[:, b, j * P:(j + 1) * P], col("mlstm_norm", f), sig_o[:, f, tok],
                            ALU.mult, ALU.mult, r2)
                    bank_free[b] = [V.now]
                    if i % 4 == 3:
                        yield
            x2_free, s5_ready = T.now, V.now
            s5_ready = [split(flat(y[:, i:i + 2, :]), x2, i, s5_ready, x2_free) for i in range(8, KT, 2)]
            background.append(mlstm())
            pace[0] = 1
            for i in range(0, KT, 2):
                b, r = gemm_pair([[A["w_out2"][i + j]] for j in range(2)], x2, [x2_free] * 4 + s5_ready, halves=[1])
                hh = flat(h[:, i:i + 2, :])
                bank_free[b] = [tt(V, hh, hh, psum[:, b, :], ALU.add, r)]
            pace[0] = 0
            while background:
                pump(1)
            mixed = V.now

            mixed = [split(flat(y[:, i:i + 2, :]), x2, i, mixed) for i in range(0, 8, 2)]
            for i in range(0, KT, 2):
                b, r = gemm_pair([[A["w_out2"][i + j]] for j in range(2)], x2, mixed, halves=[0])
                hh = flat(h[:, i:i + 2, :])
                r = tt(V, hh, hh, psum[:, b, :], ALU.add, r)
                bank_free[b] = [r]
                total = sum_squares(hh, i == 0, i == KT - 2, r)
            root(total, D)
            normed2 = scaled_split(h, x2, "norm2", KT)

            before = [V.now, A_.now, G.now, T.now]
            gate_buf, route = phase(("peer_gates", CHUNK * SEQ, F32), ("routing", 3 * KT * SEQ, F32))
            gate_place, hid_buf, hot_buf = phase(("gates_again", CHUNK * SEQ, F32), ("peer_hidden", CHUNK * 2 * SEQ, F32R),
                                        ("one_hots", 2 * HOTS * (P + 3 * CHUNK), BF16))
            assert gate_place.shape == gate_buf.shape
            gates = cut(gate_buf, 0, CHUNK, SEQ)
            hidden = cut(hid_buf, 0, CHUNK, 2, SEQ)
            hots1 = cut(hot_buf, 0, 2, HOTS, P)
            hots2 = hot_buf[:, 2 * HOTS * P:]
            hots2 = hots2.rearrange("p (b w t n) -> p b w t n", b=2, t=HOTS, w=3)

            q2 = cut(route, 0, KT, SEQ)
            sc = cut(route, 4096, PH, 4 * P)
            keys = cut(route, 8192, 2, P)
            keys_in = load([(keys, A["subkeys"])], *before)
            for i in range(0, KT, 2):
                b, r = gemm_pair([[A["wq2"][i + j]] for j in range(2)], x2, normed2)
                r = copy(V, flat(q2[:, i:i + 2, :]), psum[:, b, :], r, *before)
                bank_free[b] = [r]
                b = 3 + (i // 2) % 2
                for t in range(TT):
                    for j in range(2):
                        s = (2 * t + j) * P
                        g_ = mm(psum[:, b, s:s + P], q2[:, i + j, t * P:(t + 1) * P], keys[:, j, :], True, True,
                                r, keys_in, *bank(b), count=t == 1 and j == 1)
                bank_free[b] = [copy(A_, sc[:, i // 2, :], psum[:, b, :], g_, *before)]
            scored = A_.now
            queries_read = T.now
            top_v = work[:, 0:512].rearrange("p (h t s k) -> p h t s k", h=PH, t=TT, s=2)
            top_i = work[:, 512:1024].bitcast(U32).rearrange("p (h t s k) -> p h t s k", h=PH, t=TT, s=2)
            top_f = work[:, 1024:1536].rearrange("p (h t s k) -> p h t s k", h=PH, t=TT, s=2)

            def top16(vals, idx, src):
                a, b = slice(0, 8), slice(8, 16)
                V.run(lambda e: e.max(vals[:, a], src), V.now, scored, queries_read)
                V.run(lambda e: e.max_index(idx[:, a], vals[:, a], src), V.now)
                V.run(lambda e: e.match_replace(src, vals[:, a], src, -3.0e38), V.now)
                V.run(lambda e: e.max(vals[:, b], src), V.now)
                return V.run(lambda e: e.max_index(idx[:, b], vals[:, b], src), V.now)

            def tail(at, n):
                return route[:, 8448 + at:8448 + at + n]

            cand = tail(0, 256).rearrange("p (a b) -> p a b", a=TOPK)
            best = tail(256, 256).rearrange("p (t h k) -> p t h k", t=TT, h=PH)
            place = tail(512, 256).bitcast(U32)
            place4 = place.rearrange("p (t h k) -> p t h k", t=TT, h=PH)
            part_u = tail(768, 256).bitcast(U32)
            part = [tail(1024 + 256 * s, 256).rearrange("p (t n) -> p t n", t=TT) for s in range(2)]
            peak = tail(1536, 16)
            lists = tail(1600, 768).rearrange("p (w t n) -> p w t n", w=3, t=TT)
            hot = tail(2400, 1024)
            def routing():
                for hd in range(PH):
                    for t in range(TT):
                        for s in range(2):
                            top16(top_v[:, hd, t, s], top_i[:, hd, t, s], sc[:, hd, (2 * t + s) * P:(2 * t + s + 1) * P])
                        yield
                yield
                copy(V, work[:, 1024:1536], work[:, 512:1024].bitcast(U32), V.now)
                for t in range(TT):
                    for hd in range(PH):
                        a_s = top_v[:, hd, t, 0].unsqueeze(2).broadcast_to([P, TOPK, TOPK])
                        b_s = top_v[:, hd, t, 1].unsqueeze(1).broadcast_to([P, TOPK, TOPK])
                        tt(V, cand, a_s, b_s, ALU.add, V.now)
                        top16(best[:, t, hd], place4[:, t, hd], cand.rearrange("p a b -> p (a b)"))
                        yield
                for s, op, k in ((0, ALU.logical_shift_right, 4), (1, ALU.bitwise_and, 15)):
                    V.run(lambda e, op=op, k=k: e.tensor_scalar(part_u, place, k, None, op), V.now)
                    copy(V, part[s].rearrange("p t n -> p (t n)"), part_u, V.now)
                iota16 = con("iota")[:, 0:TOPK]
                for s in range(2):
                    for t in range(TT):
                        for hh in range(2):
                            n = 4 * TOPK
                            o = hot.rearrange("p (n k) -> p n k", n=n)
                            tt(V, o, part[s][:, t, hh * n:(hh + 1) * n].unsqueeze(2).broadcast_to([P, n, TOPK]),
                               iota16.unsqueeze(1).broadcast_to([P, n, TOPK]), ALU.is_equal, V.now)
                            for q4 in range(4):
                                o4 = o[:, q4 * TOPK:(q4 + 1) * TOPK, :]
                                tt(V, o4, o4, top_f[:, 4 * hh + q4, t, s].unsqueeze(1).broadcast_to([P, TOPK, TOPK]),
                                   ALU.mult, V.now)
                            V.run(lambda e, o=o, d=lists[:, s, t, hh * n:(hh + 1) * n]: e.tensor_reduce(
                                d, o, AX.X, ALU.add), V.now)
                            yield
                bf = tail(256, 256).rearrange("p (a k) -> p a k", k=TOPK)
                copy(V, peak, bf[:, :, 0], V.now)
                tt(V, bf, bf, peak.unsqueeze(2).broadcast_to([P, 16, TOPK]), ALU.subtract, V.now)
                r = act(tail(256, 256), tail(256, 256), ACT.Exp, V.now)
                V.run(lambda e: e.tensor_reduce(peak, bf, AX.X, ALU.add), r)
                V.run(lambda e: e.reciprocal(peak, peak), V.now)
                yield tt(V, lists[:, 2].rearrange("p t (h k) -> p (t h) k", h=PH), bf,
                            peak.unsqueeze(2).broadcast_to([P, 16, TOPK]), ALU.mult, V.now)

            pairs = work[:, 0:2 * SEQ].rearrange("p (w t) -> p w t", w=2)
            gate_parts = work[:, 2 * SEQ:4 * SEQ].bitcast(BF16).rearrange("p (w t) -> p w t", w=4)[:, 0:3, :]
            iota = con("iota")
            batches = 2
            masks = work[:, 5 * SEQ:6 * SEQ].bitcast(BF16).rearrange("p (b t n) -> p b t n", b=batches, t=HOTS)
            hot_read = [[] for _ in range(batches)]
            mask_read = [[] for _ in range(batches)]

            def turn_lists():
                for w in range(3):
                    for t in range(TT):
                        s = (2 * w + t) * P
                        r = tr(psum[:, 5 + s // 512, s % 512:s % 512 + P], lists[:, w, t, :], V.now,
                               *bank(5), *bank(6), count=w == 2 and t == 1)
                gate = work[:, 1024:1280]
                copy(V, work[:, 0:512], psum[:, 5, :], r)
                r = copy(V, gate, psum[:, 6, 0:SEQ])
                bank_free[5] = bank_free[6] = [r]
                for w in range(3):
                    r = copy(V, gate_parts[:, w, :], gate, r)
                    if w < 2:
                        r = tt(V, gate, gate, gate_parts[:, w, :], ALU.subtract, r)
                return r

            def make_hots(c, t, listed):
                k = t // HOTS % batches
                toks = slice(t, t + HOTS)
                one, two, mask = hots1[:, k], hots2[:, k], masks[:, k]
                wide, thin, parts = [P, HOTS, P], [P, HOTS, CHUNK], [P, 3, HOTS, CHUNK]
                keys2 = iota[:, CHUNK * c:CHUNK * (c + 1)].unsqueeze(1).broadcast_to(thin)
                m = tt(V, mask, keys2, pairs[:, 1, toks].unsqueeze(2).broadcast_to(thin), ALU.is_equal, listed,
                       *mask_read[k])
                v1 = tt(V, one, iota.unsqueeze(1).broadcast_to(wide), pairs[:, 0, toks].unsqueeze(2).broadcast_to(wide),
                        ALU.is_equal, *hot_read[k])
                g1 = tt(G, two, mask.unsqueeze(1).broadcast_to(parts),
                        gate_parts[:, :, toks].unsqueeze(3).broadcast_to(parts), ALU.mult, m, *hot_read[k])
                mask_read[k] = [g1]
                return [g1, v1]

            def gate_chunk(c, listed, onto, gates_read):
                made = make_hots(c, 0, listed)
                for t in range(0, SEQ, HOTS):
                    following = make_hots(c, t + HOTS, listed) if t + HOTS < SEQ else None
                    yield
                    k, b = t // HOTS % batches, 3 + (t // 16) % 2
                    for i in range(HOTS):
                        at = CHUNK * ((t + i) % 16)
                        o = psum[:, b, at:at + CHUNK]
                        for w in range(3):
                            r = mm(o, hots1[:, k, i, :], hots2[:, k, w, i, :], w == 0, w == 2, *made, *bank(b),
                                   count=i == HOTS - 1 and w == 2)
                    hot_read[k] = [r]
                    made = following
                    if (t + HOTS) % 16 == 0:
                        g = gates[:, :, t + HOTS - 16:t + HOTS]
                        p = psum[:, b, :].rearrange("p (t n) -> p n t", n=CHUNK)
                        if onto:
                            bank_free[b] = [tt(V, g, g, p, ALU.mult, r, A_.now)]
                        else:
                            bank_free[b] = [copy(A_, g, p, r, gates_read)]
                    yield

            background.append(routing())
            pace[0] = 1
            pool_helps[0] = True
            for c in range(NKEY // CHUNK):
                if c:
                    while background:
                        pump(1)
                    gates_ready = [A_.now]
                pace[0] = pace[0] if c == 0 else 0
                hidden_ready = []
                for i in range(0, CHUNK, 2):
                    b, r = gemm_pair([[A["peer_u"][CHUNK * c + i + j]] for j in range(2)], x2, normed2)
                    if c == 0:
                        bank_free[b] = [act(flat(gates[:, i:i + 2, :]), psum[:, b, :], ACT.Gelu, r, *before)]
                        continue
                    k = sq_turn[0] % 2
                    sq_turn[0] += 1
                    s = act(sq[:, k, :], psum[:, b, :], ACT.Gelu, r, sq_free[k])
                    bank_free[b] = [s]
                    s = tt(V, sq[:, k, :], sq[:, k, :], flat(gates[:, i:i + 2, :]), ALU.mult, s, *gates_ready)
                    sq_free[k] = split(sq[:, k, :], hidden, i, s, hidden_free)
                    hidden_ready.append(sq_free[k])
                if c == 0:
                    while background:
                        pump(1)
                    pace[0] = 0
                    pool_helps[0] = False
                    listed = turn_lists()
                    for _ in gate_chunk(0, listed, True, None):
                        pass
                    gated = V.now
                    hidden_ready = [split(flat(gates[:, i:i + 2, :]), hidden, i, gated) for i in range(0, CHUNK, 2)]
                if c + 1 < NKEY // CHUNK:
                    background.append(gate_chunk(c + 1, listed, False, V.now))
                    pace[0] = 1
                for i in range(0, KT, 2):
                    b, r = gemm_pair([[A["peer_v"][i + j, 2 * c + k] for k in range(2)] for j in range(2)], hidden,
                                     hidden_ready)
                    hh = flat(h[:, i:i + 2, :])
                    r = tt(V, hh, hh, psum[:, b, :], ALU.add, r)
                    bank_free[b] = [r]
                    if c == NKEY // CHUNK - 1:
                        total = sum_squares(hh, i == 0, i == KT - 2, r)
                hidden_free = T.now
            root(total, D)
            for i in range(KT):
                stt(V, h[:, i, :], h[:, i, :], col("final", i), rstd[:, :], ALU.mult, ALU.mult, V.now)


        loaded = load([(cols[:, :], A["cols"]), (const[:, :], A["consts"])])
        x_in = load([(flat(h[:, :, :]), A["x"])])
        for q in (T, V, A_, G):
            q.wait(loaded, x_in)

        first_block()
        second_block()

        store = load([(out, flat(h[:, :, :]))],
                     V.now, A_.now, G.now, T.now, queue=S)
        S.wait(store)

        block = ctx.enter_context(nc.Block())
        block.sync(lambda e: S.play(e))
        block.scalar(lambda e: A_.play(e))
        block.vector(lambda e: V.play(e))
        block.gpsimd(lambda e: G.play(e))
        block.tensor(lambda e: T.play(e))


def _units(w):
    k, f = w.shape
    w = w.reshape(k // UNIT * 1, KT, P, f // P, P) if k >= UNIT else w.reshape(1, k // P, P, f // P, P)
    return w.transpose(3, 0, 2, 1, 4).reshape(-1, P, w.shape[1] * P)


def _wide_units(w):
    return w.reshape(KT, P, -1, 2 * P).transpose(2, 1, 0, 3).reshape(-1, P, 2 * UNIT)


def _columns(v):
    v = v.reshape(-1, v.shape[-1] // P, P)
    return v.transpose(2, 0, 1).reshape(P, -1)


def _features(x):
    t, f = x.shape
    return x.reshape(t, f // P, P).transpose(2, 1, 0).reshape(P, -1)


def _bucket(dist):
    n = np.maximum(dist, 1).astype(np.float32)
    large = 16 + (np.log(n / 16) / math.log(8) * 16).astype(np.int32)
    return np.where(dist < 16, dist, np.minimum(large, NBUCKET - 1))


def _one_hot(dist):
    b = np.where(dist < 0, NBUCKET, _bucket(np.maximum(dist, 0)))
    return (b[None] == np.arange(NBUCKET + 1).reshape(-1, *[1] * dist.ndim)).astype(np.float32)


def _constants():
    i = np.arange(P)
    parts = {
        "ident": np.eye(P), "ones": np.ones((P, P)), "tri": i[:, None] <= i[None, :],
        "causal": np.where(i[None, :] <= i[:, None], 0.0, NEG), "iota": np.tile(i, (P, 1)),
        "time": np.tile(np.arange(1, SEQ + 1), (P, 1)),
        "any": np.arange(SEQ).reshape(TT, P).T >= CMP_LEN - 1,
    }
    return np.concatenate([parts[n].astype(np.float32) for n in CONST], axis=1)


def kernel(**inputs):
    import concourse.bacc as bacc
    from concourse.bass_utils import run_bass_kernel_spmd

    x = {k: np.asarray(v) for k, v in inputs.items()}
    x = {k: v[0] if v.shape[0] == 1 and k != "x" else v for k, v in x.items()}
    arrays = {"consts": _constants(), "x": _features(x["x"][0])}

    def per_state(v):
        return v.reshape(ST, P).T

    col_parts = {
        "norm_mix_pre": x["norm_mix_pre"], "norm_mix_post": x["norm_mix_post"], "norm_mlp_pre": x["norm_mlp_pre"],
        "norm_mlp_post": x["norm_mlp_post"], "conv_w": x["conv_w"], "conv_b": x["conv_b"],
        "lru_ba": x["lru_ba"].reshape(-1), "lru_bx": x["lru_bx"].reshape(-1), "lru_lambda": x["lru_lambda"],
        "gnorm_lru": x["gnorm_lru"], "gnorm_nsa": x["gnorm_nsa"], "norm1": x["norm1_g_2"],
        "conv_qk": x["conv_qk_w_2"], "mlstm_norm": x["mlstm_norm_g_2"],
        "s5_re": x["s5_lambda_re_2"].reshape(-1), "s5_im": x["s5_lambda_im_2"].reshape(-1),
        "s5_dt": np.repeat(x["s5_log_dt_2"], NSTATE), "s5_d": x["s5_d_2"].reshape(-1),
        "norm2": x["norm2_g_2"], "final": x["final_g_2"],
    }
    arrays["cols"] = np.concatenate([_columns(col_parts[n]) for n in COLS], axis=1)

    i = np.arange(384)
    t, n = np.arange(P), np.arange(NCMP)
    dist = (np.arange(TT)[:, None, None] * P + t[None, None, :]) - (n[None, :, None] * CMP_STRIDE + CMP_LEN - 1)
    arrays["hot_rel"] = _one_hot(SEQ - 1 - i)
    arrays["hot_cmp"] = _one_hot(dist).reshape(NBUCKET + 1, TT * NCMP, P)
    arrays["rel_bias"] = x["rel_bias"]
    arrays["cmp_pe"] = np.stack([x["cmp_pe_k"], x["cmp_pe_v"]]).transpose(2, 0, 1)
    arrays["cmp_w1"] = np.stack([_units(x["cmp_w1_k"]), _units(x["cmp_w1_v"])])
    arrays["cmp_w2"] = np.stack([x["cmp_w2_k"], x["cmp_w2_v"]]).reshape(2, 2, P, HEAD).transpose(2, 0, 1, 3)
    arrays["lru_w"] = np.stack([x["lru_wa"], x["lru_wx"]]).reshape(2, 8, 2, 64, 64).transpose(2, 3, 0, 1, 4)
    arrays["w_in"] = _units(x["w_in"][:, :4608])
    arrays["w_v_sel"], arrays["w_v_win"] = _wide_units(x["w_in"][:, [*range(3840, 4096), *range(4352, 4608)]])
    arrays["w_gates"] = x["w_in"][:, 4608:].reshape(KT, P, 48).transpose(1, 0, 2).reshape(P, -1)
    for name in ("w_out", "mlp_w1", "mlp_w2", "ple_gate"):
        arrays[name] = _units(x[name])
    arrays["ple_proj"] = x["ple_proj"].reshape(2, P, 2, 8, P).transpose(2, 1, 3, 0, 4).reshape(2, P, UNIT)
    arrays["p"] = _features(x["p"][0]).reshape(P, 2, SEQ)

    w = x["w_in_2"]
    arrays["w_in2"] = np.concatenate([_units(w[:, :4096]), _units(w[:, 4104:])])
    arrays["w_v2"] = _wide_units(w[:, 2048:3072])
    arrays["w_gates2"] = w[:, 4096:4104].reshape(KT, P, 8).transpose(1, 0, 2).reshape(P, -1)
    arrays["b_gates2"] = np.broadcast_to(np.tile(x["b_gates_2"], TT), (P, TT * 8))
    arrays["w_out2"] = _units(x["w_out_2"])
    b = np.stack([x["s5_b_re_2"], x["s5_b_im_2"]])
    arrays["s5_b"] = b.reshape(2, 8, 4, 2, NSTATE, GSZ).transpose(2, 3, 5, 1, 0, 4)
    c = np.stack([x["s5_c_re_2"], x["s5_c_im_2"]])
    arrays["s5_c"] = c.reshape(2, ST, 2, GSZ, NSTATE).transpose(2, 4, 0, 1, 3)
    arrays["s5_glu"] = x["s5_glu_w_2"].reshape(8, 8, GSZ, 2, GSZ).transpose(1, 2, 0, 3, 4)
    arrays["wq2"] = _units(x["peer_wq_2"])
    arrays["subkeys"] = x["peer_subkeys_2"].transpose(2, 0, 1)
    arrays["peer_u"] = x["peer_u_2"].reshape(NKEY, NKEY, KT, P).transpose(1, 3, 2, 0).reshape(NKEY, P, UNIT)
    arrays["peer_v"] = x["peer_v_2"].reshape(NKEY, 8, 16, KT, P).transpose(3, 1, 0, 2, 4).reshape(KT, 8, P, UNIT)

    nc = bacc.Bacc("TRN2", target_bir_lowering=False, num_devices=1)
    arrays = {f"in_{k}": np.ascontiguousarray(v) for k, v in arrays.items()}
    aps = {k[3:]: nc.dram_tensor(k, v.shape, mybir.dt.from_np(v.dtype), kind="ExternalInput").ap()
           for k, v in arrays.items()}
    out = nc.dram_tensor("out", (P, KT * SEQ), F32, kind="ExternalOutput").ap()
    build(nc, aps, out)
    r = run_bass_kernel_spmd(nc, [arrays], core_ids=[0])
    got = np.asarray(r.results[0]["out"])
    return np.ascontiguousarray(got.reshape(P, KT, SEQ).transpose(2, 1, 0)).reshape(1, SEQ, D)
```
